# Optimizing a Trainium2 kernel written in Bass

```python
import math, functools
import jax, jax.numpy as jnp
from jax import lax
import numpy as np

D_MODEL = 1024
BATCH = 1
SEQ = 128
DEPTH = 2
DEC_BATCH = 1
DEC_SEQ = 512
PAST_LEN = 128

GRID_W = 64
H_A = 6
DA = 32
V_A = 2 * DA
W_B = 256
CONV_W = 3
H_C = 6
NOPE_C = 64
ROPE_C = 32
QK_C = NOPE_C + ROPE_C
V_C = 64
Q_RANK = 192
KV_RANK = 128
IN_COLS = 2 * H_A * 2 * DA + H_A * V_A + 3 * W_B + Q_RANK + KV_RANK + ROPE_C
MIX_W = H_A * V_A + W_B + H_C * V_C
D_FF = 2816
N_EXPERTS = 8
TOP_K = 2
MOE_FF = 1024
N_DENSE = (DEPTH + 1) // 2
N_MOE = DEPTH // 2
ROPE_THETA = 10000.0
Q_BLOCK = 128
EPS = 1e-6
F32 = jnp.float32

kernel_name = 'hybrid_diffattn_shortconv_mla_denoise_step'

def rmsnorm(x, g):
    xf = x.astype(F32)
    y = xf * lax.rsqrt(jnp.mean(xf * xf, axis=-1, keepdims=True) + EPS)
    return (y * g.astype(F32)).astype(x.dtype)

def split_in(proj):
    sizes = (H_A * 2 * DA, H_A * 2 * DA, H_A * V_A, W_B, W_B, W_B, Q_RANK, KV_RANK, ROPE_C)
    outs = []
    start = 0
    for s in sizes:
        outs.append(proj[..., start:start + s])
        start += s
    return outs

def grid_positions(T):
    t = jnp.arange(T, dtype=jnp.int32)
    return (t // GRID_W).astype(F32), (t % GRID_W).astype(F32)

def axial_rope(x, rows, cols):
    half = x.shape[-1] // 2
    n = half // 2
    inv = jnp.power(ROPE_THETA, -jnp.arange(n, dtype=F32) / n)
    shape = (rows.shape[0],) + (1,) * (x.ndim - 3) + (n,)

    def rot(xh, pos):
        ang = pos[:, None] * inv[None, :]
        cos = jnp.cos(ang).reshape(shape).astype(x.dtype)
        sin = jnp.sin(ang).reshape(shape).astype(x.dtype)
        x1, x2 = xh[..., :n], xh[..., n:]
        return jnp.concatenate([x1 * cos - x2 * sin, x1 * sin + x2 * cos], axis=-1)

    return jnp.concatenate([rot(x[..., :half], rows), rot(x[..., half:], cols)], axis=-1)

def rope_tail(x, rows, cols):
    return jnp.concatenate([x[..., :NOPE_C], axial_rope(x[..., NOPE_C:], rows, cols)], axis=-1)

def sweep_query_blocks(fn, q):
    B, T = q.shape[:2]
    nb = T // Q_BLOCK
    qb = jnp.moveaxis(q.reshape((B, nb, Q_BLOCK) + q.shape[2:]), 1, 0)
    out = jnp.moveaxis(lax.map(fn, qb), 0, 1)
    return out.reshape((B, T) + out.shape[3:])

def diff_attention(q, k, v, lam):
    scale = DA ** -0.5

    def block(qb):
        s = jnp.einsum('bqhcd,bkhcd->bhcqk', qb, k).astype(F32) * scale
        p = jax.nn.softmax(s, axis=-1)
        w = p[:, :, 0] - lam * p[:, :, 1]
        return jnp.einsum('bhqk,bkhe->bqhe', w.astype(v.dtype), v)

    return sweep_query_blocks(block, q)

def softmax_attention(q, k, v):
    scale = QK_C ** -0.5

    def block(qb):
        s = jnp.einsum('bqhd,bkhd->bhqk', qb, k).astype(F32) * scale
        p = jax.nn.softmax(s, axis=-1)
        return jnp.einsum('bhqk,bkhe->bqhe', p.astype(v.dtype), v)

    return sweep_query_blocks(block, q)

def conv3_centred(u, w, b):
    L = u.shape[-2]
    pad = [(0, 0)] * (u.ndim - 2) + [(1, 1), (0, 0)]
    up = jnp.pad(u, pad)
    return up[..., 0:L, :] * w[0] + up[..., 1:L + 1, :] * w[1] + up[..., 2:L + 2, :] * w[2] + b

def mla_keys(ckv_n, k_rope, w_kb, w_vb, knorm_c):
    B, S = ckv_n.shape[:2]
    k_nope = (ckv_n @ w_kb).reshape(B, S, H_C, NOPE_C)
    v = (ckv_n @ w_vb).reshape(B, S, H_C, V_C)
    k_r = jnp.broadcast_to(k_rope[:, :, None, :], (B, S, H_C, ROPE_C))
    k = rmsnorm(jnp.concatenate([k_nope, k_r], axis=-1), knorm_c)
    return k, v

def swiglu(x, wg, wu, wd):
    return (jax.nn.silu(x @ wg) * (x @ wu)) @ wd

def moe_ffn(x, router_w, wg, wu, wd):
    B, T, D = x.shape
    xt = x.reshape(B * T, D)
    logits = (xt @ router_w).astype(F32)
    topv, topi = lax.top_k(logits, TOP_K)
    gates = jax.nn.softmax(topv, axis=-1)
    combine = jnp.sum(jax.nn.one_hot(topi, N_EXPERTS, dtype=F32) * gates[..., None], axis=1).astype(x.dtype)
    out = jnp.zeros_like(xt)
    for e in range(N_EXPERTS):
        out = out + combine[:, e:e + 1] * swiglu(xt, wg[e], wu[e], wd[e])
    return out.reshape(B, T, D)

def token_mixer(h, lw, lam, l_init, ctx):
    B, T, _ = h.shape
    a_q, a_k, a_v, b_b, b_c, b_x, c_q, c_kv, c_kr = split_in(h @ lw['w_in'])
    q_a = rmsnorm(a_q.reshape(B, T, H_A, 2, DA), lw['qnorm_a'])
    k_a = rmsnorm(a_k.reshape(B, T, H_A, 2, DA), lw['knorm_a'])
    v_a = a_v.reshape(B, T, H_A, V_A)
    q_c = rmsnorm((rmsnorm(c_q, lw['norm_qa']) @ lw['w_qb']).reshape(B, T, H_C, QK_C), lw['qnorm_c'])
    ckv_n = rmsnorm(c_kv, lw['norm_kva'])
    k_c, v_c = mla_keys(ckv_n, c_kr, lw['w_kb'], lw['w_vb'], lw['knorm_c'])
    u = b_c * b_x
    if ctx is None:
        state = (k_a, v_a, ckv_n, c_kr)
        ka_all, va_all, kc_all, vc_all = k_a, v_a, k_c, v_c
        conv = conv3_centred(u, lw['conv_w'], lw['conv_b'])
    else:
        state = None
        rows, cols = grid_positions(T)
        q_a = axial_rope(q_a, rows, cols)
        k_a = axial_rope(k_a, rows, cols)
        q_c = rope_tail(q_c, rows, cols)
        k_c = rope_tail(k_c, rows, cols)
        ctx_k, ctx_v, ctx_ckv, ctx_kr = ctx
        kc_ctx, vc_ctx = mla_keys(ctx_ckv, ctx_kr, lw['w_kb'], lw['w_vb'], lw['knorm_c'])
        ka_all = jnp.concatenate([ctx_k, k_a], axis=1)
        va_all = jnp.concatenate([ctx_v, v_a], axis=1)
        kc_all = jnp.concatenate([kc_ctx, k_c], axis=1)
        vc_all = jnp.concatenate([vc_ctx, v_c], axis=1)
        rows_n = T // GRID_W
        conv = conv3_centred(u.reshape(B, rows_n, GRID_W, W_B), lw['conv_w'], lw['conv_b']).reshape(B, T, W_B)
    o_a = diff_attention(q_a, ka_all, va_all, lam)
    o_a = rmsnorm(o_a, lw['subln_a']) * (1.0 - l_init)
    o_c = softmax_attention(q_c, kc_all, vc_all)
    o_b = b_b * conv
    y = jnp.concatenate([o_a.reshape(B, T, H_A * V_A), o_b, o_c.reshape(B, T, H_C * V_C)], axis=-1) @ lw['w_out']
    return y, state

def trunk_layer(x, mod, lw, lam, l_init, ffn, ctx):
    shift1, scale1, gate1, shift2, scale2, gate2 = jnp.split(mod, 6, axis=-1)
    h = rmsnorm(x, lw['norm_mix']) * (1 + scale1) + shift1
    y, state = token_mixer(h, lw, lam, l_init, ctx)
    x = x + gate1 * y
    h = rmsnorm(x, lw['norm_ffn']) * (1 + scale2) + shift2
    x = x + gate2 * ffn(h)
    return x, state

def setup_inputs(seed: int = 0) -> dict:
    key = jax.random.key(seed)
    ks = iter(jax.random.split(key, 64))

    def nrm(shape, scale=1.0):
        return scale * jax.random.normal(next(ks), shape, jnp.float32)

    def gain(shape):
        return 1.0 + 0.05 * nrm(shape)

    s = D_MODEL ** -0.5
    return {
        'x_prompt': nrm((BATCH, SEQ, D_MODEL)),
        'x_sample': nrm((DEC_BATCH, DEC_SEQ, D_MODEL)),
        'cache_diff_k': nrm((DEC_BATCH, DEPTH, PAST_LEN, H_A, 2, DA)),
        'cache_diff_v': nrm((DEC_BATCH, DEPTH, PAST_LEN, H_A, V_A)),
        'cache_mla_ckv': nrm((DEC_BATCH, DEPTH, PAST_LEN, KV_RANK)),
        'cache_mla_krope': nrm((DEC_BATCH, DEPTH, PAST_LEN, ROPE_C)),
        'c': nrm((DEC_BATCH, D_MODEL)),
        'c_ctx': nrm((D_MODEL,)),
        'w_ada': nrm((DEPTH, D_MODEL, 6 * D_MODEL), 0.5 * s),
        'b_ada': nrm((DEPTH, 6 * D_MODEL), 0.02),
        'norm_mix': gain((DEPTH, D_MODEL)),
        'norm_ffn': gain((DEPTH, D_MODEL)),
        'w_in': nrm((DEPTH, D_MODEL, IN_COLS), s),
        'qnorm_a': gain((DEPTH, DA)),
        'knorm_a': gain((DEPTH, DA)),
        'lambda_q1': nrm((DEPTH, DA), 0.1),
        'lambda_k1': nrm((DEPTH, DA), 0.1),
        'lambda_q2': nrm((DEPTH, DA), 0.1),
        'lambda_k2': nrm((DEPTH, DA), 0.1),
        'subln_a': gain((DEPTH, V_A)),
        'conv_w': nrm((DEPTH, CONV_W, W_B), CONV_W ** -0.5),
        'conv_b': nrm((DEPTH, W_B), 0.02),
        'norm_qa': gain((DEPTH, Q_RANK)),
        'w_qb': nrm((DEPTH, Q_RANK, H_C * QK_C), Q_RANK ** -0.5),
        'norm_kva': gain((DEPTH, KV_RANK)),
        'w_kb': nrm((DEPTH, KV_RANK, H_C * NOPE_C), KV_RANK ** -0.5),
        'w_vb': nrm((DEPTH, KV_RANK, H_C * V_C), KV_RANK ** -0.5),
        'qnorm_c': gain((DEPTH, QK_C)),
        'knorm_c': gain((DEPTH, QK_C)),
        'w_out': nrm((DEPTH, MIX_W, D_MODEL), MIX_W ** -0.5),
        'ffn_w_gate': nrm((N_DENSE, D_MODEL, D_FF), s),
        'ffn_w_up': nrm((N_DENSE, D_MODEL, D_FF), s),
        'ffn_w_down': nrm((N_DENSE, D_FF, D_MODEL), D_FF ** -0.5),
        'router_w': nrm((N_MOE, D_MODEL, N_EXPERTS), s),
        'moe_w_gate': nrm((N_MOE, N_EXPERTS, D_MODEL, MOE_FF), s),
        'moe_w_up': nrm((N_MOE, N_EXPERTS, D_MODEL, MOE_FF), s),
        'moe_w_down': nrm((N_MOE, N_EXPERTS, MOE_FF, D_MODEL), MOE_FF ** -0.5),
    }

def reference(x_prompt, x_sample, cache_diff_k, cache_diff_v, cache_mla_ckv, cache_mla_krope, c, c_ctx,
              w_ada, b_ada, norm_mix, norm_ffn, w_in, qnorm_a, knorm_a, lambda_q1, lambda_k1, lambda_q2,
              lambda_k2, subln_a, conv_w, conv_b, norm_qa, w_qb, norm_kva, w_kb, w_vb, qnorm_c, knorm_c,
              w_out, ffn_w_gate, ffn_w_up, ffn_w_down, router_w, moe_w_gate, moe_w_up, moe_w_down):
    xp = x_prompt
    xs = x_sample
    st_k, st_v, st_ckv, st_kr = [], [], [], []
    for l in range(DEPTH):
        lw = {
            'w_in': w_in[l], 'w_out': w_out[l], 'norm_mix': norm_mix[l], 'norm_ffn': norm_ffn[l],
            'qnorm_a': qnorm_a[l], 'knorm_a': knorm_a[l], 'subln_a': subln_a[l],
            'conv_w': conv_w[l], 'conv_b': conv_b[l],
            'norm_qa': norm_qa[l], 'w_qb': w_qb[l], 'norm_kva': norm_kva[l],
            'w_kb': w_kb[l], 'w_vb': w_vb[l], 'qnorm_c': qnorm_c[l], 'knorm_c': knorm_c[l],
        }
        l_init = 0.8 - 0.6 * math.exp(-0.3 * l)
        lam = (jnp.exp(jnp.sum(lambda_q1[l].astype(F32) * lambda_k1[l].astype(F32)))
               - jnp.exp(jnp.sum(lambda_q2[l].astype(F32) * lambda_k2[l].astype(F32))) + l_init)
        i = l // 2
        if l % 2 == 0:
            ffn = functools.partial(swiglu, wg=ffn_w_gate[i], wu=ffn_w_up[i], wd=ffn_w_down[i])
        else:
            ffn = functools.partial(moe_ffn, router_w=router_w[i], wg=moe_w_gate[i], wu=moe_w_up[i], wd=moe_w_down[i])
        mod_ctx = (jax.nn.silu(c_ctx)[None, :] @ w_ada[l] + b_ada[l])[:, None, :]
        mod_lat = (jax.nn.silu(c) @ w_ada[l] + b_ada[l])[:, None, :]
        xp, st = trunk_layer(xp, mod_ctx, lw, lam, l_init, ffn, None)
        st_k.append(st[0])
        st_v.append(st[1])
        st_ckv.append(st[2])
        st_kr.append(st[3])
        ctx = (cache_diff_k[:, l], cache_diff_v[:, l], cache_mla_ckv[:, l], cache_mla_krope[:, l])
        xs, _ = trunk_layer(xs, mod_lat, lw, lam, l_init, ffn, ctx)
    new_diff_k = jnp.stack(st_k, axis=1)
    new_diff_v = jnp.stack(st_v, axis=1)
    new_mla_ckv = jnp.stack(st_ckv, axis=1)
    new_mla_krope = jnp.stack(st_kr, axis=1)
    return (xp, xs, new_diff_k, new_diff_v, new_mla_ckv, new_mla_krope)


_drawn_inputs = setup_inputs


def setup_inputs(seed=0):
    import zlib

    import numpy as np

    out = dict(_drawn_inputs(seed))
    spreads = {}
    factors = {'cache_mla_ckv': 4.728,
     'cache_mla_krope': 8.0,
     'qnorm_a': 8.0,
     'lambda_q1': 8.0,
     'lambda_k1': 7.572,
     'lambda_q2': 8.0,
     'lambda_k2': 5.39,
     'subln_a': 3.91,
     'conv_b': 8.0,
     'norm_qa': 8.0,
     'qnorm_c': 8.0,
     'knorm_c': 8.0}
    for name, (base, spread) in spreads.items():
        noise = np.random.default_rng([zlib.crc32(name.encode()), seed]).standard_normal(out[name].shape)
        drawn = base * np.exp(spread * noise) if base else spread * noise
        out[name] = __import__('jax').numpy.asarray(drawn.astype(out[name].dtype))
    for name, factor in factors.items():
        out[name] = (out[name] * factor).astype(out[name].dtype)
    return out
```

```python
import math
from contextlib import ExitStack

import numpy as np

import concourse.bass as bass
from concourse import mybir

P = 128
D_MODEL, KC = 1024, 8
CTX, LAT = 128, 512
TOK = CTX + LAT
NT = TOK // P
HALF = TOK // 2
DEPTH = 2
HEADS = 6
DA, VA_W = 32, 64
NOPE, ROPE_W = 64, 32
QK = NOPE + ROPE_W
Q_RANK, KV_RANK = 192, 128
QR = Q_RANK // 2
A_W = HEADS * 2 * DA
W_B = 256
C_W = Q_RANK + KV_RANK + ROPE_W
IN_COLS = 3 * A_W + 3 * W_B + C_W
B_COL = 3 * A_W
C_COL = B_COL + 3 * W_B
D_FF, EXPERTS, MOE_FF = 2816, 8, 1024
GRID_W = 64
EPS = 1e-6
KEYS = 5 * P
KT_TILES = 6

RAW_SLOTS = 4
UNIT = 2048
ADA_COLS = UNIT // KC
ADA_UNITS = 6 * D_MODEL // ADA_COLS
N_ADA = DEPTH * ADA_UNITS
U_CONV, U_QKV, U_LATENT, U_OUT, U_FFN = 0, 3, 11, 12, 16
ROUND = 12
DENSE_ROUNDS = 2
TAIL_FF = D_FF - DENSE_ROUNDS * MOE_FF
TAIL_PAIRS = TAIL_FF // 256
FFN_UNITS = [DENSE_ROUNDS * ROUND + 2 * TAIL_PAIRS + 4, EXPERTS * ROUND]
LAYER_U = [0, U_FFN + FFN_UNITS[0]]
SMALL_W = HEADS * QK * 2 + 2 * A_W

R_MIX, R_FFN, R_BADA, R_CW, R_CB, R_QA, N_ROWS = 0, 8, 16, 64, 70, 72, 74
G_QA, G_KA, G_SUB, G_KV, G_QC, G_KC, G_W = 0, 32, 64, 128, 256, 352, 448
M_SHIFT1, M_SCALE1, M_GATE1, M_SHIFT2, M_SCALE2, M_GATE2 = 0, 8, 16, 24, 32, 40

NORMS = 31
TILE_ORDER = [1, 2, 3, 4, 0]


def products_before(u, parity=None):
    n = 0
    for v in range(u):
        r = v - LAYER_U[1] if v >= LAYER_U[1] else v
        if (r < U_QKV or r >= U_OUT) and (parity is None or v % 2 == parity):
            n += 1
    return n


class Chain:

    def __init__(self, engine, sem):
        self.engine, self.sem, self.n, self.offset = engine, sem, 0, 0

    def then(self, instruction):
        self.n += 1
        instruction.then_inc(self.sem, 1)
        self.engine.wait_ge(self.sem, self.n + self.offset)

    def begin(self, offset):
        self.start, self.offset = self.n, offset
        return self.n

    def end(self, start, per, trips):
        assert self.n - start == per, (self.n - start, per)
        self.n, self.offset = start + per * trips, 0


def trunk_program(nc, I, O):
    f32, f32r = mybir.dt.float32, mybir.dt.float32r
    ALU, ACT, AX = mybir.AluOpType, mybir.ActivationFunctionType, mybir.AxisListType
    nc_base = (nc.sbuf_base + 31) // 32 * 32

    ctx = ExitStack()
    with ctx:
        def at(name, shape, offset, dt=f32):
            return nc.alloc_sbuf_tensor_at(name, shape, dt, offset=nc_base + offset)

        OFF_X, OFF_RAW, OFF_SPLIT, OFF_H = 0, 20480, 53248, 86016
        OFF_R = OFF_H + 40960
        OFF_QC, OFF_E, OFF_OB = OFF_R + 35328, OFF_R + 46848, OFF_R + 62208
        OFF_U = OFF_R + 67328
        OFF_CN = OFF_U + 3200
        OFF_S = OFF_R + 77568
        xT = at("xT", [P, KC, TOK], OFF_X)
        raw = [at(f"raw{i}", [P, UNIT], OFF_RAW + i * UNIT * 4) for i in range(RAW_SLOTS)]
        split = [at(f"split{i}", [P, 2, UNIT], OFF_SPLIT + i * UNIT * 8, f32r) for i in range(2)]
        H = at("H", [P, 2, KC, TOK], OFF_H, f32r)
        MIX = at("MIX", [P, 2, KC, TOK], OFF_H, f32r)
        VC = at("VC", [P, KT_TILES, 2, A_W], OFF_H, f32r)
        KCn = at("KCn", [P, KT_TILES, HEADS, QK], OFF_H + 18432)
        OFF_CT = OFF_H + 32256
        CQT = [at(f"CQT{i}", [QR, 2, 2, P], OFF_CT + 3072 * i, f32r) for i in range(2)]
        CKT = [at(f"CKT{i}", [P, 2, P], OFF_CT + 3072 * i + 2048, f32r) for i in range(2)]
        rope_c = at("rope_c", [P, HEADS, ROPE_W], OFF_CT + 6144)
        QA = at("QA", [P, NT, A_W], OFF_R)
        KA = at("KA", [P, KT_TILES, A_W], OFF_R + 7680)
        VA = at("VA", [P, KT_TILES, 2, A_W], OFF_R + 16896, f32r)
        rope_a = at("rope_a", [P, A_W], OFF_R + 16896)
        QC = at("QC", [P, NT, HEADS, QK], OFF_QC)
        OC = at("OC", [P, NT, HEADS * QK], OFF_QC)[:, :, 0:A_W]
        VN = at("VN", [P, KT_TILES, A_W], OFF_QC)
        WL = at("WL", [P, 2, SMALL_W], OFF_E, f32r)
        E = at("E", [P, 2, 2, KEYS], OFF_E)
        PTH = at("PTH", [P, KEYS], OFF_E + 10240, f32r)
        PTL = at("PTL", [P, KEYS], OFF_E + 12800, f32r)
        CONV = at("CONV", [P, 2, TOK], OFF_OB)
        UU = at("UU", [P, 2, TOK], OFF_U)
        rstdT = at("rstdT", [P, TOK], OFF_U)
        sqn = at("sqn", [P, HEADS * QK], OFF_U)
        CC = at("CC", [P, KV_RANK + ROPE_W], OFF_U + 2560)
        HM = at("HM", [P, 2, TOK], OFF_U + 5120)
        CN = at("CN", [P, NT, C_W], OFF_CN)
        KS = at("KS", [P, KT_TILES, 2, 4, DA], OFF_U)
        CS = at("CS", [P, NT + KT_TILES, QK], OFF_U)
        QT = [at(f"QT{s}", [P, 2, TOK], OFF_SPLIT + s * 16384, f32r) for s in range(2)]
        KT = [at(f"KT{s}", [P, 2, KT_TILES * P], OFF_SPLIT + s * 16384 + 5120, f32r) for s in range(2)]
        QS = [at(f"QS{s}", [P, NT, 2, 4, DA], OFF_SPLIT + s * 16384 + 11264) for s in range(2)]
        LT = [at(f"LT{s}", [QK, 2, (NT + KT_TILES) * P], OFF_SPLIT + s * 16384, f32r) for s in range(2)]
        ACTB = at("ACTB", [P, 2, KC, TOK], OFF_R, f32r)
        COMB = at("COMB", [P, EXPERTS, TOK], OFF_R + 40960)
        SG = at("SG", [P, 2, TOK], OFF_R + 61440)
        AT = at("AT", [P, 2, TOK], OFF_R + 66560)
        RW = at("RW", [P, KC * EXPERTS], OFF_R + 71680)
        RWS = at("RWS", [P, 2, KC * EXPERTS], OFF_R + 71936, f32r)
        LG = at("LG", [P, NT, EXPERTS], OFF_R + 72448)
        TOP = at("TOP", [P, NT, 8], OFF_R + 72608)
        IDX = at("IDX", [P, NT, 8], OFF_R + 72768, mybir.dt.uint32)
        IDXF = at("IDXF", [P, NT, 8], OFF_R + 72928)
        GT = at("GT", [P, NT, 4], OFF_R + 73088)
        CB = at("CB", [P, 2, NT, EXPERTS], OFF_R + 73184)
        xn = at("xn", [P, NT, D_MODEL], OFF_H)
        VR = at("VR", [P, DEPTH, P], OFF_R)
        CR = at("CR", [2 * KC, P], OFF_R + 1024)
        LB = at("LB", [P, DEPTH, 4, DA], OFF_R + 1536)
        s_off = [OFF_S]

        def small(name, width, dt=f32):
            t = at(name, [P, width], s_off[0], dt)
            s_off[0] += -(-width * 4 // 32) * 32
            return t

        ident, ones = small("ident", P), small("ones", P)
        MOD = small("MOD", DEPTH * 48 * 2)[:, :].rearrange("p (l m v) -> p l m v", l=DEPTH, v=2)
        GS = small("GS", DEPTH * 2 * KC * 2)[:, :].rearrange("p (l n k v) -> p l n k v", l=DEPTH, n=2, v=2)
        VEC = small("VEC", DEPTH * N_ROWS)[:, :].rearrange("p (l r) -> p l r", l=DEPTH)
        ROPE = small("ROPE", 4 * 64)[:, :].rearrange("p (t s d) -> p t s d", t=4, s=2)
        GR = small("GR", DEPTH * G_W)[:, :].rearrange("p (l g) -> p l g", l=DEPTH)
        CSIL = small("CSIL", 2 * KC)[:, :].rearrange("p (v k) -> p k v", v=2)
        LAM, LTMP = small("LAM", DEPTH), small("LTMP", DEPTH * 2)
        SS, SSC = small("SS", 24), small("SSC", 4)
        RT, RTC = small("RT", 24), small("RTC", 4)
        NT_ = small("NT_", 24)
        NM, SM, RC, CNEG = small("NM", 4), small("SM", 4), small("RC", 4), small("CNEG", 2)
        iota8, eps = small("iota8", 8), small("eps", 1)
        assert nc_base + s_off[0] <= nc.sbuf_usable_end, (nc_base + s_off[0], nc.sbuf_usable_end)

        PS = ctx.enter_context(nc.psum_tensor("PS", [P, 8, 512], f32))
        PSF = PS[:, :, :].rearrange("p b n -> p (b n)")

        names = ("const_ready small_loaded x_loaded x_turned x_stored vec_turned vec_stored silu_c "
                 "ada_used mod_ready lam_in lam_summed lam_exp setup_done "
                 "split_hi split_lo unit_used sq_ready sq_used hm_ready h_hi h_lo "
                 "setA_free setB_free proj_ready proj_free "
                 "nsq_ready nsq_used root_ready x_root eps_ready normed roped v_split cache_loaded stores "
                 "ct_turned ct_hi ct_lo lat_ready lat_q lat_k v_lo subln_gained "
                 "stack_hi stack_lo turned turnA turnB scored max_ready exp_ready w_ready pt_ready "
                 "pt_hi pt_lo o_ready o_stored lstack_q lstack_k lturned lt_hi lt_lo "
                 "subln_done mix_turned mix_hi mix_lo conv_hi conv_lo act_ready act_hi act_lo "
                 "router_loaded router_hi router_lo logits_ready top_ready top_exp comb_ready comb_turned comb_stored "
                 "y_turned y_storedA y_storedB dve act pool iota_ready").split()
        S = {n: ctx.enter_context(nc.semaphore(n)) for n in names}
        raw_ready = [ctx.enter_context(nc.semaphore(f"raw_ready{i}")) for i in range(RAW_SLOTS)]
        set_free = [S["setA_free"], S["setB_free"]]
        block = ctx.enter_context(nc.Block())

        def raw_count(n):
            extra = sum(32 for l in range(DEPTH)
                        if N_ADA + LAYER_U[l] + U_LATENT <= n
                        and (N_ADA + LAYER_U[l] + U_LATENT - n) % RAW_SLOTS == 0)
            return 16 * (n // RAW_SLOTS + 1) + extra

        def layer_rounds(l):
            return (DENSE_ROUNDS, TAIL_PAIRS) if l == 0 else (EXPERTS, 0)

        V_RANGES = [(0, 0, CTX), (1, CTX, TOK)]

        HALVES = [[(0, 0, CTX), (1, CTX, HALF)], [(1, 0, HALF)]]

        root_at = [l * NORMS + m + 1 for l in range(DEPTH) for m in range(NORMS) if not 2 * NT <= m < 3 * NT]

        def sets(u, r, parity):
            n = products_before(u, parity)
            return n if r is None else r * (ROUND // 2) + n

        @block.sync
        def _(sp):
            def free_slot(n, value=None):
                if n < RAW_SLOTS:
                    return
                m = n - RAW_SLOTS
                if m < N_ADA:
                    sp.wait_ge(S["ada_used"], m + 1)
                else:
                    sp.wait_ge(S["split_lo"], m - N_ADA + 1 + (0 if value is None else value))

            def load(n, source, kc, cols, value=None):
                free_slot(n, value)
                dst = raw[n % RAW_SLOTS][:, 0:kc * cols].rearrange("p (k c) -> p k c", k=kc)
                sp.dma_start(dst, source).then_inc(raw_ready[n % RAW_SLOTS], 16)

            def chunks(w):
                return w.rearrange("(k p) n -> p k n", p=P)

            for t in range(NT):
                src = I["x_prompt"][0] if t == 0 else I["x_sample"][0, (t - 1) * P:t * P]
                sp.dma_start(xn[:, t, :], src).then_inc(S["x_loaded"], 16)
            sp.wait_ge(S["const_ready"], 3)
            for v, name in enumerate(("c_ctx", "c")):
                src = (I[name] if v == 0 else I[name][0]).rearrange("(k p) -> k p", p=P)
                sp.dma_start(CR[v * KC:(v + 1) * KC, :], src).then_inc(S["small_loaded"], 16)
            for l in range(DEPTH):
                for row, name, n in ((R_MIX, "norm_mix", 8), (R_FFN, "norm_ffn", 8), (R_BADA, "b_ada", 48),
                                     (R_CB, "conv_b", 2)):
                    sp.dma_start(VR[row:row + n, l, :], I[name][l].rearrange("(k p) -> k p", p=P)).then_inc(
                        S["small_loaded"], 16)
                sp.dma_start(VR[R_CW:R_CW + 6, l, :], I["conv_w"][l].rearrange("w (k p) -> (w k) p", p=P)).then_inc(
                    S["small_loaded"], 16)
                sp.dma_start(VR[R_QA:R_QA + 2, l, 0:QR], I["norm_qa"][l].rearrange("(k p) -> k p", p=QR)).then_inc(
                    S["small_loaded"], 16)
            N_COLUMN_LOADS = 2 + 6 * DEPTH
            for l in range(DEPTH):
                w = chunks(I["w_ada"][l])
                for j in range(ADA_UNITS):
                    n = l * ADA_UNITS + j
                    load(n, w[:, :, j * ADA_COLS:(j + 1) * ADA_COLS], KC, ADA_COLS)
            for l in range(DEPTH):
                base = N_ADA + LAYER_U[l]
                w = chunks(I["w_in"][l])
                for j, col in enumerate((B_COL + W_B, B_COL + 2 * W_B, B_COL)):
                    load(base + U_CONV + j, w[:, :, col:col + W_B], KC, W_B)
                for g in range(4):
                    col, width = (g * A_W, A_W) if g < 3 else (C_COL, C_W)
                    for half in range(2):
                        load(base + U_QKV + 2 * g + half, w[:, 4 * half:4 * half + 4, col:col + width], 4, width)
                n = base + U_LATENT
                free_slot(n)
                dst = raw[n % RAW_SLOTS]
                qw = HEADS * QK
                sp.dma_start(dst[0:QR, 0:2 * qw].rearrange("p (k c) -> p k c", k=2),
                             I["w_qb"][l].rearrange("(k p) n -> p k n", p=QR)).then_inc(raw_ready[n % RAW_SLOTS], 16)
                sp.dma_start(dst[:, 2 * qw:2 * qw + A_W], I["w_kb"][l]).then_inc(raw_ready[n % RAW_SLOTS], 16)
                sp.dma_start(dst[:, 2 * qw + A_W:SMALL_W], I["w_vb"][l]).then_inc(raw_ready[n % RAW_SLOTS], 16)
                w = chunks(I["w_out"][l])
                for j in range(4):
                    load(base + U_OUT + j, w[:, :, j * 256:(j + 1) * 256], KC, 256)

                n0 = base + U_FFN
                rounds, tail = layer_rounds(l)
                with sp.Fori(0, rounds) as r:
                    if l == 0:
                        wg = I["ffn_w_gate"][0].rearrange("(k p) (r n) -> p k r n", p=P, n=256)
                        wu = I["ffn_w_up"][0].rearrange("(k p) (r n) -> p k r n", p=P, n=256)
                        wd = I["ffn_w_down"][0].rearrange("(r p) n -> p r n", p=P)
                    for j in range(4):
                        n = n0 + 2 * j
                        if l == 0:
                            load(n, wg[:, :, bass.ds(r * 4 + j, 1), :], KC, 256, r * ROUND)
                            load(n + 1, wu[:, :, bass.ds(r * 4 + j, 1), :], KC, 256, r * ROUND)
                        else:
                            for i, name in enumerate(("moe_w_gate", "moe_w_up")):
                                w_ = I[name][0].rearrange("e (k p) n -> p (e k) n", p=P)
                                load(n + i, w_[:, bass.ds(r * KC, KC), j * 256:(j + 1) * 256], KC, 256, r * ROUND)
                    for j in range(4):
                        if l == 0:
                            src = wd[:, bass.ds(r * KC, KC), j * 256:(j + 1) * 256]
                        else:
                            w_ = I["moe_w_down"][0].rearrange("e (k p) n -> p (e k) n", p=P)
                            src = w_[:, bass.ds(r * KC, KC), j * 256:(j + 1) * 256]
                        load(n0 + 8 + j, src, KC, 256, r * ROUND)
                if tail:
                    n = n0 + rounds * ROUND
                    first = rounds * MOE_FF
                    for j in range(tail):
                        for i, name in enumerate(("ffn_w_gate", "ffn_w_up")):
                            c = first + j * 256
                            load(n + 2 * j + i, chunks(I[name][0])[:, :, c:c + 256], KC, 256)
                    for j in range(4):
                        src = I["ffn_w_down"][0][first:].rearrange("(k p) n -> p k n", p=P)
                        load(n + 2 * tail + j, src[:, :, j * 256:(j + 1) * 256], TAIL_FF // P, 256)

        @block.gpsimd
        def _(pool):
            ch = Chain(pool, S["pool"])
            nc.gpsimd.memset(ones[:, :], 1.0).then_inc(S["const_ready"], 1)
            nc.gpsimd.memset(VR[:, :, :], 0.0).then_inc(S["const_ready"], 1)
            ch.then(nc.gpsimd.memset(ident[:, :], 0.0))
            nc.gpsimd.affine_select(out=ident[:, :], in_=ident[:, :], compare_op=ALU.not_equal, fill=1.0, base=0,
                                    pattern=[[-1, P]], channel_multiplier=1).then_inc(S["const_ready"], 1)
            nc.gpsimd.memset(eps[:, :], EPS).then_inc(S["eps_ready"], 1)
            for e in range(8):
                nc.gpsimd.memset(iota8[:, e:e + 1], float(e)).then_inc(S["iota_ready"], 1)
            n_rows = 0
            for l in range(DEPTH):
                for col, name, n in ((G_QA, "qnorm_a", DA), (G_KA, "knorm_a", DA), (G_SUB, "subln_a", VA_W),
                                     (G_KV, "norm_kva", KV_RANK), (G_QC, "qnorm_c", QK), (G_KC, "knorm_c", QK)):
                    pool.dma_start(GR[:, l, col:col + n], I[name][l:l + 1, :].broadcast_to([P, n])).then_inc(
                        S["lam_in"], 16)
                for i, name in enumerate(("lambda_q1", "lambda_k1", "lambda_q2", "lambda_k2")):
                    pool.dma_start(LB[:, l, i, :], I[name][l:l + 1, :].broadcast_to([P, DA])).then_inc(
                        S["lam_in"], 16)
            pool.dma_start(ROPE[:, :, :, :], I["rope"].rearrange("p (t s d) -> p t s d", t=4, s=2)).then_inc(
                S["lam_in"], 16)

            def gain_rope(l, buf, t, groups, d, col, scratch, rotate):
                x = buf
                gain = GR[:, l, col:col + d].unsqueeze(1).broadcast_to([P, groups, d])
                ins = nc.gpsimd.tensor_tensor(x, x, gain, ALU.mult)
                if not rotate:
                    ins.then_inc(S["roped"], 1)
                    return
                ch.then(ins)
                tail = x[:, :, d - ROPE_W:d]
                pairs = tail.rearrange("p g (h s n) -> p g h s n", h=2, s=2)
                out = scratch.rearrange("p g (h s n) -> p g h s n", h=2, s=2)
                cos, sin = ROPE[:, t - 1, 0, :], ROPE[:, t - 1, 1, :].rearrange("p (h s n) -> p h s n", h=2, s=2)
                for s in range(2):
                    ins = nc.gpsimd.tensor_tensor(
                        out[:, :, :, s, :], pairs[:, :, :, 1 - s, :],
                        sin[:, :, s, :].unsqueeze(1).broadcast_to([P, groups, 2, 8]), ALU.mult)
                ch.then(ins)
                ch.then(nc.gpsimd.tensor_tensor(tail, tail, cos.unsqueeze(1).broadcast_to([P, groups, ROPE_W]),
                                                ALU.mult))
                nc.gpsimd.tensor_tensor(tail, tail, scratch, ALU.add).then_inc(S["roped"], 1)

            pool.wait_ge(S["setup_done"], 1)
            pool.wait_ge(S["iota_ready"], 8)
            stores = 0

            for l in range(DEPTH):
                for m in range(2 * NT):
                    g, t = m // NT, m % NT
                    buf = QA if g == 0 else KA
                    pool.wait_ge(S["normed"], l * 21 + m + 1)
                    gain_rope(l, buf[:, t, :].rearrange("p (g d) -> p g d", d=DA), t, 2 * HEADS, DA,
                              (G_QA, G_KA)[g], rope_a[:, :].rearrange("p (g d) -> p g d", d=DA), t > 0)
                    if g == 1 and t == 0:
                        pool.wait_ge(S["roped"], l * 21 + NT + 1)
                        pool.dma_start(O["new_diff_k"][0, l].rearrange("s h c d -> s (h c d)"),
                                       KA[:, 0, :]).then_inc(S["stores"], 16)
                        stores += 16
                pool.wait_ge(S["roped"], l * 21 + 2 * NT)
                pool.wait_ge(S["cache_loaded"], (l + 1) * 64)
                for t in range(KT_TILES):
                    if t < NT:
                        pool.wait_ge(S["proj_free"], l * 20 + 2 * NT + t + 1)
                    if t == 0:
                        pool.dma_start(O["new_diff_v"][0, l].rearrange("s h e -> s (h e)"),
                                       VN[:, 0, :]).then_inc(S["stores"], 16)
                        stores += 16
                    ch.then(nc.gpsimd.tensor_copy(VA[:, t, 0, :], VN[:, t, :]))
                    nc.gpsimd.tensor_tensor(VA[:, t, 1, :], VN[:, t, :], VA[:, t, 0, :].bitcast(f32),
                                            ALU.subtract).then_inc(S["v_split"], 1)
                pool.wait_ge(S["stores"], stores)
                pool.wait_ge(S["nsq_used"], l * NORMS + 2 * NT + 1)
                pool.dma_start(O["new_mla_ckv"][0, l], CN[:, 0, Q_RANK:Q_RANK + KV_RANK]).then_inc(S["stores"], 16)
                pool.dma_start(O["new_mla_krope"][0, l], CN[:, 0, Q_RANK + KV_RANK:C_W]).then_inc(S["stores"], 16)
                stores += 32
                tiles = [(i % 2, i // 2) for i in range(2 * NT)] + [(1, NT)]
                for i, (k, t) in enumerate(tiles):
                    pool.wait_ge(S["normed"], l * 21 + 2 * NT + i + 1)
                    gain_rope(l, KCn[:, t, :, :] if k else QC[:, t, :, :], t, HEADS, QK, G_KC if k else G_QC,
                              rope_c[:, :, :], 0 < t < 5)
                for t in range(NT):
                    pool.wait_ge(S["subln_done"], l * NT + t + 1)
                    v = QA[:, t, :].rearrange("p (h e) -> p h e", e=VA_W)
                    gain = GR[:, l, G_SUB:G_SUB + VA_W].unsqueeze(1).broadcast_to([P, HEADS, VA_W])
                    nc.gpsimd.tensor_tensor(v, v, gain, ALU.mult).then_inc(S["subln_gained"], 1)
            for t in range(NT):
                pool.wait_ge(S["y_storedA"], t + 1)
                pool.wait_ge(S["y_storedB"], t + 1)
                dst = O["y_prompt"][0] if t == 0 else O["y_sample"][0, (t - 1) * P:t * P]
                pool.dma_start(dst, xn[:, t, :]).then_inc(S["stores"], 16)
                stores += 16
            pool.wait_ge(S["stores"], stores)


        N_ROW_LOADS = 10 * DEPTH + 1

        def unit_width(l, k):
            if U_QKV <= k < U_LATENT:
                return 4 * (A_W if k < U_QKV + 6 else C_W)
            if l == 0 and k >= U_FFN + DENSE_ROUNDS * ROUND + 2 * TAIL_PAIRS:
                return TAIL_FF // P * 256
            return UNIT

        def mixer_act(A, act, l, base, split_hi, squares, nsq, root):
            act.wait_ge(S["unit_used"], base + 1)
            A.copy(UU[:, :, :].rearrange("p c (h n) -> p (c h) n", h=2), PS[:, 0:4, 0:HALF]).then_inc(S["setA_free"], 1)
            split_hi(base + 2)
            split_hi(base + 3)
            split_hi(base + 4)
            act.wait_ge(set_free[0], products_before(base, 0) + 2)
            if l:
                act.wait_ge(S["stores"], l * 64)
            act.dma_start(KA[:, 5, :], I["cache_diff_k"][0, l].rearrange("s h c d -> s (h c d)")).then_inc(
                S["cache_loaded"], 16)
            act.dma_start(VN[:, 5, :], I["cache_diff_v"][0, l].rearrange("s h e -> s (h e)")).then_inc(
                S["cache_loaded"], 16)
            act.dma_start(CC[:, 0:KV_RANK], I["cache_mla_ckv"][0, l]).then_inc(S["cache_loaded"], 16)
            act.dma_start(CC[:, KV_RANK:], I["cache_mla_krope"][0, l]).then_inc(S["cache_loaded"], 16)
            for g in range(4):
                split_hi(base + U_QKV + 2 * g + 2)
                for t in range(NT):
                    m = g * NT + t
                    if t < NT - 1:
                        act.wait_ge(S["proj_ready"], l * 16 + g * (NT - 1) + t + 1)
                    else:
                        act.wait_ge(S["unit_used"], base + U_QKV + 2 * g + 2)
                    dst, w = ((QA[:, t, :], A_W), (KA[:, t, :], A_W), (VN[:, t, :], A_W), (CN[:, t, :], C_W))[g]
                    A.copy(dst, PS[:, m % 8, 0:w]).then_inc(S["proj_free"], 1)
                    if g < 2:
                        act.wait_ge(S["proj_free"], l * 20 + m + 1)
                        squares(dst, A_W).then_inc(S["nsq_ready"], 1)
                        nsq[0] += 1
                        if t:
                            root(2 * HEADS, DA)
                if g < 2:
                    root(2 * HEADS, DA)
                if g < 3:
                    split_hi(base + U_QKV + 2 * g + 3)
            act.wait_ge(S["proj_free"], l * 20 + 20)
            for t in range(NT):
                ssq = SSC[:, 2 * (t % 2):2 * (t % 2) + 2]
                squares(CN[:, t, 0:Q_RANK], Q_RANK, accum=ssq[:, 0:1]).then_inc(S["act"], 1)
                act.wait_ge(S["act"], 3 * (l * NT + t) + 1)
                A.activation(sqn[:, 0:KV_RANK], CN[:, t, Q_RANK:Q_RANK + KV_RANK], ACT.Square,
                             accum_out=ssq[:, 1:2]).then_inc(S["act"], 1)
                act.wait_ge(S["act"], 3 * (l * NT + t) + 2)
                A.activation(ssq[:, 0:1], ssq[:, 0:1], ACT.Identity, bias=eps[:, :], scale=1.0 / Q_RANK)
                A.activation(ssq[:, 1:2], ssq[:, 1:2], ACT.Identity, bias=eps[:, :], scale=1.0 / KV_RANK).then_inc(
                    S["act"], 1)
                act.wait_ge(S["act"], 3 * (l * NT + t) + 3)
                A.activation(RTC[:, 2 * (t % 2):2 * (t % 2) + 2], ssq, ACT.Sqrt).then_inc(S["nsq_ready"], 1)
                nsq[0] += 1

            act.wait_ge(S["unit_used"], base + U_LATENT)
            act.wait_ge(S["stores"], l * 64 + 32)
            act.wait_ge(S["v_split"], 6 * (l + 1))

            def turned_hi(t):
                act.wait_ge(S["ct_turned"], l * KT_TILES + t + 1)
                bank = PS[:, t % 2, :]
                if t < NT:
                    for j in range(2):
                        A.activation(CQT[t % 2][:, 0, j, :], bank[0:QR, j * P:(j + 1) * P], ACT.Identity,
                                     scale=VEC[0:QR, l, R_QA + j:R_QA + j + 1])
                A.copy(CKT[t % 2][:, 0, :], bank[:, 2 * P:3 * P]).then_inc(S["ct_hi"], 1)

            turned_hi(0)
            for t in range(KT_TILES):
                if t + 1 < KT_TILES:
                    turned_hi(t + 1)
                act.wait_ge(S["lat_ready"], l * KT_TILES + t + 1)
                if t < NT:
                    A.copy(QC[:, t, :, :].rearrange("p h d -> p (h d)").rearrange("p (a n) -> p a n", a=2),
                           PS[:, 2:4, 0:288]).then_inc(S["lat_q"], 1)
                rope = CN[:, t, Q_RANK + KV_RANK:C_W] if t < NT else CC[:, KV_RANK:]
                A.copy(KCn[:, t, :, NOPE:QK], rope.unsqueeze(1).broadcast_to([P, HEADS, ROPE_W]))
                A.copy(KCn[:, t, :, 0:NOPE], PS[:, 4, 0:A_W].rearrange("p (h d) -> p h d", h=HEADS))
                A.copy(VC[:, t, 0, :], PS[:, 5, 0:A_W]).then_inc(S["lat_k"], 1)
                if t < NT:
                    act.wait_ge(S["lat_q"], l * NT + t + 1)
                    squares(QC[:, t, :, :], HEADS * QK, HEADS).then_inc(S["nsq_ready"], 1)
                    nsq[0] += 1
                act.wait_ge(S["lat_k"], l * KT_TILES + t + 1)
                squares(KCn[:, t, :, :], HEADS * QK, HEADS).then_inc(S["nsq_ready"], 1)
                nsq[0] += 1
                if t < NT:
                    root(HEADS, QK)
                root(HEADS, QK)

            act.wait_ge(S["roped"], (l + 1) * 21)
            act.wait_ge(S["cache_loaded"], (l + 1) * 64)
            act.wait_ge(S["stores"], (l + 1) * 64)

            def head_items(comps, head, item0, score0):
                def exps(ti):
                    par = (head + ti) % 2
                    cols = KEYS if TILE_ORDER[ti] else P
                    for c in range(comps):
                        slot = c if comps == 2 else par
                        act.wait_ge(S["max_ready"], score0 + comps * ti + c + 1)
                        out = E[:, par, c, 0:cols]
                        if cols == KEYS:
                            src, out = PS[:, 2 + 2 * slot:4 + 2 * slot, 0:HALF], out.rearrange("p (a n) -> p a n", a=2)
                        else:
                            src = PS[:, 2 + 2 * slot, 0:P]
                        A.activation(out, src, ACT.Exp, bias=NM[:, 2 * par + c:2 * par + c + 1],
                                     accum_out=SM[:, 2 * par + c:2 * par + c + 1]).then_inc(S["exp_ready"], 1)

                exps(0)
                for ti in range(NT):
                    if ti + 1 < NT:
                        exps(ti + 1)
                    cols = KEYS if TILE_ORDER[ti] else P
                    act.wait_ge(S["pt_ready"], item0 + ti + 1)
                    if ti:
                        act.wait_ge(S["o_ready"], item0 + ti)
                    A.copy(PTH[:, 0:cols], PSF[:, 3072:3072 + cols]).then_inc(S["pt_hi"], 1)

            with act.Fori(0, HEADS // 2) as i:
                for s in range(2):
                    h = i * 2 + s
                    item0 = h * NT + l * 60
                    for buf, stack, rows in ((QA, QS[s], (0, 2)), (KA, KS, (0, 1))):
                        src = buf[:, :, bass.ds(h * 2 * DA, 2 * DA)].rearrange("p t (c d) -> p t c d", c=2)
                        for row in rows:
                            ins = A.copy(stack[:, :, :, row, :].bitcast(f32r), src)
                    ins.then_inc(S["stack_hi"], 1)
                    for g in (0, 2, 4):
                        act.wait_ge(S["turned"], h * 6 + l * 36 + g + 1)
                        dst = (QT[s] if g < 3 else KT[s])[:, :, :].rearrange("p c n -> p (c n)")
                        first = 512 * (g % 3)
                        n = min(512, (2 * TOK if g < 3 else 12 * P) - first)
                        A.copy(dst[:, first:first + n], PS[:, 0, 0:n]).then_inc(S["turnA"], 1)
                    head_items(2, s, item0, h * 10 + l * 90)

            with act.Fori(0, HEADS // 2) as i:
                for s in range(2):
                    h = i * 2 + s
                    item0 = h * NT + l * 60 + 30
                    act.wait_ge(S["o_ready"], item0)
                    A.copy(CS[:, 0:NT, :], QC[:, :, bass.ds(h, 1), :].rearrange("p t a d -> p t (a d)")).then_inc(
                        S["lstack_q"], 1)
                    for g in range(3):
                        act.wait_ge(S["lturned"], h * 3 + l * 18 + g + 1)
                        n = min(512, 11 * P - 512 * g)
                        A.copy(LT[s][:, 0, 512 * g:512 * g + n], PS[0:QK, g % 2, 0:n]).then_inc(S["lt_hi"], 1)
                    head_items(1, s, item0, h * NT + l * 90 + 60)

            act.wait_ge(S["o_stored"], (l + 1) * 60)
            split_hi(base + U_OUT)
            A.copy(MIX[:, 0, 3:5, :], CONV[:, :, :]).then_inc(S["conv_hi"], 1)
            for t in range(NT):
                squares(QA[:, t, :], A_W).then_inc(S["nsq_ready"], 1)
                nsq[0] += 1
                if t:
                    root(HEADS, VA_W)
            root(HEADS, VA_W)
            for w in range(2 * NT):
                t, i = w // 2, w % 2
                act.wait_ge(S["mix_turned"], l * 10 + w + 1)
                A.copy(MIX[:, 0, 5 * i:5 * i + 3, t * P:(t + 1) * P],
                       PS[:, i, 0:3 * P].rearrange("p (c n) -> p c n", c=3)).then_inc(S["mix_hi"], 1)
            for k in range(1, 6):
                split_hi(base + U_OUT + k)
            if l == 1:
                act.dma_start(RW[:, :].rearrange("p (k e) -> p k e", e=EXPERTS),
                              I["router_w"][0].rearrange("(k p) e -> p k e", p=P)).then_inc(S["router_loaded"], 16)
                act.wait_ge(S["router_loaded"], 16)
                A.copy(RWS[:, 0, :], RW[:, :]).then_inc(S["router_hi"], 1)

        def ffn_act(A, act, l, base, split_hi):
            rounds, tail = layer_rounds(l)
            acts0 = 0 if l == 0 else 4 * DENSE_ROUNDS + TAIL_PAIRS

            def round_(r, u0, pairs, extra, ahead):
                d_pairs, d_u = extra
                for k in range(2 * pairs + 4):
                    if k < 2 * pairs:
                        j = k // 2
                        if k % 2 == 0:
                            act.wait_ge(S["unit_used"], u0 + k + 1 + d_u)
                            act.wait_ge(set_free[1], sets(u0 + k, r, 1))
                            A.activation(SG[:, :, :].rearrange("p c (h n) -> p (c h) n", h=2), PS[:, 0:4, 0:HALF],
                                         ACT.Silu).then_inc(set_free[0], 1)
                        else:
                            if l == 0:
                                act.wait_ge(set_free[1], sets(u0 + k, r, 1) + 1)
                            else:
                                act.wait_ge(S["act_ready"], j + 1 + d_pairs)
                            if j == 0:
                                act.wait_ge(S["unit_used"], u0 + d_u)
                            A.copy(ACTB[:, 0, 2 * j:2 * j + 2, :], AT[:, :, :]).then_inc(S["act_hi"], 1)
                    if k + 2 < 2 * pairs + 4 or ahead:
                        split_hi(u0 + k + 2, r)

            u0 = base + U_FFN
            looped = rounds if tail else rounds - 1
            with act.Fori(0, looped) as r:
                round_(r, u0, 4, (r * 4, r * ROUND), True)
            if tail:
                round_(None, u0 + rounds * ROUND, tail, (rounds * 4, 0), True)
            else:
                round_(None, u0 + looped * ROUND, 4, (looped * 4, 0), False)

        @block.scalar
        def _(act):
            A = nc.scalar

            def split_hi(u, r=None):
                du = 0 if r is None else r * ROUND
                n = N_ADA + u
                act.wait_ge(raw_ready[n % RAW_SLOTS], raw_count(n) + (0 if r is None else r * (ROUND // RAW_SLOTS * 16)))
                if u >= 2:
                    act.wait_ge(S["unit_used"], u - 1 + du)
                k = u - LAYER_U[1] if u >= LAYER_U[1] else u
                src = raw[n % RAW_SLOTS]
                if k == U_LATENT:
                    qw = 2 * HEADS * QK
                    A.copy(WL[0:QR, 0, 0:qw], src[0:QR, 0:qw])
                    A.copy(WL[:, 0, qw:SMALL_W], src[:, qw:SMALL_W]).then_inc(S["split_hi"], 1)
                    return
                w = unit_width(int(u >= LAYER_U[1]), k)
                A.copy(split[u % 2][:, 0, 0:w], src[:, 0:w]).then_inc(S["split_hi"], 1)

            act.wait_ge(S["vec_stored"], 1)
            A.activation(CSIL, CSIL, ACT.Silu).then_inc(S["silu_c"], 1)
            act.wait_ge(S["lam_summed"], 1)
            A.activation(LTMP[:, :], LTMP[:, :], ACT.Exp).then_inc(S["lam_exp"], 1)
            act.wait_ge(S["setup_done"], 1)
            act.wait_ge(S["eps_ready"], 1)
            split_hi(0)
            split_hi(1)
            nsq = [0]

            def squares(src, n, g=None, accum=None):
                if nsq[0]:
                    act.wait_ge(S["nsq_used"], nsq[0])
                ins = A.activation(sqn[:, 0:n] if g is None else sqn[:, 0:n].rearrange("p (g d) -> p g d", g=g), src,
                                   ACT.Square, **({} if accum is None else {"accum_out": accum}))
                return ins

            nroot = [0]

            def root(g, d):
                m = nroot[0] % 2
                act.wait_ge(S["nsq_used"], root_at[nroot[0]])
                sums = SS[:, 12 * m:12 * m + g]
                A.activation(RT[:, 12 * m:12 * m + g], sums, ACT.Sqrt).then_inc(S["root_ready"], 1)
                nroot[0] += 1

            for l in range(DEPTH):
                base = LAYER_U[l]
                for norm in range(2):
                    q = 2 * l + norm
                    if q == 0:
                        act.wait_ge(S["x_stored"], 2 * NT)
                        act.wait_ge(S["small_loaded"], 16)
                    else:
                        last = base if norm == 0 else base + U_FFN
                        for s in range(2):
                            act.wait_ge(set_free[s], products_before(last, s))
                    for kc in range(KC):
                        if kc >= 2:
                            act.wait_ge(S["sq_used"], q * KC + kc - 1)
                        A.activation(HM[:, kc % 2, :], xT[:, kc, :], ACT.Square).then_inc(S["sq_ready"], 1)
                    act.wait_ge(S["sq_used"], (q + 1) * KC)
                    A.activation(rstdT[:, :].rearrange("p (h n) -> p h n", h=2), PS[:, 0:2, 0:HALF], ACT.Sqrt,
                                 bias=eps[:, :], scale=1.0 / D_MODEL).then_inc(S["x_root"], 1)
                    if q == 0:
                        act.wait_ge(S["mod_ready"], 1)
                    for kc in range(KC):
                        act.wait_ge(S["hm_ready"], q * KC + kc + 1)
                        for v, a, b in V_RANGES:
                            sh = MOD[:, l, (M_SHIFT1, M_SHIFT2)[norm] + kc, v:v + 1]
                            ins = A.activation(H[:, 0, kc, a:b], HM[:, kc % 2, a:b], ACT.Identity, bias=sh)
                        ins.then_inc(S["h_hi"], 1)
                    if norm == 0:
                        mixer_act(A, act, l, base, split_hi, squares, nsq, root)
                    else:
                        if l == 1:
                            act.wait_ge(S["top_ready"], 1)
                            A.activation(GT[:, :, 1:2], GT[:, :, 0:1], ACT.Exp).then_inc(S["top_exp"], 1)
                        ffn_act(A, act, l, base, split_hi)
            for t in range(NT):
                act.wait_ge(S["y_turned"], 2 * t + 1)
                A.copy(xn[:, t, 0:512], PS[:, 0, :]).then_inc(S["y_storedA"], 1)

        def mixer_dve(V, dve, ch, l, base, split_lo, sums, finish, refine, nsq):
            for g in range(4):
                split_lo(base + U_QKV + 2 * g + 2)
                if g < 2:
                    for t in range(NT + 1):
                        n = l * 21 + g * NT
                        if t < NT:
                            sums(2 * HEADS, DA, (S["normed"], n + t - 1) if g * NT + t > 1 else None)
                        if t:
                            finish((QA, KA)[g][:, t - 1, :].rearrange("p (g d) -> p g d", d=DA)).then_inc(
                                S["normed"], 1)
                if g < 3:
                    split_lo(base + U_QKV + 2 * g + 3)
            for t in range(NT):
                dve.wait_ge(S["nsq_ready"], nsq[0] + 1)
                nsq[0] += 1
                h = 2 * (t % 2)
                r = RTC[:, h:h + 2]
                refine(r, r, SSC[:, h:h + 2], NT_[:, h:h + 2])
                V.tensor_scalar(CN[:, t, 0:Q_RANK], CN[:, t, 0:Q_RANK], r[:, 0:1], None, ALU.mult)
                kv = CN[:, t, Q_RANK:Q_RANK + KV_RANK]
                V.scalar_tensor_tensor(out=kv, in0=kv, scalar=r[:, 1:2], in1=GR[:, l, G_KV:G_KV + KV_RANK],
                                       op0=ALU.mult, op1=ALU.mult).then_inc(S["nsq_used"], 1)

            def turned_lo(t):
                dve.wait_ge(S["ct_hi"], l * KT_TILES + t + 1)
                bank = PS[:, t % 2, :]
                if t < NT:
                    for j in range(2):
                        V.scalar_tensor_tensor(out=CQT[t % 2][:, 1, j, :], in0=bank[0:QR, j * P:(j + 1) * P],
                                               scalar=VEC[0:QR, l, R_QA + j:R_QA + j + 1],
                                               in1=CQT[t % 2][:, 0, j, :].bitcast(f32), op0=ALU.mult, op1=ALU.subtract)
                V.tensor_tensor(CKT[t % 2][:, 1, :], bank[:, 2 * P:3 * P], CKT[t % 2][:, 0, :].bitcast(f32),
                                ALU.subtract).then_inc(S["ct_lo"], 1)

            turned_lo(0)
            for t in range(KT_TILES):
                if t + 1 < KT_TILES:
                    turned_lo(t + 1)
                dve.wait_ge(S["lat_k"], l * KT_TILES + t + 1)
                V.tensor_tensor(VC[:, t, 1, :], PS[:, 5, 0:A_W], VC[:, t, 0, :].bitcast(f32), ALU.subtract).then_inc(
                    S["v_lo"], 1)
                n = l * 21 + 2 * NT + 2 * t
                if t < NT:
                    sums(HEADS, QK, (S["normed"], n))
                sums(HEADS, QK, (S["normed"], n))
                if t < NT:
                    finish(QC[:, t, :, :]).then_inc(S["normed"], 1)
                finish(KCn[:, t, :, :]).then_inc(S["normed"], 1)

            def head_items(comps, head, item0, score0, store):
                def maxima(ti):
                    par = (head + ti) % 2
                    for c in range(comps):
                        slot = c if comps == 2 else par
                        dve.wait_ge(S["scored"], score0 + comps * ti + c + 1)
                        if TILE_ORDER[ti]:
                            src, ax = PS[:, 2 + 2 * slot:4 + 2 * slot, 0:HALF], AX.XY
                        else:
                            src, ax = PS[:, 2 + 2 * slot, 0:P], AX.X
                        V.tensor_reduce(NM[:, 2 * par + c:2 * par + c + 1], src, op=ALU.max, axis=ax,
                                        negate=True).then_inc(S["max_ready"], 1)

                maxima(0)
                for ti in range(NT):
                    if ti + 1 < NT:
                        maxima(ti + 1)
                    par = (head + ti) % 2
                    cols = KEYS if TILE_ORDER[ti] else P
                    dve.wait_ge(S["exp_ready"], score0 + comps * (ti + 1))
                    ch.then(V.reciprocal(RC[:, 2 * par:2 * par + comps], SM[:, 2 * par:2 * par + comps]))
                    if comps == 2:
                        ch.then(V.tensor_scalar(CNEG[:, par:par + 1], RC[:, 2 * par + 1:2 * par + 2],
                                                SM[:, 2 * par:2 * par + 1], LAM[:, l:l + 1], ALU.mult, ALU.mult))
                        V.scalar_tensor_tensor(out=E[:, par, 0, 0:cols], in0=E[:, par, 1, 0:cols],
                                               scalar=CNEG[:, par:par + 1], in1=E[:, par, 0, 0:cols],
                                               op0=ALU.mult, op1=ALU.add).then_inc(S["w_ready"], 1)
                    dve.wait_ge(S["pt_hi"], item0 + ti + 1)
                    V.tensor_tensor(PTL[:, 0:cols], PSF[:, 3072:3072 + cols], PTH[:, 0:cols].bitcast(f32),
                                    ALU.subtract).then_inc(S["pt_lo"], 1)
                    dve.wait_ge(S["o_ready"], item0 + ti + 1)
                    V.tensor_scalar(store(TILE_ORDER[ti]), PS[:, par, 0:VA_W],
                                    RC[:, 2 * par:2 * par + 1], None, ALU.mult).then_inc(S["o_stored"], 1)

            dve.wait_ge(S["roped"], (l + 1) * 21)
            dve.wait_ge(S["cache_loaded"], (l + 1) * 64)
            with dve.Fori(0, HEADS // 2) as i:
                start = ch.begin(i * 20)
                for s in range(2):
                    h = i * 2 + s
                    dve.wait_ge(S["stack_hi"], h + l * HEADS + 1)
                    for buf, stack, rows in ((QA, QS[s], (1, 3)), (KA, KS, (2, 3))):
                        src = buf[:, :, bass.ds(h * 2 * DA, 2 * DA)].rearrange("p t (c d) -> p t c d", c=2)
                        for row in rows:
                            ins = V.tensor_tensor(stack[:, :, :, row, :].bitcast(f32r), src, stack[:, :, :, 0, :],
                                                  ALU.subtract)
                    ins.then_inc(S["stack_lo"], 1)
                    for g in (1, 3, 5):
                        dve.wait_ge(S["turned"], h * 6 + l * 36 + g + 1)
                        dst = (QT[s] if g < 3 else KT[s])[:, :, :].rearrange("p c n -> p (c n)")
                        first = 512 * (g % 3)
                        V.tensor_copy(dst[:, first:first + 512], PS[:, 1, :]).then_inc(S["turnB"], 1)
                    head_items(2, s, h * NT + l * 60, h * 10 + l * 90,
                               lambda t, h=h: QA[:, t, bass.ds(h * VA_W, VA_W)])
                ch.end(start, 20, HEADS // 2)
            with dve.Fori(0, HEADS // 2) as i:
                start = ch.begin(i * 10)
                for s in range(2):
                    h = i * 2 + s
                    dve.wait_ge(S["o_ready"], h * NT + l * 60 + 30)
                    V.tensor_copy(CS[:, NT:, :], KCn[:, :, bass.ds(h, 1), :].rearrange("p t a d -> p t (a d)")).then_inc(
                        S["lstack_k"], 1)
                    for g in range(3):
                        dve.wait_ge(S["lt_hi"], h * 3 + l * 18 + g + 1)
                        n = min(512, 11 * P - 512 * g)
                        V.tensor_tensor(LT[s][:, 1, 512 * g:512 * g + n], PS[0:QK, g % 2, 0:n],
                                        LT[s][:, 0, 512 * g:512 * g + n].bitcast(f32), ALU.subtract).then_inc(
                            S["lt_lo"], 1)
                    head_items(1, s, h * NT + l * 60 + 30, h * NT + l * 90 + 60,
                               lambda t, h=h: OC[:, t, bass.ds(h * VA_W, VA_W)])
                ch.end(start, 10, HEADS // 2)
            dve.wait_ge(S["o_stored"], (l + 1) * 60)
            split_lo(base + U_OUT)
            dve.wait_ge(S["conv_hi"], l + 1)
            V.tensor_tensor(MIX[:, 1, 3:5, :], CONV[:, :, :], MIX[:, 0, 3:5, :].bitcast(f32), ALU.subtract).then_inc(
                S["conv_lo"], 1)
            for t in range(NT + 1):
                if t < NT:
                    sums(HEADS, VA_W, (S["subln_done"], l * NT + t - 1) if t > 1 else (S["normed"], (l + 1) * 21))
                if t:
                    finish(QA[:, t - 1, :].rearrange("p (h e) -> p h e", e=VA_W)).then_inc(S["subln_done"], 1)
            for w in range(2 * NT):
                t, i = w // 2, w % 2
                dve.wait_ge(S["mix_hi"], l * 10 + w + 1)
                V.tensor_tensor(MIX[:, 1, 5 * i:5 * i + 3, t * P:(t + 1) * P],
                                PS[:, i, 0:3 * P].rearrange("p (c n) -> p c n", c=3),
                                MIX[:, 0, 5 * i:5 * i + 3, t * P:(t + 1) * P].bitcast(f32), ALU.subtract).then_inc(
                    S["mix_lo"], 1)
            split_lo(base + U_OUT + 1)

        def router_dve(V, dve, ch):
            dve.wait_ge(S["router_hi"], 1)
            dve.wait_ge(S["iota_ready"], 8)
            V.tensor_tensor(RWS[:, 1, :], RW[:, :], RWS[:, 0, :].bitcast(f32), ALU.subtract).then_inc(S["router_lo"], 1)
            dve.wait_ge(S["logits_ready"], 1)
            ch.then(V.tensor_copy(LG[:, :, :].rearrange("p t e -> p (t e)"), PS[:, 2, 0:NT * EXPERTS]))
            for t in range(NT):
                ch.then(V.max(TOP[:, t, :], LG[:, t, :]))
                ch.then(V.max_index(IDX[:, t, :], TOP[:, t, :], LG[:, t, :]))
            V.tensor_tensor(GT[:, :, 0:1], TOP[:, :, 1:2], TOP[:, :, 0:1], ALU.subtract).then_inc(S["top_ready"], 1)
            ch.then(V.tensor_copy(IDXF[:, :, :], IDX[:, :, :]))
            dve.wait_ge(S["top_exp"], 1)
            ch.then(V.tensor_scalar(GT[:, :, 2:3], GT[:, :, 1:2], 1.0, None, ALU.add))
            ch.then(V.reciprocal(GT[:, :, 2:3], GT[:, :, 2:3]))
            ch.then(V.tensor_tensor(GT[:, :, 3:4], GT[:, :, 2:3], GT[:, :, 1:2], ALU.mult))
            for t in range(NT):
                for i in range(2):
                    ins = V.tensor_scalar(CB[:, i, t, :], iota8[:, :], IDXF[:, t, i:i + 1], GT[:, t, 2 + i:3 + i],
                                          ALU.is_equal, ALU.mult)
            ch.then(ins)
            V.tensor_tensor(CB[:, 0, :, :], CB[:, 0, :, :], CB[:, 1, :, :], ALU.add).then_inc(S["comb_ready"], 1)
            flat = COMB[:, :, :].rearrange("p e n -> p (e n)")
            for g in range(10):
                dve.wait_ge(S["comb_turned"], g + 1)
                V.tensor_copy(flat[:, 512 * g:512 * g + 512], PS[:, g % 8, :]).then_inc(S["comb_stored"], 1)

        def ffn_dve(V, dve, ch, l, base, split_lo, gated_add):
            rounds, tail = layer_rounds(l)
            acts0 = 0 if l == 0 else 4 * DENSE_ROUNDS + TAIL_PAIRS

            def round_(r, e, u0, pairs, extra, ahead):
                d_pairs, d_u = extra
                n_units = 2 * pairs + 4
                for k in range(n_units):
                    if k < 2 * pairs:
                        j = k // 2
                        if k % 2:
                            dve.wait_ge(S["unit_used"], u0 + k + 1 + d_u)
                            dve.wait_ge(set_free[0], sets(u0 + k - 1, r, 0) + 1)
                            at_ = AT[:, :, :].rearrange("p c (h n) -> p (c h) n", h=2)
                            sg = SG[:, :, :].rearrange("p c (h n) -> p (c h) n", h=2)
                            V.tensor_tensor(at_, sg, PS[:, 4:8, 0:HALF], ALU.mult).then_inc(set_free[1], 1)
                            dve.wait_ge(set_free[1], sets(u0 + k, r, 1) + 1)
                            if l == 1:
                                w = COMB[:, e:e + 1, :] if r is None else COMB[:, bass.ds(e, 1), :]
                                V.tensor_tensor(AT[:, :, :], AT[:, :, :], w.broadcast_to([P, 2, TOK]),
                                                ALU.mult).then_inc(S["act_ready"], 1)
                            dve.wait_ge(S["act_hi"], acts0 + j + 1 + d_pairs)
                            V.tensor_tensor(ACTB[:, 1, 2 * j:2 * j + 2, :], AT[:, :, :],
                                            ACTB[:, 0, 2 * j:2 * j + 2, :].bitcast(f32), ALU.subtract).then_inc(
                                S["act_lo"], 1)
                    else:
                        dve.wait_ge(S["unit_used"], u0 + k + 1 + d_u)
                        gated_add(l, M_GATE2, u0 + k, 2 * (k - 2 * pairs))
                    if k + 2 < n_units or ahead:
                        split_lo(u0 + k + 2, r)

            u0 = base + U_FFN

            looped = rounds if tail else rounds - 1
            with dve.Fori(0, looped) as r:
                round_(r, r, u0, 4, (r * 4, r * ROUND), True)
            if tail:
                round_(None, rounds, u0 + rounds * ROUND, tail, (rounds * 4, 0), True)
            else:
                round_(None, looped, u0 + looped * ROUND, 4, (looped * 4, 0), False)

        @block.vector
        def _(dve):
            V = nc.vector
            ch = Chain(dve, S["dve"])

            def split_lo(u, r=None):
                n = N_ADA + u
                dve.wait_ge(S["split_hi"], u + 1 + (0 if r is None else r * ROUND))
                k = u - LAYER_U[1] if u >= LAYER_U[1] else u
                src = raw[n % RAW_SLOTS]
                if k == U_LATENT:
                    qw = 2 * HEADS * QK
                    V.tensor_tensor(WL[0:QR, 1, 0:qw], src[0:QR, 0:qw], WL[0:QR, 0, 0:qw].bitcast(f32), ALU.subtract)
                    V.tensor_tensor(WL[:, 1, qw:SMALL_W], src[:, qw:SMALL_W], WL[:, 0, qw:SMALL_W].bitcast(f32),
                                    ALU.subtract).then_inc(S["split_lo"], 1)
                    return
                w = unit_width(int(u >= LAYER_U[1]), k)
                V.tensor_tensor(split[u % 2][:, 1, 0:w], src[:, 0:w], split[u % 2][:, 0, 0:w].bitcast(f32),
                                ALU.subtract).then_inc(S["split_lo"], 1)

            for i in range(2 * NT):
                t, half = i // 2, i % 2
                dve.wait_ge(S["x_turned"], i + 1)
                V.tensor_copy(xT[:, 4 * half:4 * half + 4, t * P:(t + 1) * P],
                              PS[:, i % 2, :].rearrange("p (k n) -> p k n", k=4)).then_inc(S["x_stored"], 1)
            dve.wait_ge(S["vec_turned"], 1)
            V.tensor_copy(VEC[:, :, :], PS[:, 2, 0:2 * P].rearrange("p (l r) -> p l r", l=2)[:, :, 0:N_ROWS])
            V.tensor_copy(CSIL, PS[:, 2, 2 * P:2 * P + 2 * KC].rearrange("p (v k) -> p k v", v=2)).then_inc(
                S["vec_stored"], 1)
            dve.wait_ge(S["lam_in"], 16 * N_ROW_LOADS)
            ch.then(V.tensor_tensor(LB[:, :, 0:4:2, :], LB[:, :, 0:4:2, :], LB[:, :, 1:4:2, :], ALU.mult))
            V.tensor_reduce(LTMP[:, :].rearrange("p (l i) -> p l i", l=DEPTH), LB[:, :, 0:4:2, :], op=ALU.add,
                            axis=AX.X).then_inc(S["lam_summed"], 1)
            for l in range(DEPTH):
                l_init = 0.8 - 0.6 * math.exp(-0.3 * l)
                for col, n, factor in ((G_QA, DA, DA ** -0.5), (G_SUB, VA_W, 1.0 - l_init), (G_QC, QK, QK ** -0.5)):
                    V.tensor_scalar(GR[:, l, col:col + n], GR[:, l, col:col + n], float(factor), None, ALU.mult)
            dve.wait_ge(S["lam_exp"], 1)
            for l in range(DEPTH):
                l_init = 0.8 - 0.6 * math.exp(-0.3 * l)
                ch.then(V.tensor_tensor(LAM[:, l:l + 1], LTMP[:, 2 * l + 1:2 * l + 2], LTMP[:, 2 * l:2 * l + 1],
                                        ALU.subtract))
                ins = V.tensor_scalar(LAM[:, l:l + 1], LAM[:, l:l + 1], float(-l_init), None, ALU.add)
            ins.then_inc(S["setup_done"], 1)
            for l in range(DEPTH):
                dve.wait_ge(S["ada_used"], (l + 1) * ADA_UNITS)
                bias = VEC[:, l, R_BADA:R_BADA + 48].unsqueeze(2).broadcast_to([P, 48, 2])
                ch.then(V.tensor_tensor(MOD[:, l, :, :], PS[:, 3 + l, 0:96].rearrange("p (m v) -> p m v", v=2),
                                        bias, ALU.add))
                for norm, m in ((0, M_SCALE1), (1, M_SCALE2)):
                    ch.then(V.tensor_scalar(GS[:, l, norm, :, :], MOD[:, l, m:m + KC, :], 1.0, None, ALU.add))
                    g = VEC[:, l, (R_MIX, R_FFN)[norm]:(R_MIX, R_FFN)[norm] + KC].unsqueeze(2).broadcast_to([P, KC, 2])
                    ins = V.tensor_tensor(GS[:, l, norm, :, :], GS[:, l, norm, :, :], g, ALU.mult)
                    if l == 1 and norm == 1:
                        ins.then_inc(S["mod_ready"], 1)
                    else:
                        ch.then(ins)
            dve.wait_ge(S["mod_ready"], 1)
            split_lo(0)
            split_lo(1)
            nsq = [0]

            def refine(r, root_, mean, tmp):
                ch.then(V.reciprocal(r, root_))
                ch.then(V.tensor_tensor(tmp, r, r, ALU.mult))
                ch.then(V.scalar_tensor_tensor(out=tmp, in0=tmp, scalar=-0.5, in1=mean, op0=ALU.mult, op1=ALU.mult))
                ch.then(V.scalar_tensor_tensor(out=r, in0=tmp, scalar=1.5, in1=r, op0=ALU.add, op1=ALU.mult))

            nroot = [0, 0]

            def sums(g, d, former=None):
                if former is not None:
                    dve.wait_ge(*former)
                dve.wait_ge(S["nsq_ready"], nsq[0] + 1)
                nsq[0] += 1
                m = nroot[0] % 2
                s_ = SS[:, 12 * m:12 * m + g]
                ch.then(V.tensor_reduce(s_, sqn[:, 0:g * d].rearrange("p (g d) -> p g d", g=g), op=ALU.add, axis=AX.X))
                V.tensor_scalar(s_, s_, 1.0 / d, EPS, ALU.mult, ALU.add).then_inc(S["nsq_used"], 1)
                nroot[0] += 1

            def finish(x):
                g, d = x.shape[1], x.shape[2]
                m = nroot[1] % 2
                nroot[1] += 1
                dve.wait_ge(S["root_ready"], nroot[1])
                r = RT[:, 12 * m:12 * m + g]
                refine(r, r, SS[:, 12 * m:12 * m + g], NT_[:, 12 * m:12 * m + g])
                return V.tensor_tensor(x, x, r.unsqueeze(2).broadcast_to([P, g, d]), ALU.mult)

            def gated_add(l, gate, u, chunks):
                for c in range(2):
                    for hf in range(2):
                        for v, a, b in HALVES[hf]:
                            k = chunks + c
                            x = xT[:, k, hf * HALF + a:hf * HALF + b]
                            ins = V.scalar_tensor_tensor(out=x, in0=PS[:, 4 * (u % 2) + 2 * c + hf, a:b],
                                                         scalar=MOD[:, l, gate + k, v:v + 1], in1=x,
                                                         op0=ALU.mult, op1=ALU.add)
                ins.then_inc(set_free[u % 2], 1)

            for l in range(DEPTH):
                base = LAYER_U[l]
                for norm in range(2):
                    q = 2 * l + norm
                    dve.wait_ge(S["x_root"], q + 1)
                    mean = HM[:, 0, :]
                    ch.then(V.tensor_scalar(mean.rearrange("p (h n) -> p h n", h=2), PS[:, 0:2, 0:HALF],
                                            1.0 / D_MODEL, EPS, ALU.mult, ALU.add))
                    refine(rstdT[:, :], rstdT[:, :], mean, HM[:, 1, :])
                    for kc in range(KC + 1):
                        if kc < KC:
                            if kc >= 2:
                                dve.wait_ge(S["h_lo"], q * KC + kc - 1)
                            for v, a, b in V_RANGES:
                                ins = V.scalar_tensor_tensor(out=HM[:, kc % 2, a:b], in0=xT[:, kc, a:b],
                                                             scalar=GS[:, l, norm, kc, v:v + 1], in1=rstdT[:, a:b],
                                                             op0=ALU.mult, op1=ALU.mult)
                            ins.then_inc(S["hm_ready"], 1)
                        if kc:
                            k = kc - 1
                            dve.wait_ge(S["hm_ready"], q * KC + k + 1)
                            dve.wait_ge(S["h_hi"], q * KC + k + 1)
                            for v, a, b in V_RANGES:
                                sh = MOD[:, l, (M_SHIFT1, M_SHIFT2)[norm] + k, v:v + 1]
                                ins = V.scalar_tensor_tensor(out=H[:, 1, k, a:b], in0=HM[:, k % 2, a:b], scalar=sh,
                                                             in1=H[:, 0, k, a:b].bitcast(f32), op0=ALU.add,
                                                             op1=ALU.subtract)
                            ins.then_inc(S["h_lo"], 1)
                    if norm == 0:
                        split_lo(base + 2)
                        dve.wait_ge(S["unit_used"], base + 2)
                        dve.wait_ge(S["setA_free"], products_before(base, 0) + 1)
                        uu = UU[:, :, :].rearrange("p c (h n) -> p (c h) n", h=2)
                        V.tensor_tensor(uu, uu, PS[:, 4:8, 0:HALF], ALU.mult).then_inc(set_free[1], 1)
                        dve.wait_ge(set_free[1], products_before(base, 1) + 1)
                        split_lo(base + 3)
                        for c in range(2):
                            tap = [VEC[:, l, R_CW + 2 * w + c:R_CW + 2 * w + c + 1] for w in range(3)]
                            ch.then(V.tensor_scalar(CONV[:, c, :], UU[:, c, :], tap[1],
                                                    VEC[:, l, R_CB + c:R_CB + c + 1], ALU.mult, ALU.add))
                            for a, b, w in ((0, CTX, CTX), (CTX, TOK, GRID_W)):
                                src = UU[:, c, a:b].rearrange("p (r w) -> p r w", w=w)
                                dst = CONV[:, c, a:b].rearrange("p (r w) -> p r w", w=w)
                                ch.then(V.scalar_tensor_tensor(out=dst[:, :, 1:w], in0=src[:, :, 0:w - 1], scalar=tap[0],
                                                               in1=dst[:, :, 1:w], op0=ALU.mult, op1=ALU.add))
                                ch.then(V.scalar_tensor_tensor(out=dst[:, :, 0:w - 1], in0=src[:, :, 1:w],
                                                               scalar=tap[2], in1=dst[:, :, 0:w - 1], op0=ALU.mult,
                                                               op1=ALU.add))
                        dve.wait_ge(S["unit_used"], base + 3)
                        cv = CONV[:, :, :].rearrange("p c (h n) -> p (c h) n", h=2)
                        V.tensor_tensor(cv, cv, PS[:, 0:4, 0:HALF], ALU.mult).then_inc(set_free[0], 1)
                        split_lo(base + 4)
                        mixer_dve(V, dve, ch, l, base, split_lo, sums, finish, refine, nsq)
                        for j in range(4):
                            u = base + U_OUT + j
                            dve.wait_ge(S["unit_used"], u + 1)
                            gated_add(l, M_GATE1, u, 2 * j)
                            split_lo(u + 2)
                    else:
                        if l == 1:
                            router_dve(V, dve, ch)
                        ffn_dve(V, dve, ch, l, base, split_lo, gated_add)
            for t in range(NT):
                dve.wait_ge(S["y_turned"], 2 * t + 2)
                V.tensor_copy(xn[:, t, 512:1024], PS[:, 1, :]).then_inc(S["y_storedB"], 1)

        def mixer_pe(T, pe, l, base, turn, product):
            for j in range(3):
                if j == 2:
                    pe.wait_ge(set_free[0], products_before(base, 0) + 1)
                product(base + j, KC, H)
            for s in range(2):
                pe.wait_ge(set_free[s], products_before(base + U_QKV, s))
            for g in range(4):
                w_ = A_W if g < 3 else C_W
                for half in range(2):
                    u = base + U_QKV + 2 * g + half
                    pe.wait_ge(S["split_lo"], u + 1)
                    W = split[u % 2][:, :, 0:4 * w_].rearrange("p s (k n) -> p s k n", k=4)
                    for t in range(NT):
                        m = g * NT + t
                        if half == 0 and m >= 8:
                            pe.wait_ge(S["proj_free"], l * 20 + m - 7)
                        for k in range(4):
                            for w, a in ((0, 0), (0, 1), (1, 0)):
                                ins = T.matmul(PS[:, m % 8, 0:w_], H[:, a, 4 * half + k, t * P:(t + 1) * P], W[:, w, k, :],
                                               start=(half == 0 and k == 0 and w == 0 and a == 0),
                                               stop=(half == 1 and k == 3 and w == 1))
                        if half == 1 and t < NT - 1:
                            ins.then_inc(S["proj_ready"], 1)
                    ins.then_inc(S["unit_used"], 1)
            pe.wait_ge(S["proj_free"], (l + 1) * 20)

            def turn_c(t):
                if t >= 2:
                    pe.wait_ge(S["ct_lo"], l * KT_TILES + t - 1)
                if t < NT:
                    pe.wait_ge(S["nsq_used"], l * NORMS + 2 * NT + t + 1)
                    for j in range(2):
                        turn(PS[0:QR, t % 2, j * P:(j + 1) * P], CN[:, t, j * QR:(j + 1) * QR])
                    kv = CN[:, t, Q_RANK:Q_RANK + KV_RANK]
                else:
                    pe.wait_ge(S["cache_loaded"], (l + 1) * 64)
                    kv = CC[:, 0:KV_RANK]
                turn(PS[:, t % 2, 2 * P:3 * P], kv).then_inc(S["ct_turned"], 1)

            pe.wait_ge(S["split_lo"], base + U_LATENT + 1)
            qw = HEADS * QK
            passes = ((0, 0), (1, 0), (0, 1))
            turn_c(0)
            for t in range(KT_TILES):
                if t + 1 < KT_TILES:
                    turn_c(t + 1)
                pe.wait_ge(S["ct_lo"], l * KT_TILES + t + 1)
                if t:
                    pe.wait_ge(S["lat_k"], l * KT_TILES + t)
                    pe.wait_ge(S["v_lo"], l * KT_TILES + t)
                if t < NT:
                    for hf in range(2):
                        for j in range(2):
                            for a, w in passes:
                                T.matmul(PS[:, 2 + hf, 0:288], CQT[t % 2][:, a, j, :],
                                         WL[0:QR, w, j * qw + hf * 288:j * qw + (hf + 1) * 288],
                                         start=(j == 0 and a == 0 and w == 0), stop=(j == 1 and w == 1))
                for i in range(2):
                    for a, w in passes:
                        ins = T.matmul(PS[:, 4 + i, 0:A_W], CKT[t % 2][:, a, :],
                                       WL[:, w, 2 * qw + i * A_W:2 * qw + (i + 1) * A_W],
                                       start=(a == 0 and w == 0), stop=(w == 1))
                ins.then_inc(S["lat_ready"], 1)
            pe.wait_ge(S["lat_ready"], (l + 1) * KT_TILES)
            pe.sem_inc(S["unit_used"], 1)

            def head_items(comps, head, item0, score0, scores, V, v_at):
                def score(ti):
                    par = (head + ti) % 2
                    t = TILE_ORDER[ti]
                    for c in range(comps):
                        slot = c if comps == 2 else par
                        if comps * ti + c >= 2:
                            pe.wait_ge(S["exp_ready"], score0 + comps * ti + c - 1)
                        for hf in range(2 if t else 1):
                            ins = scores(c, t, hf, PS[:, 2 + 2 * slot + hf, 0:HALF if t else P])
                        ins.then_inc(S["scored"], 1)

                score(0)
                for ti in range(NT):
                    if ti + 1 < NT:
                        score(ti + 1)
                    par, t = (head + ti) % 2, TILE_ORDER[ti]
                    if comps == 2:
                        pe.wait_ge(S["w_ready"], item0 - l * 30 + ti + 1)
                    else:
                        pe.wait_ge(S["exp_ready"], score0 + ti + 1)
                    n = 5 if t else 1
                    for j in range(n):
                        ins = turn(PSF[:, 3072 + j * P:3072 + (j + 1) * P], E[:, par, 0, j * P:(j + 1) * P])
                    ins.then_inc(S["pt_ready"], 1)
                    pe.wait_ge(S["pt_lo"], item0 + ti + 1)
                    if ti >= 2:
                        pe.wait_ge(S["o_stored"], item0 + ti - 1)
                    for j in range(n):
                        tile_ = 1 + j if t else 0
                        for pt, s_ in ((PTH, 0), (PTH, 1), (PTL, 0)):
                            ins = T.matmul(PS[:, par, 0:VA_W], pt[:, j * P:(j + 1) * P],
                                           V[:, tile_, s_, v_at], start=(j == 0 and s_ == 0 and pt is PTH),
                                           stop=(j == n - 1 and pt is PTL))
                    ins.then_inc(S["o_ready"], 1)
                pe.wait_ge(S["o_stored"], item0 + NT)

            pe.wait_ge(S["v_split"], (l + 1) * 6)
            with pe.Fori(0, HEADS // 2) as i:
                for s in range(2):
                    h = i * 2 + s
                    pe.wait_ge(S["stack_lo"], h + l * HEADS + 1)
                    for g in range(6):
                        if g >= 2:
                            pe.wait_ge(S[("turnA", "turnB")[g % 2]], h * 3 + l * 18 + g // 2)
                        stack, tiles, first = (QS[s], NT, 4 * g) if g < 3 else (KS, KT_TILES, 4 * (g - 3))
                        for j in range(first, min(first + 4, 2 * tiles)):
                            ins = turn(PS[:, g % 2, (j - first) * P:(j - first + 1) * P],
                                       stack[:, j % tiles, j // tiles, :, :].rearrange("p a d -> p (a d)"))
                        ins.then_inc(S["turned"], 1)
                    pe.wait_ge(S["turnA"], h * 3 + l * 18 + 3)
                    pe.wait_ge(S["turnB"], h * 3 + l * 18 + 3)

                    def scores(c, t, hf, out, s=s):
                        first = P + hf * HALF if t else 0
                        return T.matmul(out, QT[s][:, c, t * P:(t + 1) * P],
                                        KT[s][:, c, first:first + (HALF if t else P)], start=True, stop=True)

                    head_items(2, s, h * NT + l * 60, h * 10 + l * 90, scores, VA, bass.ds(h * VA_W, VA_W))
            pe.wait_ge(S["v_lo"], (l + 1) * KT_TILES)
            with pe.Fori(0, HEADS // 2) as i:
                for s in range(2):
                    h = i * 2 + s
                    pe.wait_ge(S["lstack_q"], h + l * HEADS + 1)
                    pe.wait_ge(S["lstack_k"], h + l * HEADS + 1)
                    for g in range(3):
                        if g == 2:
                            pe.wait_ge(S["lt_lo"], h * 3 + l * 18 + 1)
                        for j in range(4 * g, min(4 * g + 4, NT + KT_TILES)):
                            ins = turn(PS[0:QK, g % 2, (j - 4 * g) * P:(j - 4 * g + 1) * P], CS[:, j, :])
                        ins.then_inc(S["lturned"], 1)
                    pe.wait_ge(S["lt_lo"], h * 3 + l * 18 + 3)

                    def scores(c, t, hf, out, s=s):
                        first = TOK + (P + hf * HALF if t else 0)
                        n = HALF if t else P
                        for a, b in passes:
                            ins = T.matmul(out, LT[s][:, a, t * P:(t + 1) * P], LT[s][:, b, first:first + n],
                                           start=(a == 0 and b == 0), stop=(b == 1))
                        return ins

                    head_items(1, s, h * NT + l * 60 + 30, h * NT + l * 90 + 60, scores, VC,
                               bass.ds(h * VA_W, VA_W))
            pe.wait_ge(S["o_stored"], (l + 1) * 60)
            for w in range(2 * NT):
                t, i = w // 2, w % 2
                if i == 0:
                    pe.wait_ge(S["subln_gained"], l * NT + t + 1)
                if w >= 2:
                    pe.wait_ge(S["mix_lo"], l * 10 + w - 1)
                for c in range(3):
                    src = QA[:, t, c * P:(c + 1) * P] if i == 0 else OC[:, t, c * P:(c + 1) * P]
                    ins = turn(PS[:, i, c * P:(c + 1) * P], src)
                ins.then_inc(S["mix_turned"], 1)
            pe.wait_ge(S["mix_lo"], (l + 1) * 10)
            pe.wait_ge(S["conv_lo"], l + 1)
            for j in range(4):
                u = base + U_OUT + j
                if j >= 2:
                    pe.wait_ge(set_free[u % 2], products_before(u, u % 2))
                product(u, KC, MIX)

        def ffn_pe(T, pe, l, base, turn, product):
            if l == 1:
                pe.wait_ge(S["router_lo"], 1)
                for t in range(NT):
                    for k in range(KC):
                        for a, w in ((0, 0), (1, 0), (0, 1)):
                            ins = T.matmul(PS[:, 2, t * EXPERTS:(t + 1) * EXPERTS], H[:, a, k, t * P:(t + 1) * P],
                                           RWS[:, w, k * EXPERTS:(k + 1) * EXPERTS], start=(k == 0 and a == 0 and w == 0),
                                           stop=(k == KC - 1 and w == 1))
                ins.then_inc(S["logits_ready"], 1)
                pe.wait_ge(S["comb_ready"], 1)
                for g in range(10):
                    if g >= 8:
                        pe.wait_ge(S["comb_stored"], g - 7)
                    for j in range(4):
                        e, t = (4 * g + j) // NT, (4 * g + j) % NT
                        ins = T.matmul(PS[:, g % 8, j * P:(j + 1) * P], CB[:, 0, t, e:e + 1].broadcast_to([P, P]),
                                       ident[:, :], start=True, stop=True)
                    ins.then_inc(S["comb_turned"], 1)
                pe.wait_ge(S["comb_stored"], 10)
            rounds, tail = layer_rounds(l)
            acts0 = 0 if l == 0 else 4 * DENSE_ROUNDS + TAIL_PAIRS

            def round_(r, u0, pairs, kd, d_pairs):
                for k in range(2 * pairs + 4):
                    u = u0 + k
                    free = products_before(u, u % 2)
                    pe.wait_ge(set_free[u % 2], free if r is None else r * (ROUND // 2) + free)
                    if k == 2 * pairs:
                        pe.wait_ge(S["act_lo"], acts0 + pairs + d_pairs)
                    product(u, KC if k < 2 * pairs else kd, H if k < 2 * pairs else ACTB, r)

            u0 = base + U_FFN
            with pe.Fori(0, rounds) as r:
                round_(r, u0, 4, KC, r * 4)
            if tail:
                round_(None, u0 + rounds * ROUND, tail, TAIL_FF // P, rounds * 4)

        @block.tensor
        def _(pe):
            T = nc.tensor

            def turn(out, in_):
                return T.transpose(out, in_, ident[0:in_.shape[0], 0:in_.shape[0]])

            def product(u, k_chunks, A, r=None, cols=256):
                pe.wait_ge(S["split_lo"], u + 1 + (0 if r is None else r * ROUND))
                W = split[u % 2][:, :, 0:k_chunks * cols].rearrange("p s (k n) -> p s k n", k=k_chunks)
                for c in range(2):
                    for k in range(k_chunks):
                        for w, a in ((0, 0), (0, 1), (1, 0)):
                            for hf in range(2):
                                ins = T.matmul(PS[:, 4 * (u % 2) + 2 * c + hf, 0:HALF],
                                               W[:, w, k, c * P:(c + 1) * P], A[:, a, k, hf * HALF:(hf + 1) * HALF],
                                               start=(k == 0 and w == 0 and a == 0),
                                               stop=(k == k_chunks - 1 and w == 1))
                ins.then_inc(S["unit_used"], 1)

            pe.wait_ge(S["const_ready"], 3)
            pe.wait_ge(S["x_loaded"], 16 * NT)
            for i in range(2 * NT):
                if i >= 2:
                    pe.wait_ge(S["x_stored"], i - 1)
                for k in range(4):
                    kc = 4 * (i % 2) + k
                    ins = turn(PS[:, i % 2, k * P:(k + 1) * P], xn[:, i // 2, kc * P:(kc + 1) * P])
                ins.then_inc(S["x_turned"], 1)
            pe.wait_ge(S["small_loaded"], 16 * (2 + 6 * DEPTH))
            for l in range(DEPTH):
                turn(PS[:, 2, l * P:(l + 1) * P], VR[:, l, :])
            turn(PS[:, 2, 2 * P:2 * P + 2 * KC], CR[:, :]).then_inc(S["vec_turned"], 1)
            pe.wait_ge(S["silu_c"], 1)
            per = ADA_COLS // P
            for l in range(DEPTH):
                with pe.Fori(0, ADA_UNITS // RAW_SLOTS) as i:
                    for s in range(RAW_SLOTS):
                        n = l * ADA_UNITS + s
                        pe.wait_ge(raw_ready[s], 16 * (l * ADA_UNITS // RAW_SLOTS + 1) + i * 16)
                        W = raw[s][:, :].rearrange("p (k n) -> p k n", k=KC)
                        for c in range(per):
                            for k in range(KC):
                                ins = T.matmul(PS[:, 3 + l, bass.ds(2 * (s * per + c) + i * (2 * per * RAW_SLOTS), 2)],
                                               W[:, k, c * P:(c + 1) * P], CSIL[:, k, :], start=(k == 0),
                                               stop=(k == KC - 1))
                        ins.then_inc(S["ada_used"], 1)

            for l in range(DEPTH):
                base = LAYER_U[l]
                for norm in range(2):
                    q = 2 * l + norm
                    for kc in range(KC):
                        pe.wait_ge(S["sq_ready"], q * KC + kc + 1)
                        for hf in range(2):
                            ins = T.matmul(PS[:, hf, 0:HALF], ones[:, :], HM[:, kc % 2, hf * HALF:(hf + 1) * HALF],
                                           start=(kc == 0), stop=(kc == KC - 1))
                        ins.then_inc(S["sq_used"], 1)
                    pe.wait_ge(S["h_lo"], (q + 1) * KC)
                    if norm == 0:
                        mixer_pe(T, pe, l, base, turn, product)
                    else:
                        ffn_pe(T, pe, l, base, turn, product)
            for i in range(2 * NT):
                t = i // 2
                if i == 0:
                    for s in range(2):
                        pe.wait_ge(set_free[s], products_before(LAYER_U[1] + U_FFN + FFN_UNITS[1], s))
                elif i >= 2:
                    pe.wait_ge(S[("y_storedA", "y_storedB")[i % 2]], t)
                for k in range(4):
                    ins = turn(PS[:, i % 2, k * P:(k + 1) * P], xT[:, 4 * (i % 2) + k, t * P:(t + 1) * P])
                ins.then_inc(S["y_turned"], 1)

_INPUTS = ["x_prompt", "x_sample", "cache_diff_k", "cache_diff_v", "cache_mla_ckv", "cache_mla_krope", "c", "c_ctx",
           "w_ada", "b_ada", "norm_mix", "norm_ffn", "w_in", "qnorm_a", "knorm_a", "lambda_q1", "lambda_k1",
           "lambda_q2", "lambda_k2", "subln_a", "conv_w", "conv_b", "norm_qa", "w_qb", "norm_kva", "w_kb", "w_vb",
           "qnorm_c", "knorm_c", "w_out", "ffn_w_gate", "ffn_w_up", "ffn_w_down", "router_w", "moe_w_gate",
           "moe_w_up", "moe_w_down"]
_OUTPUTS = [("y_prompt", (1, CTX, D_MODEL)), ("y_sample", (1, LAT, D_MODEL)),
            ("new_diff_k", (1, DEPTH, CTX, HEADS, 2, DA)), ("new_diff_v", (1, DEPTH, CTX, HEADS, VA_W)),
            ("new_mla_ckv", (1, DEPTH, CTX, KV_RANK)), ("new_mla_krope", (1, DEPTH, CTX, ROPE_W))]


def rope_table():
    n = ROPE_W // 4
    inv = np.power(np.float32(10000.0), -np.arange(n, dtype=np.float32) / np.float32(n)).astype(np.float32)
    t = np.arange(LAT)
    out = np.zeros((LAT, 2, 2, 2, n), np.float32)
    for half, pos in enumerate((t // GRID_W, t % GRID_W)):
        ang = pos.astype(np.float32)[:, None] * inv[None, :]
        out[:, 0, half, 0] = out[:, 0, half, 1] = np.cos(ang)
        out[:, 1, half, 0], out[:, 1, half, 1] = -np.sin(ang), np.sin(ang)
    return np.ascontiguousarray(out.reshape(4, P, 64).transpose(1, 0, 2).reshape(P, 256))


def kernel(**inputs):
    import concourse.bacc as bacc
    from concourse.bass_utils import run_bass_kernel_spmd

    nc = bacc.Bacc("TRN2", target_bir_lowering=False, num_devices=1)
    arrays, I, O = {}, {}, {}
    for name in _INPUTS:
        a = np.ascontiguousarray(inputs[name])
        arrays["in_" + name] = a
        I[name] = nc.dram_tensor("in_" + name, a.shape, mybir.dt.from_np(a.dtype), kind="ExternalInput").ap()
    table = rope_table()
    arrays["in_rope"] = table
    I["rope"] = nc.dram_tensor("in_rope", table.shape, mybir.dt.float32, kind="ExternalInput").ap()
    for name, shape in _OUTPUTS:
        O[name] = nc.dram_tensor("out_" + name, shape, mybir.dt.float32, kind="ExternalOutput").ap()
    trunk_program(nc, I, O)
    result = run_bass_kernel_spmd(nc, [arrays], core_ids=[0]).results[0]
    return tuple(result["out_" + name] for name, _ in _OUTPUTS)
```

```python
import math
from contextlib import ExitStack

import numpy as np

import concourse.bass as bass
from concourse import mybir

P = 128
D_MODEL, KC = 1024, 8
CTX, LAT = 128, 512
TOK = CTX + LAT
NT = TOK // P
HALF = TOK // 2
DEPTH = 2
HEADS = 6
DA, VA_W = 32, 64
NOPE, ROPE_W = 64, 32
QK = NOPE + ROPE_W
Q_RANK, KV_RANK = 192, 128
QR = Q_RANK // 2
A_W = HEADS * 2 * DA
W_B = 256
C_W = Q_RANK + KV_RANK + ROPE_W
IN_COLS = 3 * A_W + 3 * W_B + C_W
B_COL = 3 * A_W
C_COL = B_COL + 3 * W_B
D_FF, EXPERTS, MOE_FF = 2816, 8, 1024
GRID_W = 64
EPS = 1e-6
KEYS = 5 * P
KT_TILES = 6

RAW_SLOTS = 4
UNIT = 2048
ADA_COLS = UNIT // KC
ADA_UNITS = 6 * D_MODEL // ADA_COLS
N_ADA = DEPTH * ADA_UNITS
U_CONV, U_QKV, U_LATENT, U_OUT, U_FFN = 0, 3, 11, 12, 16
ROUND = 12
DENSE_ROUNDS = 2
TAIL_FF = D_FF - DENSE_ROUNDS * MOE_FF
TAIL_PAIRS = TAIL_FF // 256
FFN_UNITS = [DENSE_ROUNDS * ROUND + 2 * TAIL_PAIRS + 4, EXPERTS * ROUND]
LAYER_U = [0, U_FFN + FFN_UNITS[0]]
SMALL_W = HEADS * QK * 2 + 2 * A_W

R_MIX, R_FFN, R_BADA, R_CW, R_CB, R_QA, N_ROWS = 0, 8, 16, 64, 70, 72, 74
G_QA, G_KA, G_SUB, G_KV, G_QC, G_KC, G_W = 0, 32, 64, 128, 256, 352, 448
M_SHIFT1, M_SCALE1, M_GATE1, M_SHIFT2, M_SCALE2, M_GATE2 = 0, 8, 16, 24, 32, 40

NORMS = 31
ITEMS = 2 * HEADS * NT
A_ITEMS = HEADS * NT
SCORES = 3 * HEADS * NT
TURNS = 9 * HEADS
TILE_ORDER = [1, 2, 3, 4, 0]


def products_before(u, parity=None):
    n = 0
    for v in range(u):
        r = v - LAYER_U[1] if v >= LAYER_U[1] else v
        if (r < U_QKV or r >= U_OUT) and (parity is None or v % 2 == parity):
            n += 1
    return n


def score_of(j, c):
    return 2 * j + c if j < A_ITEMS else A_ITEMS + j


def comps_of(j):
    return 2 if j < A_ITEMS else 1


def groups_of(h):
    return 6 if h < HEADS else 3


def groups_before(h):
    return 6 * min(h, HEADS) + 3 * max(h - HEADS, 0)


def groups_at(k, place):
    if k < 0 or k % NT > 2 or k // NT + 1 >= 2 * HEADS:
        return None
    h = k // NT + 1
    if groups_of(h) == 6:
        return h, 2 * (k % NT) + place
    return (h, k % NT) if place == 0 else None


class Chain:

    def __init__(self, engine, sem):
        self.engine, self.sem, self.n, self.offset = engine, sem, 0, 0

    def then(self, instruction):
        self.n += 1
        instruction.then_inc(self.sem, 1)
        self.engine.wait_ge(self.sem, self.n + self.offset)

    def begin(self, offset):
        self.start, self.offset = self.n, offset
        return self.n

    def end(self, start, per, trips):
        assert self.n - start == per, (self.n - start, per)
        self.n, self.offset = start + per * trips, 0


def trunk_program(nc, I, O):
    f32, f32r = mybir.dt.float32, mybir.dt.float32r
    ALU, ACT, AX = mybir.AluOpType, mybir.ActivationFunctionType, mybir.AxisListType
    nc_base = (nc.sbuf_base + 31) // 32 * 32

    ctx = ExitStack()
    with ctx:
        def at(name, shape, offset, dt=f32):
            return nc.alloc_sbuf_tensor_at(name, shape, dt, offset=nc_base + offset)

        OFF_X, OFF_RAW, OFF_SPLIT, OFF_H = 0, 20480, 53248, 86016
        OFF_R = OFF_H + 40960
        OFF_QC, OFF_E, OFF_OB = OFF_R + 35328, OFF_R + 46848, OFF_R + 62208
        OFF_U = OFF_R + 67328
        OFF_CN = OFF_U + 3200
        OFF_S = OFF_R + 77568
        xT = at("xT", [P, KC, TOK], OFF_X)
        raw = [at(f"raw{i}", [P, UNIT], OFF_RAW + i * UNIT * 4) for i in range(RAW_SLOTS)]
        split = [at(f"split{i}", [P, 2, UNIT], OFF_SPLIT + i * UNIT * 8, f32r) for i in range(2)]
        H = at("H", [P, 2, KC, TOK], OFF_H, f32r)
        MIX = at("MIX", [P, 2, KC, TOK], OFF_H, f32r)
        VC = at("VC", [P, KT_TILES, A_W], OFF_H)
        PT = [at(f"PT{i}", [P, KEYS], OFF_H + 9216 + 2560 * i) for i in range(2)]
        KCn = at("KCn", [P, KT_TILES, HEADS, QK], OFF_H + 18432)
        OFF_CT = OFF_H + 32256
        CQT = [at(f"CQT{i}", [QR, 2, 2, P], OFF_CT + 3072 * i, f32r) for i in range(2)]
        CKT = [at(f"CKT{i}", [P, 2, P], OFF_CT + 3072 * i + 2048, f32r) for i in range(2)]
        rope_c = at("rope_c", [P, HEADS, ROPE_W], OFF_CT + 6144)
        QA = at("QA", [P, NT, A_W], OFF_R)
        KA = at("KA", [P, KT_TILES, A_W], OFF_R + 7680)
        VA = at("VA", [P, KT_TILES, A_W], OFF_R + 16896)
        rope_a = at("rope_a", [P, A_W], OFF_R + 26112)
        QC = at("QC", [P, NT, HEADS, QK], OFF_QC)
        OC = at("OC", [P, NT, HEADS * QK], OFF_QC)[:, :, 0:A_W]
        WL = at("WL", [P, 2, SMALL_W], OFF_E, f32r)
        E = at("E", [P, 3, 2, KEYS], OFF_E)
        CONV = at("CONV", [P, 2, TOK], OFF_OB)
        UU = at("UU", [P, 2, TOK], OFF_U)
        rstdT = at("rstdT", [P, TOK], OFF_U)
        sqn = at("sqn", [P, HEADS * QK], OFF_U)
        CC = at("CC", [P, KV_RANK + ROPE_W], OFF_U + 2560)
        HM = at("HM", [P, 2, TOK], OFF_U + 5120)
        CN = at("CN", [P, NT, C_W], OFF_CN)
        KS = at("KS", [P, KT_TILES, 2, 4, DA], OFF_U)
        QT = [at(f"QT{s}", [P, 2, TOK], OFF_SPLIT + s * 16384, f32r) for s in range(2)]
        KT = [at(f"KT{s}", [P, 2, KT_TILES * P], OFF_SPLIT + s * 16384 + 5120, f32r) for s in range(2)]
        QS = [at(f"QS{s}", [P, NT, 2, 4, DA], OFF_SPLIT + s * 16384 + 11264) for s in range(2)]
        LT = [at(f"LT{s}", [QK, (NT + KT_TILES) * P], OFF_SPLIT + s * 16384) for s in range(2)]
        ACTB = at("ACTB", [P, 2, KC, TOK], OFF_R, f32r)
        COMB = at("COMB", [P, EXPERTS, TOK], OFF_R + 40960)
        SG = at("SG", [P, 2, TOK], OFF_R + 61440)
        AT = at("AT", [P, 2, TOK], OFF_R + 66560)
        RW = at("RW", [P, KC * EXPERTS], OFF_R + 71680)
        RWS = at("RWS", [P, 2, KC * EXPERTS], OFF_R + 71936, f32r)
        LG = at("LG", [P, NT, EXPERTS], OFF_R + 72448)
        TOP = at("TOP", [P, NT, 8], OFF_R + 72608)
        IDX = at("IDX", [P, NT, 8], OFF_R + 72768, mybir.dt.uint32)
        IDXF = at("IDXF", [P, NT, 8], OFF_R + 72928)
        GT = at("GT", [P, NT, 4], OFF_R + 73088)
        CB = at("CB", [P, 2, NT, EXPERTS], OFF_R + 73184)
        xn = at("xn", [P, NT, D_MODEL], OFF_H)
        VR = at("VR", [P, DEPTH, P], OFF_R)
        CR = at("CR", [2 * KC, P], OFF_R + 1024)
        LB = at("LB", [P, DEPTH, 4, DA], OFF_R + 1536)
        s_off = [OFF_S]

        def small(name, width, dt=f32):
            t = at(name, [P, width], s_off[0], dt)
            s_off[0] += -(-width * 4 // 32) * 32
            return t

        ident, ones = small("ident", P), small("ones", P)
        MOD = small("MOD", DEPTH * 48 * 2)[:, :].rearrange("p (l m v) -> p l m v", l=DEPTH, v=2)
        GS = small("GS", DEPTH * 2 * KC * 2)[:, :].rearrange("p (l n k v) -> p l n k v", l=DEPTH, n=2, v=2)
        VEC = small("VEC", DEPTH * N_ROWS)[:, :].rearrange("p (l r) -> p l r", l=DEPTH)
        ROPE = small("ROPE", 4 * 64)[:, :].rearrange("p (t s d) -> p t s d", t=4, s=2)
        GR = small("GR", DEPTH * G_W)[:, :].rearrange("p (l g) -> p l g", l=DEPTH)
        CSIL = small("CSIL", 2 * KC)[:, :].rearrange("p (v k) -> p k v", v=2)
        LAM, LTMP = small("LAM", DEPTH), small("LTMP", DEPTH * 2)
        SS, SSC = small("SS", 24), small("SSC", 4)
        RT, RTC = small("RT", 24), small("RTC", 4)
        NT_ = small("NT_", 24)
        NM, SM, RC, CNEG = small("NM", 6), small("SM", 6), small("RC", 6), small("CNEG", 3)
        iota8, eps = small("iota8", 8), small("eps", 1)
        assert nc_base + s_off[0] <= nc.sbuf_usable_end, (nc_base + s_off[0], nc.sbuf_usable_end)

        PS = ctx.enter_context(nc.psum_tensor("PS", [P, 8, 512], f32))
        PSF = PS[:, :, :].rearrange("p b n -> p (b n)")

        names = ("const_ready small_loaded x_loaded x_turned x_stored vec_turned vec_stored silu_c "
                 "ada_used ada_out mod_ready lam_in lam_summed lam_exp setup_done "
                 "split_hi split_lo unit_used sq_ready sq_used hm_ready h_hi h_lo "
                 "setA_free setB_free proj_ready proj_free "
                 "nsq_ready nsq_used root_ready x_root eps_ready normed roped cache_loaded stores "
                 "ct_turned ct_hi ct_lo lat_ready lat_q lat_k subln_gained "
                 "stacked turned turn_out scored max_ready exp_ready w_ready pt_ready pt_out o_ready o_stored "
                 "subln_done mix_turned mix_hi mix_lo conv_hi conv_lo act_ready act_hi act_lo "
                 "router_loaded router_hi router_lo logits_ready top_ready top_exp comb_ready comb_turned comb_stored "
                 "y_turned y_storedA y_storedB dve act pool iota_ready").split()
        S = {n: ctx.enter_context(nc.semaphore(n)) for n in names}
        raw_ready = [ctx.enter_context(nc.semaphore(f"raw_ready{i}")) for i in range(RAW_SLOTS)]
        set_free = [S["setA_free"], S["setB_free"]]
        block = ctx.enter_context(nc.Block())

        def raw_count(n):
            extra = sum(32 for l in range(DEPTH)
                        if N_ADA + LAYER_U[l] + U_LATENT <= n
                        and (N_ADA + LAYER_U[l] + U_LATENT - n) % RAW_SLOTS == 0)
            return 16 * (n // RAW_SLOTS + 1) + extra

        def layer_rounds(l):
            return (DENSE_ROUNDS, TAIL_PAIRS) if l == 0 else (EXPERTS, 0)

        V_RANGES = [(0, 0, CTX), (1, CTX, TOK)]

        HALVES = [[(0, 0, CTX), (1, CTX, HALF)], [(1, 0, HALF)]]

        root_at = [l * NORMS + m + 1 for l in range(DEPTH) for m in range(NORMS) if not 2 * NT <= m < 3 * NT]

        def sets(u, r, parity):
            n = products_before(u, parity)
            return n if r is None else r * (ROUND // 2) + n

        @block.sync
        def _(sp):
            def free_slot(n, value=None):
                if n < RAW_SLOTS:
                    return
                m = n - RAW_SLOTS
                if m < N_ADA:
                    sp.wait_ge(S["ada_used"], m + 1)
                else:
                    sp.wait_ge(S["split_lo"], m - N_ADA + 1 + (0 if value is None else value))

            def load(n, source, kc, cols, value=None):
                free_slot(n, value)
                dst = raw[n % RAW_SLOTS][:, 0:kc * cols].rearrange("p (k c) -> p k c", k=kc)
                sp.dma_start(dst, source).then_inc(raw_ready[n % RAW_SLOTS], 16)

            def chunks(w):
                return w.rearrange("(k p) n -> p k n", p=P)

            for t in range(NT):
                src = I["x_prompt"][0] if t == 0 else I["x_sample"][0, (t - 1) * P:t * P]
                sp.dma_start(xn[:, t, :], src).then_inc(S["x_loaded"], 16)
            sp.wait_ge(S["const_ready"], 3)
            for v, name in enumerate(("c_ctx", "c")):
                src = (I[name] if v == 0 else I[name][0]).rearrange("(k p) -> k p", p=P)
                sp.dma_start(CR[v * KC:(v + 1) * KC, :], src).then_inc(S["small_loaded"], 16)
            for l in range(DEPTH):
                for row, name, n in ((R_MIX, "norm_mix", 8), (R_FFN, "norm_ffn", 8), (R_BADA, "b_ada", 48),
                                     (R_CB, "conv_b", 2)):
                    sp.dma_start(VR[row:row + n, l, :], I[name][l].rearrange("(k p) -> k p", p=P)).then_inc(
                        S["small_loaded"], 16)
                sp.dma_start(VR[R_CW:R_CW + 6, l, :], I["conv_w"][l].rearrange("w (k p) -> (w k) p", p=P)).then_inc(
                    S["small_loaded"], 16)
                sp.dma_start(VR[R_QA:R_QA + 2, l, 0:QR], I["norm_qa"][l].rearrange("(k p) -> k p", p=QR)).then_inc(
                    S["small_loaded"], 16)
            N_COLUMN_LOADS = 2 + 6 * DEPTH
            for l in range(DEPTH):
                w = chunks(I["w_ada"][l])
                for j in range(ADA_UNITS):
                    n = l * ADA_UNITS + j
                    load(n, w[:, :, j * ADA_COLS:(j + 1) * ADA_COLS], KC, ADA_COLS)
            for l in range(DEPTH):
                base = N_ADA + LAYER_U[l]
                w = chunks(I["w_in"][l])
                for j, col in enumerate((B_COL + W_B, B_COL + 2 * W_B, B_COL)):
                    load(base + U_CONV + j, w[:, :, col:col + W_B], KC, W_B)
                for g in range(4):
                    col, width = (g * A_W, A_W) if g < 3 else (C_COL, C_W)
                    for half in range(2):
                        load(base + U_QKV + 2 * g + half, w[:, 4 * half:4 * half + 4, col:col + width], 4, width)
                n = base + U_LATENT
                free_slot(n)
                dst = raw[n % RAW_SLOTS]
                qw = HEADS * QK
                sp.dma_start(dst[0:QR, 0:2 * qw].rearrange("p (k c) -> p k c", k=2),
                             I["w_qb"][l].rearrange("(k p) n -> p k n", p=QR)).then_inc(raw_ready[n % RAW_SLOTS], 16)
                sp.dma_start(dst[:, 2 * qw:2 * qw + A_W], I["w_kb"][l]).then_inc(raw_ready[n % RAW_SLOTS], 16)
                sp.dma_start(dst[:, 2 * qw + A_W:SMALL_W], I["w_vb"][l]).then_inc(raw_ready[n % RAW_SLOTS], 16)
                w = chunks(I["w_out"][l])
                for j in range(4):
                    load(base + U_OUT + j, w[:, :, j * 256:(j + 1) * 256], KC, 256)

                n0 = base + U_FFN
                rounds, tail = layer_rounds(l)
                with sp.Fori(0, rounds) as r:
                    if l == 0:
                        wg = I["ffn_w_gate"][0].rearrange("(k p) (r n) -> p k r n", p=P, n=256)
                        wu = I["ffn_w_up"][0].rearrange("(k p) (r n) -> p k r n", p=P, n=256)
                        wd = I["ffn_w_down"][0].rearrange("(r p) n -> p r n", p=P)
                    for j in range(4):
                        n = n0 + 2 * j
                        if l == 0:
                            load(n, wg[:, :, bass.ds(r * 4 + j, 1), :], KC, 256, r * ROUND)
                            load(n + 1, wu[:, :, bass.ds(r * 4 + j, 1), :], KC, 256, r * ROUND)
                        else:
                            for i, name in enumerate(("moe_w_gate", "moe_w_up")):
                                w_ = I[name][0].rearrange("e (k p) n -> p (e k) n", p=P)
                                load(n + i, w_[:, bass.ds(r * KC, KC), j * 256:(j + 1) * 256], KC, 256, r * ROUND)
                    for j in range(4):
                        if l == 0:
                            src = wd[:, bass.ds(r * KC, KC), j * 256:(j + 1) * 256]
                        else:
                            w_ = I["moe_w_down"][0].rearrange("e (k p) n -> p (e k) n", p=P)
                            src = w_[:, bass.ds(r * KC, KC), j * 256:(j + 1) * 256]
                        load(n0 + 8 + j, src, KC, 256, r * ROUND)
                if tail:
                    n = n0 + rounds * ROUND
                    first = rounds * MOE_FF
                    for j in range(tail):
                        for i, name in enumerate(("ffn_w_gate", "ffn_w_up")):
                            c = first + j * 256
                            load(n + 2 * j + i, chunks(I[name][0])[:, :, c:c + 256], KC, 256)
                    for j in range(4):
                        src = I["ffn_w_down"][0][first:].rearrange("(k p) n -> p k n", p=P)
                        load(n + 2 * tail + j, src[:, :, j * 256:(j + 1) * 256], TAIL_FF // P, 256)

        @block.gpsimd
        def _(pool):
            ch = Chain(pool, S["pool"])
            nc.gpsimd.memset(ones[:, :], 1.0).then_inc(S["const_ready"], 1)
            nc.gpsimd.memset(VR[:, :, :], 0.0).then_inc(S["const_ready"], 1)
            ch.then(nc.gpsimd.memset(ident[:, :], 0.0))
            nc.gpsimd.affine_select(out=ident[:, :], in_=ident[:, :], compare_op=ALU.not_equal, fill=1.0, base=0,
                                    pattern=[[-1, P]], channel_multiplier=1).then_inc(S["const_ready"], 1)
            nc.gpsimd.memset(eps[:, :], EPS).then_inc(S["eps_ready"], 1)
            for e in range(8):
                nc.gpsimd.memset(iota8[:, e:e + 1], float(e)).then_inc(S["iota_ready"], 1)
            n_rows = 0
            for l in range(DEPTH):
                for col, name, n in ((G_QA, "qnorm_a", DA), (G_KA, "knorm_a", DA), (G_SUB, "subln_a", VA_W),
                                     (G_KV, "norm_kva", KV_RANK), (G_QC, "qnorm_c", QK), (G_KC, "knorm_c", QK)):
                    pool.dma_start(GR[:, l, col:col + n], I[name][l:l + 1, :].broadcast_to([P, n])).then_inc(
                        S["lam_in"], 16)
                for i, name in enumerate(("lambda_q1", "lambda_k1", "lambda_q2", "lambda_k2")):
                    pool.dma_start(LB[:, l, i, :], I[name][l:l + 1, :].broadcast_to([P, DA])).then_inc(
                        S["lam_in"], 16)
            pool.dma_start(ROPE[:, :, :, :], I["rope"].rearrange("p (t s d) -> p t s d", t=4, s=2)).then_inc(
                S["lam_in"], 16)

            def gain_rope(l, buf, t, groups, d, col, scratch, rotate):
                x = buf
                gain = GR[:, l, col:col + d].unsqueeze(1).broadcast_to([P, groups, d])
                ins = nc.gpsimd.tensor_tensor(x, x, gain, ALU.mult)
                if not rotate:
                    ins.then_inc(S["roped"], 1)
                    return
                ch.then(ins)
                tail = x[:, :, d - ROPE_W:d]
                pairs = tail.rearrange("p g (h s n) -> p g h s n", h=2, s=2)
                out = scratch.rearrange("p g (h s n) -> p g h s n", h=2, s=2)
                cos, sin = ROPE[:, t - 1, 0, :], ROPE[:, t - 1, 1, :].rearrange("p (h s n) -> p h s n", h=2, s=2)
                for s in range(2):
                    ins = nc.gpsimd.tensor_tensor(
                        out[:, :, :, s, :], pairs[:, :, :, 1 - s, :],
                        sin[:, :, s, :].unsqueeze(1).broadcast_to([P, groups, 2, 8]), ALU.mult)
                ch.then(ins)
                ch.then(nc.gpsimd.tensor_tensor(tail, tail, cos.unsqueeze(1).broadcast_to([P, groups, ROPE_W]),
                                                ALU.mult))
                nc.gpsimd.tensor_tensor(tail, tail, scratch, ALU.add).then_inc(S["roped"], 1)

            pool.wait_ge(S["setup_done"], 1)
            pool.wait_ge(S["iota_ready"], 8)
            stores = 0

            for l in range(DEPTH):
                for m in range(2 * NT):
                    g, t = m // NT, m % NT
                    buf = QA if g == 0 else KA
                    pool.wait_ge(S["normed"], l * 21 + m + 1)
                    gain_rope(l, buf[:, t, :].rearrange("p (g d) -> p g d", d=DA), t, 2 * HEADS, DA,
                              (G_QA, G_KA)[g], rope_a[:, :].rearrange("p (g d) -> p g d", d=DA), t > 0)
                    if g == 1 and t == 0:
                        pool.wait_ge(S["roped"], l * 21 + NT + 1)
                        pool.dma_start(O["new_diff_k"][0, l].rearrange("s h c d -> s (h c d)"),
                                       KA[:, 0, :]).then_inc(S["stores"], 16)
                        stores += 16
                pool.wait_ge(S["proj_free"], l * 20 + 2 * NT + 1)
                pool.dma_start(O["new_diff_v"][0, l].rearrange("s h e -> s (h e)"), VA[:, 0, :]).then_inc(S["stores"], 16)
                stores += 16
                pool.wait_ge(S["nsq_used"], l * NORMS + 2 * NT + 1)
                pool.dma_start(O["new_mla_ckv"][0, l], CN[:, 0, Q_RANK:Q_RANK + KV_RANK]).then_inc(S["stores"], 16)
                pool.dma_start(O["new_mla_krope"][0, l], CN[:, 0, Q_RANK + KV_RANK:C_W]).then_inc(S["stores"], 16)
                stores += 32
                tiles = [(i % 2, i // 2) for i in range(2 * NT)] + [(1, NT)]
                for i, (k, t) in enumerate(tiles):
                    pool.wait_ge(S["normed"], l * 21 + 2 * NT + i + 1)
                    gain_rope(l, KCn[:, t, :, :] if k else QC[:, t, :, :], t, HEADS, QK, G_KC if k else G_QC,
                              rope_c[:, :, :], 0 < t < 5)
                pool.wait_ge(S["roped"], (l + 1) * 21)
                pool.wait_ge(S["cache_loaded"], (l + 1) * 64)
                pool.wait_ge(S["unit_used"], LAYER_U[l] + U_LATENT + 1)
                pool.wait_ge(S["lat_k"], (l + 1) * KT_TILES)
                pool.wait_ge(S["stores"], stores)
                for h in range(HEADS):
                    if h:
                        pool.wait_ge(S["turned"], l * TURNS + 6 * h)
                    for buf, stack, hi, lo in ((QA, QS[h % 2], (0, 2), (1, 3)), (KA, KS, (0, 1), (2, 3))):
                        src = buf[:, :, h * 2 * DA:(h + 1) * 2 * DA].rearrange("p t (c d) -> p t c d", c=2)
                        nc.gpsimd.tensor_copy(stack[:, :, :, hi[1], :].bitcast(f32r), src)
                        ch.then(nc.gpsimd.tensor_copy(stack[:, :, :, hi[0], :].bitcast(f32r), src))
                        for row in lo:
                            ins = nc.gpsimd.tensor_tensor(stack[:, :, :, row, :].bitcast(f32r), src, stack[:, :, :, 0, :],
                                                          ALU.subtract)
                    ins.then_inc(S["stacked"], 1)
                for t in range(NT):
                    pool.wait_ge(S["subln_done"], l * NT + t + 1)
                    v = QA[:, t, :].rearrange("p (h e) -> p h e", e=VA_W)
                    gain = GR[:, l, G_SUB:G_SUB + VA_W].unsqueeze(1).broadcast_to([P, HEADS, VA_W])
                    nc.gpsimd.tensor_tensor(v, v, gain, ALU.mult).then_inc(S["subln_gained"], 1)
            for t in range(NT):
                pool.wait_ge(S["y_storedA"], t + 1)
                pool.wait_ge(S["y_storedB"], t + 1)
                dst = O["y_prompt"][0] if t == 0 else O["y_sample"][0, (t - 1) * P:t * P]
                pool.dma_start(dst, xn[:, t, :]).then_inc(S["stores"], 16)
                stores += 16
            pool.wait_ge(S["stores"], stores)


        N_ROW_LOADS = 10 * DEPTH + 1

        def unit_width(l, k):
            if U_QKV <= k < U_LATENT:
                return 4 * (A_W if k < U_QKV + 6 else C_W)
            if l == 0 and k >= U_FFN + DENSE_ROUNDS * ROUND + 2 * TAIL_PAIRS:
                return TAIL_FF // P * 256
            return UNIT

        def mixer_act(A, act, l, base, split_hi, squares, nsq, root):
            act.wait_ge(S["unit_used"], base + 1)
            A.copy(UU[:, :, :].rearrange("p c (h n) -> p (c h) n", h=2), PS[:, 0:4, 0:HALF]).then_inc(S["setA_free"], 1)
            split_hi(base + 2)
            split_hi(base + 3)
            split_hi(base + 4)
            act.wait_ge(set_free[0], products_before(base, 0) + 2)
            if l:
                act.wait_ge(S["stores"], l * 64)
            act.dma_start(KA[:, 5, :], I["cache_diff_k"][0, l].rearrange("s h c d -> s (h c d)")).then_inc(
                S["cache_loaded"], 16)
            act.dma_start(VA[:, 5, :], I["cache_diff_v"][0, l].rearrange("s h e -> s (h e)")).then_inc(
                S["cache_loaded"], 16)
            act.dma_start(CC[:, 0:KV_RANK], I["cache_mla_ckv"][0, l]).then_inc(S["cache_loaded"], 16)
            act.dma_start(CC[:, KV_RANK:], I["cache_mla_krope"][0, l]).then_inc(S["cache_loaded"], 16)
            for g in range(4):
                split_hi(base + U_QKV + 2 * g + 2)
                for t in range(NT):
                    m = g * NT + t
                    if t < NT - 1:
                        act.wait_ge(S["proj_ready"], l * 16 + g * (NT - 1) + t + 1)
                    else:
                        act.wait_ge(S["unit_used"], base + U_QKV + 2 * g + 2)
                    dst, w = ((QA[:, t, :], A_W), (KA[:, t, :], A_W), (VA[:, t, :], A_W), (CN[:, t, :], C_W))[g]
                    A.copy(dst, PS[:, m % 8, 0:w]).then_inc(S["proj_free"], 1)
                    if g < 2:
                        act.wait_ge(S["proj_free"], l * 20 + m + 1)
                        squares(dst, A_W).then_inc(S["nsq_ready"], 1)
                        nsq[0] += 1
                        if t:
                            root(2 * HEADS, DA)
                if g < 2:
                    root(2 * HEADS, DA)
                if g < 3:
                    split_hi(base + U_QKV + 2 * g + 3)
            act.wait_ge(S["proj_free"], l * 20 + 20)
            for t in range(NT):
                ssq = SSC[:, 2 * (t % 2):2 * (t % 2) + 2]
                squares(CN[:, t, 0:Q_RANK], Q_RANK, accum=ssq[:, 0:1]).then_inc(S["act"], 1)
                act.wait_ge(S["act"], 3 * (l * NT + t) + 1)
                A.activation(sqn[:, 0:KV_RANK], CN[:, t, Q_RANK:Q_RANK + KV_RANK], ACT.Square,
                             accum_out=ssq[:, 1:2]).then_inc(S["act"], 1)
                act.wait_ge(S["act"], 3 * (l * NT + t) + 2)
                A.activation(ssq[:, 0:1], ssq[:, 0:1], ACT.Identity, bias=eps[:, :], scale=1.0 / Q_RANK)
                A.activation(ssq[:, 1:2], ssq[:, 1:2], ACT.Identity, bias=eps[:, :], scale=1.0 / KV_RANK).then_inc(
                    S["act"], 1)
                act.wait_ge(S["act"], 3 * (l * NT + t) + 3)
                A.activation(RTC[:, 2 * (t % 2):2 * (t % 2) + 2], ssq, ACT.Sqrt).then_inc(S["nsq_ready"], 1)
                nsq[0] += 1

            act.wait_ge(S["unit_used"], base + U_LATENT)

            def turned_hi(t):
                act.wait_ge(S["ct_turned"], l * KT_TILES + t + 1)
                bank = PS[:, t % 2, :]
                if t < NT:
                    for j in range(2):
                        A.activation(CQT[t % 2][:, 0, j, :], bank[0:QR, j * P:(j + 1) * P], ACT.Identity,
                                     scale=VEC[0:QR, l, R_QA + j:R_QA + j + 1])
                A.copy(CKT[t % 2][:, 0, :], bank[:, 2 * P:3 * P]).then_inc(S["ct_hi"], 1)

            turned_hi(0)
            for t in range(KT_TILES):
                if t + 1 < KT_TILES:
                    turned_hi(t + 1)
                act.wait_ge(S["lat_ready"], l * KT_TILES + t + 1)
                if t < NT:
                    A.copy(QC[:, t, :, :].rearrange("p h d -> p (h d)").rearrange("p (a n) -> p a n", a=2),
                           PS[:, 2:4, 0:288]).then_inc(S["lat_q"], 1)
                rope = CN[:, t, Q_RANK + KV_RANK:C_W] if t < NT else CC[:, KV_RANK:]
                A.copy(KCn[:, t, :, NOPE:QK], rope.unsqueeze(1).broadcast_to([P, HEADS, ROPE_W]))
                A.copy(KCn[:, t, :, 0:NOPE], PS[:, 4, 0:A_W].rearrange("p (h d) -> p h d", h=HEADS))
                A.copy(VC[:, t, :], PS[:, 5, 0:A_W]).then_inc(S["lat_k"], 1)
                if t < NT:
                    act.wait_ge(S["lat_q"], l * NT + t + 1)
                    squares(QC[:, t, :, :], HEADS * QK, HEADS).then_inc(S["nsq_ready"], 1)
                    nsq[0] += 1
                act.wait_ge(S["lat_k"], l * KT_TILES + t + 1)
                squares(KCn[:, t, :, :], HEADS * QK, HEADS).then_inc(S["nsq_ready"], 1)
                nsq[0] += 1
                if t < NT:
                    root(HEADS, QK)
                root(HEADS, QK)

            def turn_out(h, g):
                act.wait_ge(S["turned"], l * TURNS + groups_before(h) + g + 1)
                s = h % 2
                if h < HEADS:
                    dst = (QT[s] if g < 3 else KT[s])[:, :, :].rearrange("p c n -> p (c n)")
                    first, end = 512 * (g % 3), (2 * TOK if g < 3 else 12 * P)
                else:
                    dst, first, end = LT[s], 512 * g, 11 * P
                n = min(512, end - first)
                A.copy(dst[:, first:first + n], PS[0:dst.shape[0], 1, 0:n]).then_inc(S["turn_out"], 1)

            for g in range(6):
                turn_out(0, g)
            for k in range(-2, ITEMS):
                if k + 2 < ITEMS:
                    j = k + 2
                    cols = KEYS if TILE_ORDER[j % NT] else P
                    for c in range(comps_of(j)):
                        n = score_of(j, c)
                        bank, m = 2 + 2 * (n % 2), 2 * (j % 3) + c
                        act.wait_ge(S["max_ready"], l * SCORES + n + 1)
                        out = E[:, j % 3, c, 0:cols]
                        if cols == KEYS:
                            src, out = PS[:, bank:bank + 2, 0:HALF], out.rearrange("p (a n) -> p a n", a=2)
                        else:
                            src = PS[:, bank, 0:P]
                        A.activation(out, src, ACT.Exp, bias=NM[:, m:m + 1], accum_out=SM[:, m:m + 1]).then_inc(
                            S["exp_ready"], 1)
                if (hg := groups_at(k, 0)) is not None:
                    turn_out(*hg)
                if k >= 0:
                    cols = KEYS if TILE_ORDER[k % NT] else P
                    act.wait_ge(S["pt_ready"], l * ITEMS + k + 1)
                    A.copy(PT[k % 2][:, 0:cols], PSF[:, 3072:3072 + cols]).then_inc(S["pt_out"], 1)
                if (hg := groups_at(k, 1)) is not None:
                    turn_out(*hg)

            act.wait_ge(S["o_stored"], (l + 1) * 60)
            split_hi(base + U_OUT)
            A.copy(MIX[:, 0, 3:5, :], CONV[:, :, :]).then_inc(S["conv_hi"], 1)
            for t in range(NT):
                squares(QA[:, t, :], A_W).then_inc(S["nsq_ready"], 1)
                nsq[0] += 1
                if t:
                    root(HEADS, VA_W)
            root(HEADS, VA_W)
            for w in range(2 * NT):
                t, i = w // 2, w % 2
                act.wait_ge(S["mix_turned"], l * 10 + w + 1)
                A.copy(MIX[:, 0, 5 * i:5 * i + 3, t * P:(t + 1) * P],
                       PS[:, i, 0:3 * P].rearrange("p (c n) -> p c n", c=3)).then_inc(S["mix_hi"], 1)
            for k in range(1, 6):
                split_hi(base + U_OUT + k)
            if l == 1:
                act.dma_start(RW[:, :].rearrange("p (k e) -> p k e", e=EXPERTS),
                              I["router_w"][0].rearrange("(k p) e -> p k e", p=P)).then_inc(S["router_loaded"], 16)
                act.wait_ge(S["router_loaded"], 16)
                A.copy(RWS[:, 0, :], RW[:, :]).then_inc(S["router_hi"], 1)

        def ffn_act(A, act, l, base, split_hi):
            rounds, tail = layer_rounds(l)
            acts0 = 0 if l == 0 else 4 * DENSE_ROUNDS + TAIL_PAIRS

            def round_(r, u0, pairs, extra, ahead):
                d_pairs, d_u = extra
                for k in range(2 * pairs + 4):
                    if k < 2 * pairs:
                        j = k // 2
                        if k % 2 == 0:
                            act.wait_ge(S["unit_used"], u0 + k + 1 + d_u)
                            act.wait_ge(set_free[1], sets(u0 + k, r, 1))
                            A.activation(SG[:, :, :].rearrange("p c (h n) -> p (c h) n", h=2), PS[:, 0:4, 0:HALF],
                                         ACT.Silu).then_inc(set_free[0], 1)
                        else:
                            if l == 0:
                                act.wait_ge(set_free[1], sets(u0 + k, r, 1) + 1)
                            else:
                                act.wait_ge(S["act_ready"], j + 1 + d_pairs)
                            if j == 0:
                                act.wait_ge(S["unit_used"], u0 + d_u)
                            A.copy(ACTB[:, 0, 2 * j:2 * j + 2, :], AT[:, :, :]).then_inc(S["act_hi"], 1)
                    if k + 2 < 2 * pairs + 4 or ahead:
                        split_hi(u0 + k + 2, r)

            u0 = base + U_FFN
            looped = rounds if tail else rounds - 1
            with act.Fori(0, looped) as r:
                round_(r, u0, 4, (r * 4, r * ROUND), True)
            if tail:
                round_(None, u0 + rounds * ROUND, tail, (rounds * 4, 0), True)
            else:
                round_(None, u0 + looped * ROUND, 4, (looped * 4, 0), False)

        @block.scalar
        def _(act):
            A = nc.scalar

            def split_hi(u, r=None):
                du = 0 if r is None else r * ROUND
                n = N_ADA + u
                act.wait_ge(raw_ready[n % RAW_SLOTS], raw_count(n) + (0 if r is None else r * (ROUND // RAW_SLOTS * 16)))
                if u >= 2:
                    act.wait_ge(S["unit_used"], u - 1 + du)
                k = u - LAYER_U[1] if u >= LAYER_U[1] else u
                src = raw[n % RAW_SLOTS]
                if k == U_LATENT:
                    qw = 2 * HEADS * QK
                    A.copy(WL[0:QR, 0, 0:qw], src[0:QR, 0:qw])
                    A.copy(WL[:, 0, qw:SMALL_W], src[:, qw:SMALL_W]).then_inc(S["split_hi"], 1)
                    return
                w = unit_width(int(u >= LAYER_U[1]), k)
                A.copy(split[u % 2][:, 0, 0:w], src[:, 0:w]).then_inc(S["split_hi"], 1)

            act.wait_ge(S["vec_stored"], 1)
            A.activation(CSIL, CSIL, ACT.Silu).then_inc(S["silu_c"], 1)
            act.wait_ge(S["lam_summed"], 1)
            A.activation(LTMP[:, :], LTMP[:, :], ACT.Exp).then_inc(S["lam_exp"], 1)
            act.wait_ge(S["setup_done"], 1)
            act.wait_ge(S["eps_ready"], 1)
            split_hi(0)
            split_hi(1)
            nsq = [0]

            def squares(src, n, g=None, accum=None):
                if nsq[0]:
                    act.wait_ge(S["nsq_used"], nsq[0])
                ins = A.activation(sqn[:, 0:n] if g is None else sqn[:, 0:n].rearrange("p (g d) -> p g d", g=g), src,
                                   ACT.Square, **({} if accum is None else {"accum_out": accum}))
                return ins

            nroot = [0]

            def root(g, d):
                m = nroot[0] % 2
                act.wait_ge(S["nsq_used"], root_at[nroot[0]])
                sums = SS[:, 12 * m:12 * m + g]
                A.activation(RT[:, 12 * m:12 * m + g], sums, ACT.Sqrt).then_inc(S["root_ready"], 1)
                nroot[0] += 1

            for l in range(DEPTH):
                base = LAYER_U[l]
                for norm in range(2):
                    q = 2 * l + norm
                    if q == 0:
                        act.wait_ge(S["x_stored"], 2 * NT)
                        act.wait_ge(S["small_loaded"], 16)
                    else:
                        last = base if norm == 0 else base + U_FFN
                        for s in range(2):
                            act.wait_ge(set_free[s], products_before(last, s))
                    for kc in range(KC):
                        if kc >= 2:
                            act.wait_ge(S["sq_used"], q * KC + kc - 1)
                        A.activation(HM[:, kc % 2, :], xT[:, kc, :], ACT.Square).then_inc(S["sq_ready"], 1)
                    act.wait_ge(S["sq_used"], (q + 1) * KC)
                    A.activation(rstdT[:, :].rearrange("p (h n) -> p h n", h=2), PS[:, 0:2, 0:HALF], ACT.Sqrt,
                                 bias=eps[:, :], scale=1.0 / D_MODEL).then_inc(S["x_root"], 1)
                    if q == 0:
                        act.wait_ge(S["mod_ready"], 1)
                    for kc in range(KC):
                        act.wait_ge(S["hm_ready"], q * KC + kc + 1)
                        for v, a, b in V_RANGES:
                            sh = MOD[:, l, (M_SHIFT1, M_SHIFT2)[norm] + kc, v:v + 1]
                            ins = A.activation(H[:, 0, kc, a:b], HM[:, kc % 2, a:b], ACT.Identity, bias=sh)
                        ins.then_inc(S["h_hi"], 1)
                    if norm == 0:
                        mixer_act(A, act, l, base, split_hi, squares, nsq, root)
                    else:
                        if l == 1:
                            act.wait_ge(S["top_ready"], 1)
                            A.activation(GT[:, :, 1:2], GT[:, :, 0:1], ACT.Exp).then_inc(S["top_exp"], 1)
                        ffn_act(A, act, l, base, split_hi)
            for t in range(NT):
                act.wait_ge(S["y_turned"], 2 * t + 1)
                A.copy(xn[:, t, 0:512], PS[:, 0, :]).then_inc(S["y_storedA"], 1)

        def mixer_dve(V, dve, ch, l, base, split_lo, sums, finish, refine, nsq):
            for g in range(4):
                split_lo(base + U_QKV + 2 * g + 2)
                if g < 2:
                    for t in range(NT + 1):
                        n = l * 21 + g * NT
                        if t < NT:
                            sums(2 * HEADS, DA, (S["normed"], n + t - 1) if g * NT + t > 1 else None)
                        if t:
                            finish((QA, KA)[g][:, t - 1, :].rearrange("p (g d) -> p g d", d=DA)).then_inc(
                                S["normed"], 1)
                if g < 3:
                    split_lo(base + U_QKV + 2 * g + 3)
            for t in range(NT):
                dve.wait_ge(S["nsq_ready"], nsq[0] + 1)
                nsq[0] += 1
                h = 2 * (t % 2)
                r = RTC[:, h:h + 2]
                refine(r, r, SSC[:, h:h + 2], NT_[:, h:h + 2])
                V.tensor_scalar(CN[:, t, 0:Q_RANK], CN[:, t, 0:Q_RANK], r[:, 0:1], None, ALU.mult)
                kv = CN[:, t, Q_RANK:Q_RANK + KV_RANK]
                V.scalar_tensor_tensor(out=kv, in0=kv, scalar=r[:, 1:2], in1=GR[:, l, G_KV:G_KV + KV_RANK],
                                       op0=ALU.mult, op1=ALU.mult).then_inc(S["nsq_used"], 1)

            def turned_lo(t):
                dve.wait_ge(S["ct_hi"], l * KT_TILES + t + 1)
                bank = PS[:, t % 2, :]
                if t < NT:
                    for j in range(2):
                        V.scalar_tensor_tensor(out=CQT[t % 2][:, 1, j, :], in0=bank[0:QR, j * P:(j + 1) * P],
                                               scalar=VEC[0:QR, l, R_QA + j:R_QA + j + 1],
                                               in1=CQT[t % 2][:, 0, j, :].bitcast(f32), op0=ALU.mult, op1=ALU.subtract)
                V.tensor_tensor(CKT[t % 2][:, 1, :], bank[:, 2 * P:3 * P], CKT[t % 2][:, 0, :].bitcast(f32),
                                ALU.subtract).then_inc(S["ct_lo"], 1)

            turned_lo(0)
            for t in range(KT_TILES):
                if t + 1 < KT_TILES:
                    turned_lo(t + 1)
                n = l * 21 + 2 * NT + 2 * t
                if t < NT:
                    sums(HEADS, QK, (S["normed"], n))
                sums(HEADS, QK, (S["normed"], n))
                if t < NT:
                    finish(QC[:, t, :, :]).then_inc(S["normed"], 1)
                finish(KCn[:, t, :, :]).then_inc(S["normed"], 1)

            for k in range(-2, ITEMS + 1):
                if k + 2 < ITEMS:
                    j = k + 2
                    for c in range(comps_of(j)):
                        n = score_of(j, c)
                        bank, m = 2 + 2 * (n % 2), 2 * (j % 3) + c
                        dve.wait_ge(S["scored"], l * SCORES + n + 1)
                        if TILE_ORDER[j % NT]:
                            src, ax = PS[:, bank:bank + 2, 0:HALF], AX.XY
                        else:
                            src, ax = PS[:, bank, 0:P], AX.X
                        V.tensor_reduce(NM[:, m:m + 1], src, op=ALU.max, axis=ax, negate=True).then_inc(
                            S["max_ready"], 1)
                if 0 <= k + 1 < ITEMS:
                    j = k + 1
                    m, cols = 2 * (j % 3), KEYS if TILE_ORDER[j % NT] else P
                    dve.wait_ge(S["exp_ready"], l * SCORES + score_of(j, comps_of(j) - 1) + 1)
                    if j >= 3:
                        dve.wait_ge(S["o_stored"], l * ITEMS + j - 2)
                    n = comps_of(j)
                    ch.then(V.reciprocal(RC[:, m:m + n], SM[:, m:m + n]))
                    if n == 2:
                        ch.then(V.tensor_scalar(CNEG[:, j % 3:j % 3 + 1], RC[:, m + 1:m + 2], SM[:, m:m + 1],
                                                LAM[:, l:l + 1], ALU.mult, ALU.mult))
                        V.scalar_tensor_tensor(out=E[:, j % 3, 0, 0:cols], in0=E[:, j % 3, 1, 0:cols],
                                               scalar=CNEG[:, j % 3:j % 3 + 1], in1=E[:, j % 3, 0, 0:cols],
                                               op0=ALU.mult, op1=ALU.add).then_inc(S["w_ready"], 1)
                if k >= 1:
                    j = k - 1
                    h, t, m = j // NT, TILE_ORDER[j % NT], 2 * (j % 3)
                    dst = (QA[:, t, h * VA_W:(h + 1) * VA_W] if h < HEADS else
                           OC[:, t, (h - HEADS) * VA_W:(h - HEADS + 1) * VA_W])
                    dve.wait_ge(S["o_ready"], l * ITEMS + j + 1)
                    V.tensor_scalar(dst, PS[:, 0, 0:VA_W], RC[:, m:m + 1], None, ALU.mult).then_inc(S["o_stored"], 1)
            dve.wait_ge(S["o_stored"], (l + 1) * 60)
            split_lo(base + U_OUT)
            dve.wait_ge(S["conv_hi"], l + 1)
            V.tensor_tensor(MIX[:, 1, 3:5, :], CONV[:, :, :], MIX[:, 0, 3:5, :].bitcast(f32), ALU.subtract).then_inc(
                S["conv_lo"], 1)
            for t in range(NT + 1):
                if t < NT:
                    sums(HEADS, VA_W, (S["subln_done"], l * NT + t - 1) if t > 1 else (S["normed"], (l + 1) * 21))
                if t:
                    finish(QA[:, t - 1, :].rearrange("p (h e) -> p h e", e=VA_W)).then_inc(S["subln_done"], 1)
            for w in range(2 * NT):
                t, i = w // 2, w % 2
                dve.wait_ge(S["mix_hi"], l * 10 + w + 1)
                V.tensor_tensor(MIX[:, 1, 5 * i:5 * i + 3, t * P:(t + 1) * P],
                                PS[:, i, 0:3 * P].rearrange("p (c n) -> p c n", c=3),
                                MIX[:, 0, 5 * i:5 * i + 3, t * P:(t + 1) * P].bitcast(f32), ALU.subtract).then_inc(
                    S["mix_lo"], 1)
            split_lo(base + U_OUT + 1)

        def router_dve(V, dve, ch):
            dve.wait_ge(S["router_hi"], 1)
            dve.wait_ge(S["iota_ready"], 8)
            V.tensor_tensor(RWS[:, 1, :], RW[:, :], RWS[:, 0, :].bitcast(f32), ALU.subtract).then_inc(S["router_lo"], 1)
            dve.wait_ge(S["logits_ready"], 1)
            ch.then(V.tensor_copy(LG[:, :, :].rearrange("p t e -> p (t e)"), PS[:, 2, 0:NT * EXPERTS]))
            for t in range(NT):
                ch.then(V.max(TOP[:, t, :], LG[:, t, :]))
                ch.then(V.max_index(IDX[:, t, :], TOP[:, t, :], LG[:, t, :]))
            V.tensor_tensor(GT[:, :, 0:1], TOP[:, :, 1:2], TOP[:, :, 0:1], ALU.subtract).then_inc(S["top_ready"], 1)
            ch.then(V.tensor_copy(IDXF[:, :, :], IDX[:, :, :]))
            dve.wait_ge(S["top_exp"], 1)
            ch.then(V.tensor_scalar(GT[:, :, 2:3], GT[:, :, 1:2], 1.0, None, ALU.add))
            ch.then(V.reciprocal(GT[:, :, 2:3], GT[:, :, 2:3]))
            ch.then(V.tensor_tensor(GT[:, :, 3:4], GT[:, :, 2:3], GT[:, :, 1:2], ALU.mult))
            for t in range(NT):
                for i in range(2):
                    ins = V.tensor_scalar(CB[:, i, t, :], iota8[:, :], IDXF[:, t, i:i + 1], GT[:, t, 2 + i:3 + i],
                                          ALU.is_equal, ALU.mult)
            ch.then(ins)
            V.tensor_tensor(CB[:, 0, :, :], CB[:, 0, :, :], CB[:, 1, :, :], ALU.add).then_inc(S["comb_ready"], 1)
            flat = COMB[:, :, :].rearrange("p e n -> p (e n)")
            for g in range(10):
                dve.wait_ge(S["comb_turned"], g + 1)
                V.tensor_copy(flat[:, 512 * g:512 * g + 512], PS[:, g % 8, :]).then_inc(S["comb_stored"], 1)

        def ffn_dve(V, dve, ch, l, base, split_lo, gated_add):
            rounds, tail = layer_rounds(l)
            acts0 = 0 if l == 0 else 4 * DENSE_ROUNDS + TAIL_PAIRS

            def round_(r, e, u0, pairs, extra, ahead):
                d_pairs, d_u = extra
                n_units = 2 * pairs + 4
                for k in range(n_units):
                    if k < 2 * pairs:
                        j = k // 2
                        if k % 2:
                            dve.wait_ge(S["unit_used"], u0 + k + 1 + d_u)
                            dve.wait_ge(set_free[0], sets(u0 + k - 1, r, 0) + 1)
                            at_ = AT[:, :, :].rearrange("p c (h n) -> p (c h) n", h=2)
                            sg = SG[:, :, :].rearrange("p c (h n) -> p (c h) n", h=2)
                            V.tensor_tensor(at_, sg, PS[:, 4:8, 0:HALF], ALU.mult).then_inc(set_free[1], 1)
                            dve.wait_ge(set_free[1], sets(u0 + k, r, 1) + 1)
                            if l == 1:
                                w = COMB[:, e:e + 1, :] if r is None else COMB[:, bass.ds(e, 1), :]
                                V.tensor_tensor(AT[:, :, :], AT[:, :, :], w.broadcast_to([P, 2, TOK]),
                                                ALU.mult).then_inc(S["act_ready"], 1)
                            dve.wait_ge(S["act_hi"], acts0 + j + 1 + d_pairs)
                            V.tensor_tensor(ACTB[:, 1, 2 * j:2 * j + 2, :], AT[:, :, :],
                                            ACTB[:, 0, 2 * j:2 * j + 2, :].bitcast(f32), ALU.subtract).then_inc(
                                S["act_lo"], 1)
                    else:
                        dve.wait_ge(S["unit_used"], u0 + k + 1 + d_u)
                        gated_add(l, M_GATE2, u0 + k, 2 * (k - 2 * pairs))
                    if k + 2 < n_units or ahead:
                        split_lo(u0 + k + 2, r)

            u0 = base + U_FFN

            looped = rounds if tail else rounds - 1
            with dve.Fori(0, looped) as r:
                round_(r, r, u0, 4, (r * 4, r * ROUND), True)
            if tail:
                round_(None, rounds, u0 + rounds * ROUND, tail, (rounds * 4, 0), True)
            else:
                round_(None, looped, u0 + looped * ROUND, 4, (looped * 4, 0), False)

        @block.vector
        def _(dve):
            V = nc.vector
            ch = Chain(dve, S["dve"])

            def split_lo(u, r=None):
                n = N_ADA + u
                dve.wait_ge(S["split_hi"], u + 1 + (0 if r is None else r * ROUND))
                k = u - LAYER_U[1] if u >= LAYER_U[1] else u
                src = raw[n % RAW_SLOTS]
                if k == U_LATENT:
                    qw = 2 * HEADS * QK
                    V.tensor_tensor(WL[0:QR, 1, 0:qw], src[0:QR, 0:qw], WL[0:QR, 0, 0:qw].bitcast(f32), ALU.subtract)
                    V.tensor_tensor(WL[:, 1, qw:SMALL_W], src[:, qw:SMALL_W], WL[:, 0, qw:SMALL_W].bitcast(f32),
                                    ALU.subtract).then_inc(S["split_lo"], 1)
                    return
                w = unit_width(int(u >= LAYER_U[1]), k)
                V.tensor_tensor(split[u % 2][:, 1, 0:w], src[:, 0:w], split[u % 2][:, 0, 0:w].bitcast(f32),
                                ALU.subtract).then_inc(S["split_lo"], 1)

            for i in range(2 * NT):
                t, half = i // 2, i % 2
                dve.wait_ge(S["x_turned"], i + 1)
                V.tensor_copy(xT[:, 4 * half:4 * half + 4, t * P:(t + 1) * P],
                              PS[:, i % 2, :].rearrange("p (k n) -> p k n", k=4)).then_inc(S["x_stored"], 1)
            dve.wait_ge(S["vec_turned"], 1)
            V.tensor_copy(VEC[:, :, :], PS[:, 2, 0:2 * P].rearrange("p (l r) -> p l r", l=2)[:, :, 0:N_ROWS])
            V.tensor_copy(CSIL, PS[:, 2, 2 * P:2 * P + 2 * KC].rearrange("p (v k) -> p k v", v=2)).then_inc(
                S["vec_stored"], 1)
            dve.wait_ge(S["lam_in"], 16 * N_ROW_LOADS)
            ch.then(V.tensor_tensor(LB[:, :, 0:4:2, :], LB[:, :, 0:4:2, :], LB[:, :, 1:4:2, :], ALU.mult))
            V.tensor_reduce(LTMP[:, :].rearrange("p (l i) -> p l i", l=DEPTH), LB[:, :, 0:4:2, :], op=ALU.add,
                            axis=AX.X).then_inc(S["lam_summed"], 1)
            for l in range(DEPTH):
                l_init = 0.8 - 0.6 * math.exp(-0.3 * l)
                for col, n, factor in ((G_QA, DA, DA ** -0.5), (G_SUB, VA_W, 1.0 - l_init), (G_QC, QK, QK ** -0.5)):
                    V.tensor_scalar(GR[:, l, col:col + n], GR[:, l, col:col + n], float(factor), None, ALU.mult)
            dve.wait_ge(S["lam_exp"], 1)
            for l in range(DEPTH):
                l_init = 0.8 - 0.6 * math.exp(-0.3 * l)
                ch.then(V.tensor_tensor(LAM[:, l:l + 1], LTMP[:, 2 * l + 1:2 * l + 2], LTMP[:, 2 * l:2 * l + 1],
                                        ALU.subtract))
                ins = V.tensor_scalar(LAM[:, l:l + 1], LAM[:, l:l + 1], float(-l_init), None, ALU.add)
            ins.then_inc(S["setup_done"], 1)
            for l in range(DEPTH):
                with dve.Fori(0, ADA_UNITS // RAW_SLOTS) as i:
                    for s in range(RAW_SLOTS):
                        dve.wait_ge(S["ada_used"], l * ADA_UNITS + s + 1 + i * RAW_SLOTS)
                        m = 2 * (i * RAW_SLOTS + s)
                        bias = VEC[:, l, bass.ds(R_BADA + m, 2)].unsqueeze(2).broadcast_to([P, 2, 2])
                        V.tensor_tensor(MOD[:, l, bass.ds(m, 2), :], PS[:, 4 + s, 0:4].rearrange("p (m v) -> p m v", v=2),
                                        bias, ALU.add).then_inc(S["ada_out"], 1)
                dve.wait_ge(S["ada_out"], (l + 1) * ADA_UNITS)
                for norm, m in ((0, M_SCALE1), (1, M_SCALE2)):
                    ch.then(V.tensor_scalar(GS[:, l, norm, :, :], MOD[:, l, m:m + KC, :], 1.0, None, ALU.add))
                    g = VEC[:, l, (R_MIX, R_FFN)[norm]:(R_MIX, R_FFN)[norm] + KC].unsqueeze(2).broadcast_to([P, KC, 2])
                    ins = V.tensor_tensor(GS[:, l, norm, :, :], GS[:, l, norm, :, :], g, ALU.mult)
                    if l == 1 and norm == 1:
                        ins.then_inc(S["mod_ready"], 1)
                    else:
                        ch.then(ins)
            dve.wait_ge(S["mod_ready"], 1)
            split_lo(0)
            split_lo(1)
            nsq = [0]

            def refine(r, root_, mean, tmp):
                ch.then(V.reciprocal(r, root_))
                ch.then(V.tensor_tensor(tmp, r, r, ALU.mult))
                ch.then(V.scalar_tensor_tensor(out=tmp, in0=tmp, scalar=-0.5, in1=mean, op0=ALU.mult, op1=ALU.mult))
                ch.then(V.scalar_tensor_tensor(out=r, in0=tmp, scalar=1.5, in1=r, op0=ALU.add, op1=ALU.mult))

            nroot = [0, 0]

            def sums(g, d, former=None):
                if former is not None:
                    dve.wait_ge(*former)
                dve.wait_ge(S["nsq_ready"], nsq[0] + 1)
                nsq[0] += 1
                m = nroot[0] % 2
                s_ = SS[:, 12 * m:12 * m + g]
                ch.then(V.tensor_reduce(s_, sqn[:, 0:g * d].rearrange("p (g d) -> p g d", g=g), op=ALU.add, axis=AX.X))
                V.tensor_scalar(s_, s_, 1.0 / d, EPS, ALU.mult, ALU.add).then_inc(S["nsq_used"], 1)
                nroot[0] += 1

            def finish(x):
                g, d = x.shape[1], x.shape[2]
                m = nroot[1] % 2
                nroot[1] += 1
                dve.wait_ge(S["root_ready"], nroot[1])
                r = RT[:, 12 * m:12 * m + g]
                refine(r, r, SS[:, 12 * m:12 * m + g], NT_[:, 12 * m:12 * m + g])
                return V.tensor_tensor(x, x, r.unsqueeze(2).broadcast_to([P, g, d]), ALU.mult)

            def gated_add(l, gate, u, chunks):
                for c in range(2):
                    for hf in range(2):
                        for v, a, b in HALVES[hf]:
                            k = chunks + c
                            x = xT[:, k, hf * HALF + a:hf * HALF + b]
                            ins = V.scalar_tensor_tensor(out=x, in0=PS[:, 4 * (u % 2) + 2 * c + hf, a:b],
                                                         scalar=MOD[:, l, gate + k, v:v + 1], in1=x,
                                                         op0=ALU.mult, op1=ALU.add)
                ins.then_inc(set_free[u % 2], 1)

            for l in range(DEPTH):
                base = LAYER_U[l]
                for norm in range(2):
                    q = 2 * l + norm
                    dve.wait_ge(S["x_root"], q + 1)
                    mean = HM[:, 0, :]
                    ch.then(V.tensor_scalar(mean.rearrange("p (h n) -> p h n", h=2), PS[:, 0:2, 0:HALF],
                                            1.0 / D_MODEL, EPS, ALU.mult, ALU.add))
                    refine(rstdT[:, :], rstdT[:, :], mean, HM[:, 1, :])
                    for kc in range(KC + 1):
                        if kc < KC:
                            if kc >= 2:
                                dve.wait_ge(S["h_lo"], q * KC + kc - 1)
                            for v, a, b in V_RANGES:
                                ins = V.scalar_tensor_tensor(out=HM[:, kc % 2, a:b], in0=xT[:, kc, a:b],
                                                             scalar=GS[:, l, norm, kc, v:v + 1], in1=rstdT[:, a:b],
                                                             op0=ALU.mult, op1=ALU.mult)
                            ins.then_inc(S["hm_ready"], 1)
                        if kc:
                            k = kc - 1
                            dve.wait_ge(S["hm_ready"], q * KC + k + 1)
                            dve.wait_ge(S["h_hi"], q * KC + k + 1)
                            for v, a, b in V_RANGES:
                                sh = MOD[:, l, (M_SHIFT1, M_SHIFT2)[norm] + k, v:v + 1]
                                ins = V.scalar_tensor_tensor(out=H[:, 1, k, a:b], in0=HM[:, k % 2, a:b], scalar=sh,
                                                             in1=H[:, 0, k, a:b].bitcast(f32), op0=ALU.add,
                                                             op1=ALU.subtract)
                            ins.then_inc(S["h_lo"], 1)
                    if norm == 0:
                        split_lo(base + 2)
                        dve.wait_ge(S["unit_used"], base + 2)
                        dve.wait_ge(S["setA_free"], products_before(base, 0) + 1)
                        uu = UU[:, :, :].rearrange("p c (h n) -> p (c h) n", h=2)
                        V.tensor_tensor(uu, uu, PS[:, 4:8, 0:HALF], ALU.mult).then_inc(set_free[1], 1)
                        dve.wait_ge(set_free[1], products_before(base, 1) + 1)
                        split_lo(base + 3)
                        for c in range(2):
                            tap = [VEC[:, l, R_CW + 2 * w + c:R_CW + 2 * w + c + 1] for w in range(3)]
                            ch.then(V.tensor_scalar(CONV[:, c, :], UU[:, c, :], tap[1],
                                                    VEC[:, l, R_CB + c:R_CB + c + 1], ALU.mult, ALU.add))
                            for a, b, w in ((0, CTX, CTX), (CTX, TOK, GRID_W)):
                                src = UU[:, c, a:b].rearrange("p (r w) -> p r w", w=w)
                                dst = CONV[:, c, a:b].rearrange("p (r w) -> p r w", w=w)
                                ch.then(V.scalar_tensor_tensor(out=dst[:, :, 1:w], in0=src[:, :, 0:w - 1], scalar=tap[0],
                                                               in1=dst[:, :, 1:w], op0=ALU.mult, op1=ALU.add))
                                ch.then(V.scalar_tensor_tensor(out=dst[:, :, 0:w - 1], in0=src[:, :, 1:w],
                                                               scalar=tap[2], in1=dst[:, :, 0:w - 1], op0=ALU.mult,
                                                               op1=ALU.add))
                        dve.wait_ge(S["unit_used"], base + 3)
                        cv = CONV[:, :, :].rearrange("p c (h n) -> p (c h) n", h=2)
                        V.tensor_tensor(cv, cv, PS[:, 0:4, 0:HALF], ALU.mult).then_inc(set_free[0], 1)
                        split_lo(base + 4)
                        mixer_dve(V, dve, ch, l, base, split_lo, sums, finish, refine, nsq)
                        for j in range(4):
                            u = base + U_OUT + j
                            dve.wait_ge(S["unit_used"], u + 1)
                            gated_add(l, M_GATE1, u, 2 * j)
                            split_lo(u + 2)
                    else:
                        if l == 1:
                            router_dve(V, dve, ch)
                        ffn_dve(V, dve, ch, l, base, split_lo, gated_add)
            for t in range(NT):
                dve.wait_ge(S["y_turned"], 2 * t + 2)
                V.tensor_copy(xn[:, t, 512:1024], PS[:, 1, :]).then_inc(S["y_storedB"], 1)

        def mixer_pe(T, pe, l, base, turn, product):
            for j in range(3):
                if j == 2:
                    pe.wait_ge(set_free[0], products_before(base, 0) + 1)
                product(base + j, KC, H)
            for s in range(2):
                pe.wait_ge(set_free[s], products_before(base + U_QKV, s))
            for g in range(4):
                w_ = A_W if g < 3 else C_W
                for half in range(2):
                    u = base + U_QKV + 2 * g + half
                    pe.wait_ge(S["split_lo"], u + 1)
                    W = split[u % 2][:, :, 0:4 * w_].rearrange("p s (k n) -> p s k n", k=4)
                    for t in range(NT):
                        m = g * NT + t
                        if half == 0 and m >= 8:
                            pe.wait_ge(S["proj_free"], l * 20 + m - 7)
                        for k in range(4):
                            for w, a in ((0, 0), (0, 1), (1, 0)):
                                ins = T.matmul(PS[:, m % 8, 0:w_], H[:, a, 4 * half + k, t * P:(t + 1) * P], W[:, w, k, :],
                                               start=(half == 0 and k == 0 and w == 0 and a == 0),
                                               stop=(half == 1 and k == 3 and w == 1))
                        if half == 1 and t < NT - 1:
                            ins.then_inc(S["proj_ready"], 1)
                    ins.then_inc(S["unit_used"], 1)
            pe.wait_ge(S["proj_free"], (l + 1) * 20)

            def turn_c(t):
                if t >= 2:
                    pe.wait_ge(S["ct_lo"], l * KT_TILES + t - 1)
                if t < NT:
                    pe.wait_ge(S["nsq_used"], l * NORMS + 2 * NT + t + 1)
                    for j in range(2):
                        turn(PS[0:QR, t % 2, j * P:(j + 1) * P], CN[:, t, j * QR:(j + 1) * QR])
                    kv = CN[:, t, Q_RANK:Q_RANK + KV_RANK]
                else:
                    pe.wait_ge(S["cache_loaded"], (l + 1) * 64)
                    kv = CC[:, 0:KV_RANK]
                turn(PS[:, t % 2, 2 * P:3 * P], kv).then_inc(S["ct_turned"], 1)

            pe.wait_ge(S["split_lo"], base + U_LATENT + 1)
            qw = HEADS * QK
            passes = ((0, 0), (1, 0), (0, 1))
            turn_c(0)
            for t in range(KT_TILES):
                if t + 1 < KT_TILES:
                    turn_c(t + 1)
                pe.wait_ge(S["ct_lo"], l * KT_TILES + t + 1)
                if t:
                    pe.wait_ge(S["lat_k"], l * KT_TILES + t)
                if t < NT:
                    for hf in range(2):
                        for j in range(2):
                            for a, w in passes:
                                T.matmul(PS[:, 2 + hf, 0:288], CQT[t % 2][:, a, j, :],
                                         WL[0:QR, w, j * qw + hf * 288:j * qw + (hf + 1) * 288],
                                         start=(j == 0 and a == 0 and w == 0), stop=(j == 1 and w == 1))
                for i in range(2):
                    for a, w in passes:
                        ins = T.matmul(PS[:, 4 + i, 0:A_W], CKT[t % 2][:, a, :],
                                       WL[:, w, 2 * qw + i * A_W:2 * qw + (i + 1) * A_W],
                                       start=(a == 0 and w == 0), stop=(w == 1))
                ins.then_inc(S["lat_ready"], 1)
            pe.wait_ge(S["lat_ready"], (l + 1) * KT_TILES)
            pe.sem_inc(S["unit_used"], 1)

            def turn_group(h, g):
                n = l * TURNS + groups_before(h) + g
                if h or g:
                    pe.wait_ge(S["turn_out"], n)
                if h < HEADS:
                    stack, tiles, first = (QS[h % 2], NT, 4 * g) if g < 3 else (KS, KT_TILES, 4 * (g - 3))
                    blocks = [stack[:, j % tiles, j // tiles, :, :].rearrange("p a d -> p (a d)")
                              for j in range(first, min(first + 4, 2 * tiles))]
                else:
                    blocks = [QC[:, j, h - HEADS, :] if j < NT else KCn[:, j - NT, h - HEADS, :]
                              for j in range(4 * g, min(4 * g + 4, NT + KT_TILES))]
                for i, block in enumerate(blocks):
                    ins = turn(PS[0:block.shape[1], 1, i * P:(i + 1) * P], block)
                ins.then_inc(S["turned"], 1)

            def score(j, c):
                h, t, n = j // NT, TILE_ORDER[j % NT], score_of(j, c)
                s = h % 2
                if n >= 2:
                    pe.wait_ge(S["exp_ready"], l * SCORES + n - 1)
                if j % NT == 0 and c == 0:
                    pe.wait_ge(S["turn_out"], l * TURNS + groups_before(h + 1))
                width = HALF if t else P
                for hf in range(2 if t else 1):
                    first = P + hf * HALF if t else 0
                    if h < HEADS:
                        q, k_ = QT[s][:, c, t * P:(t + 1) * P], KT[s][:, c, first:first + width]
                    else:
                        q, k_ = LT[s][:, t * P:(t + 1) * P], LT[s][:, TOK + first:TOK + first + width]
                    ins = T.matmul(PS[:, 2 + 2 * (n % 2) + hf, 0:width], q, k_, start=True, stop=True)
                ins.then_inc(S["scored"], 1)

            pe.wait_ge(S["lat_k"], (l + 1) * KT_TILES)
            pe.wait_ge(S["roped"], (l + 1) * 21)
            pe.wait_ge(S["stacked"], l * HEADS + 1)
            for g in range(6):
                turn_group(0, g)
            for k in range(-2, ITEMS + 1):
                if k + 2 < ITEMS:
                    for c in range(comps_of(k + 2)):
                        score(k + 2, c)
                if (hg := groups_at(k, 0)) is not None:
                    if hg[0] < HEADS and hg[1] == 0:
                        pe.wait_ge(S["stacked"], l * HEADS + hg[0] + 1)
                    turn_group(*hg)
                if k >= 1:
                    j = k - 1
                    h, t = j // NT, TILE_ORDER[j % NT]
                    pe.wait_ge(S["pt_out"], l * ITEMS + j + 1)
                    if j:
                        pe.wait_ge(S["o_stored"], l * ITEMS + j)
                    tiles = range(1, 6) if t else range(1)
                    V, col = (VA, h * VA_W) if h < HEADS else (VC, (h - HEADS) * VA_W)
                    for i, kt in enumerate(tiles):
                        ins = T.matmul(PS[:, 0, 0:VA_W], PT[j % 2][:, i * P:(i + 1) * P], V[:, kt, col:col + VA_W],
                                       start=(i == 0), stop=(i == len(tiles) - 1))
                    ins.then_inc(S["o_ready"], 1)
                if 0 <= k < ITEMS:
                    if comps_of(k) == 2:
                        pe.wait_ge(S["w_ready"], l * A_ITEMS + k + 1)
                    else:
                        pe.wait_ge(S["exp_ready"], l * SCORES + score_of(k, 0) + 1)
                    for i in range(5 if TILE_ORDER[k % NT] else 1):
                        ins = turn(PSF[:, 3072 + i * P:3072 + (i + 1) * P], E[:, k % 3, 0, i * P:(i + 1) * P])
                    ins.then_inc(S["pt_ready"], 1)
                if (hg := groups_at(k, 1)) is not None:
                    turn_group(*hg)
            pe.wait_ge(S["o_stored"], (l + 1) * 60)
            for w in range(2 * NT):
                t, i = w // 2, w % 2
                if i == 0:
                    pe.wait_ge(S["subln_gained"], l * NT + t + 1)
                if w >= 2:
                    pe.wait_ge(S["mix_lo"], l * 10 + w - 1)
                for c in range(3):
                    src = QA[:, t, c * P:(c + 1) * P] if i == 0 else OC[:, t, c * P:(c + 1) * P]
                    ins = turn(PS[:, i, c * P:(c + 1) * P], src)
                ins.then_inc(S["mix_turned"], 1)
            pe.wait_ge(S["mix_lo"], (l + 1) * 10)
            pe.wait_ge(S["conv_lo"], l + 1)
            for j in range(4):
                u = base + U_OUT + j
                if j >= 2:
                    pe.wait_ge(set_free[u % 2], products_before(u, u % 2))
                product(u, KC, MIX)

        def ffn_pe(T, pe, l, base, turn, product):
            if l == 1:
                pe.wait_ge(S["router_lo"], 1)
                for t in range(NT):
                    for k in range(KC):
                        for a, w in ((0, 0), (1, 0), (0, 1)):
                            ins = T.matmul(PS[:, 2, t * EXPERTS:(t + 1) * EXPERTS], H[:, a, k, t * P:(t + 1) * P],
                                           RWS[:, w, k * EXPERTS:(k + 1) * EXPERTS], start=(k == 0 and a == 0 and w == 0),
                                           stop=(k == KC - 1 and w == 1))
                ins.then_inc(S["logits_ready"], 1)
                pe.wait_ge(S["comb_ready"], 1)
                for g in range(10):
                    if g >= 8:
                        pe.wait_ge(S["comb_stored"], g - 7)
                    for j in range(4):
                        e, t = (4 * g + j) // NT, (4 * g + j) % NT
                        ins = T.matmul(PS[:, g % 8, j * P:(j + 1) * P], CB[:, 0, t, e:e + 1].broadcast_to([P, P]),
                                       ident[:, :], start=True, stop=True)
                    ins.then_inc(S["comb_turned"], 1)
                pe.wait_ge(S["comb_stored"], 10)
            rounds, tail = layer_rounds(l)
            acts0 = 0 if l == 0 else 4 * DENSE_ROUNDS + TAIL_PAIRS

            def round_(r, u0, pairs, kd, d_pairs):
                for k in range(2 * pairs + 4):
                    u = u0 + k
                    free = products_before(u, u % 2)
                    pe.wait_ge(set_free[u % 2], free if r is None else r * (ROUND // 2) + free)
                    if k == 2 * pairs:
                        pe.wait_ge(S["act_lo"], acts0 + pairs + d_pairs)
                    product(u, KC if k < 2 * pairs else kd, H if k < 2 * pairs else ACTB, r)

            u0 = base + U_FFN
            with pe.Fori(0, rounds) as r:
                round_(r, u0, 4, KC, r * 4)
            if tail:
                round_(None, u0 + rounds * ROUND, tail, TAIL_FF // P, rounds * 4)

        @block.tensor
        def _(pe):
            T = nc.tensor

            def turn(out, in_):
                return T.transpose(out, in_, ident[0:in_.shape[0], 0:in_.shape[0]])

            def product(u, k_chunks, A, r=None, cols=256):
                pe.wait_ge(S["split_lo"], u + 1 + (0 if r is None else r * ROUND))
                W = split[u % 2][:, :, 0:k_chunks * cols].rearrange("p s (k n) -> p s k n", k=k_chunks)
                for c in range(2):
                    for k in range(k_chunks):
                        for w, a in ((0, 0), (0, 1), (1, 0)):
                            for hf in range(2):
                                ins = T.matmul(PS[:, 4 * (u % 2) + 2 * c + hf, 0:HALF],
                                               W[:, w, k, c * P:(c + 1) * P], A[:, a, k, hf * HALF:(hf + 1) * HALF],
                                               start=(k == 0 and w == 0 and a == 0),
                                               stop=(k == k_chunks - 1 and w == 1))
                ins.then_inc(S["unit_used"], 1)

            pe.wait_ge(S["const_ready"], 3)
            pe.wait_ge(S["x_loaded"], 16 * NT)
            for i in range(2 * NT):
                if i >= 2:
                    pe.wait_ge(S["x_stored"], i - 1)
                for k in range(4):
                    kc = 4 * (i % 2) + k
                    ins = turn(PS[:, i % 2, k * P:(k + 1) * P], xn[:, i // 2, kc * P:(kc + 1) * P])
                ins.then_inc(S["x_turned"], 1)
            pe.wait_ge(S["small_loaded"], 16 * (2 + 6 * DEPTH))
            for l in range(DEPTH):
                turn(PS[:, 2, l * P:(l + 1) * P], VR[:, l, :])
            turn(PS[:, 2, 2 * P:2 * P + 2 * KC], CR[:, :]).then_inc(S["vec_turned"], 1)
            pe.wait_ge(S["silu_c"], 1)
            per = ADA_COLS // P
            def modulation(i, first):
                for s in range(RAW_SLOTS):
                    pe.wait_ge(raw_ready[s], 16 + i * 16)
                    if not first:
                        pe.wait_ge(S["ada_out"], s + 1 - RAW_SLOTS + i * RAW_SLOTS)
                    W = raw[s][:, :].rearrange("p (k n) -> p k n", k=KC)
                    for c in range(per):
                        for k in range(KC):
                            ins = T.matmul(PS[:, 4 + s, 2 * c:2 * c + 2], W[:, k, c * P:(c + 1) * P], CSIL[:, k, :],
                                           start=(k == 0), stop=(k == KC - 1))
                    ins.then_inc(S["ada_used"], 1)

            modulation(0, True)
            with pe.Fori(1, N_ADA // RAW_SLOTS) as i:
                modulation(i, False)

            for l in range(DEPTH):
                base = LAYER_U[l]
                for norm in range(2):
                    q = 2 * l + norm
                    for kc in range(KC):
                        pe.wait_ge(S["sq_ready"], q * KC + kc + 1)
                        for hf in range(2):
                            ins = T.matmul(PS[:, hf, 0:HALF], ones[:, :], HM[:, kc % 2, hf * HALF:(hf + 1) * HALF],
                                           start=(kc == 0), stop=(kc == KC - 1))
                        ins.then_inc(S["sq_used"], 1)
                    pe.wait_ge(S["h_lo"], (q + 1) * KC)
                    if norm == 0:
                        mixer_pe(T, pe, l, base, turn, product)
                    else:
                        ffn_pe(T, pe, l, base, turn, product)
            for i in range(2 * NT):
                t = i // 2
                if i == 0:
                    for s in range(2):
                        pe.wait_ge(set_free[s], products_before(LAYER_U[1] + U_FFN + FFN_UNITS[1], s))
                elif i >= 2:
                    pe.wait_ge(S[("y_storedA", "y_storedB")[i % 2]], t)
                for k in range(4):
                    ins = turn(PS[:, i % 2, k * P:(k + 1) * P], xT[:, 4 * (i % 2) + k, t * P:(t + 1) * P])
                ins.then_inc(S["y_turned"], 1)

_INPUTS = ["x_prompt", "x_sample", "cache_diff_k", "cache_diff_v", "cache_mla_ckv", "cache_mla_krope", "c", "c_ctx",
           "w_ada", "b_ada", "norm_mix", "norm_ffn", "w_in", "qnorm_a", "knorm_a", "lambda_q1", "lambda_k1",
           "lambda_q2", "lambda_k2", "subln_a", "conv_w", "conv_b", "norm_qa", "w_qb", "norm_kva", "w_kb", "w_vb",
           "qnorm_c", "knorm_c", "w_out", "ffn_w_gate", "ffn_w_up", "ffn_w_down", "router_w", "moe_w_gate",
           "moe_w_up", "moe_w_down"]
_OUTPUTS = [("y_prompt", (1, CTX, D_MODEL)), ("y_sample", (1, LAT, D_MODEL)),
            ("new_diff_k", (1, DEPTH, CTX, HEADS, 2, DA)), ("new_diff_v", (1, DEPTH, CTX, HEADS, VA_W)),
            ("new_mla_ckv", (1, DEPTH, CTX, KV_RANK)), ("new_mla_krope", (1, DEPTH, CTX, ROPE_W))]


def rope_table():
    n = ROPE_W // 4
    inv = np.power(np.float32(10000.0), -np.arange(n, dtype=np.float32) / np.float32(n)).astype(np.float32)
    t = np.arange(LAT)
    out = np.zeros((LAT, 2, 2, 2, n), np.float32)
    for half, pos in enumerate((t // GRID_W, t % GRID_W)):
        ang = pos.astype(np.float32)[:, None] * inv[None, :]
        out[:, 0, half, 0] = out[:, 0, half, 1] = np.cos(ang)
        out[:, 1, half, 0], out[:, 1, half, 1] = -np.sin(ang), np.sin(ang)
    return np.ascontiguousarray(out.reshape(4, P, 64).transpose(1, 0, 2).reshape(P, 256))


def kernel(**inputs):
    import concourse.bacc as bacc
    from concourse.bass_utils import run_bass_kernel_spmd

    nc = bacc.Bacc("TRN2", target_bir_lowering=False, num_devices=1)
    arrays, I, O = {}, {}, {}
    for name in _INPUTS:
        a = np.ascontiguousarray(inputs[name])
        arrays["in_" + name] = a
        I[name] = nc.dram_tensor("in_" + name, a.shape, mybir.dt.from_np(a.dtype), kind="ExternalInput").ap()
    table = rope_table()
    arrays["in_rope"] = table
    I["rope"] = nc.dram_tensor("in_rope", table.shape, mybir.dt.float32, kind="ExternalInput").ap()
    for name, shape in _OUTPUTS:
        O[name] = nc.dram_tensor("out_" + name, shape, mybir.dt.float32, kind="ExternalOutput").ap()
    trunk_program(nc, I, O)
    result = run_bass_kernel_spmd(nc, [arrays], core_ids=[0]).results[0]
    return tuple(result["out_" + name] for name, _ in _OUTPUTS)
```

```python
import math
from contextlib import ExitStack

import numpy as np

import concourse.bass as bass
from concourse import mybir

P = 128
D_MODEL, KC = 1024, 8
CTX, LAT = 128, 512
TOK = CTX + LAT
NT = TOK // P
HALF = TOK // 2
DEPTH = 2
HEADS = 6
DA, VA_W = 32, 64
NOPE, ROPE_W = 64, 32
QK = NOPE + ROPE_W
Q_RANK, KV_RANK = 192, 128
QR = Q_RANK // 2
A_W = HEADS * 2 * DA
W_B = 256
C_W = Q_RANK + KV_RANK + ROPE_W
IN_COLS = 3 * A_W + 3 * W_B + C_W
B_COL = 3 * A_W
C_COL = B_COL + 3 * W_B
PROJ = [(0, A_W), (A_W, A_W), (C_COL, C_W), (2 * A_W, A_W)]
D_FF, EXPERTS, MOE_FF = 2816, 8, 1024
GRID_W = 64
EPS = 1e-6
KEYS = 5 * P
KT_TILES = 6

RAW_SLOTS = 4
UNIT = 2048
ADA_COLS = 512
ADA_BLOCKS = 6 * D_MODEL // ADA_COLS
ADA_UNITS = 2 * ADA_BLOCKS
N_ADA = DEPTH * ADA_UNITS
U_CONV, U_QKV, U_LATENT, U_OUT, U_FFN = 0, 3, 11, 12, 16
ROUND = 12
DENSE_ROUNDS = 2
TAIL_FF = D_FF - DENSE_ROUNDS * MOE_FF
TAIL_PAIRS = TAIL_FF // 256
FFN_UNITS = [DENSE_ROUNDS * ROUND + 2 * TAIL_PAIRS + 4, EXPERTS * ROUND]
LAYER_U = [N_ADA, N_ADA + U_FFN + FFN_UNITS[0]]
SMALL_W = HEADS * QK * 2 + 2 * A_W

R_MIX, R_FFN, R_BADA, R_CW, R_CB, R_QA, N_ROWS = 0, 8, 16, 64, 70, 72, 74
G_QA, G_KA, G_SUB, G_KV, G_QC, G_KC, G_W = 0, 32, 64, 128, 256, 352, 448
M_SHIFT1, M_SCALE1, M_GATE1, M_SHIFT2, M_SCALE2, M_GATE2 = 0, 8, 16, 24, 32, 40

NORMS = 26
ITEMS = 2 * HEADS * NT
A_ITEMS = HEADS * NT
SCORES = 3 * HEADS * NT
TURNS = 9 * HEADS
K_SUM, K_ROOT, K_NORM, K_OUT = A_ITEMS + 4, A_ITEMS + 14, A_ITEMS + 16, ITEMS - NT - 1
TILE_ORDER = [1, 2, 3, 4, 0]


def products_before(u, parity=None):
    n = 0
    for v in range(N_ADA, u):
        r = v - LAYER_U[v >= LAYER_U[1]]
        if (r < U_QKV or r >= U_OUT) and (parity is None or v % 2 == parity):
            n += 1
    return n


def score_of(j, c):
    return 2 * j + c if j < A_ITEMS else A_ITEMS + j


def comps_of(j):
    return 2 if j < A_ITEMS else 1


def groups_of(h):
    return 6 if h < HEADS else 3


def groups_before(h):
    return 6 * min(h, HEADS) + 3 * max(h - HEADS, 0)


def groups_at(k, place):
    if k < 0 or k % NT > 2 or k // NT + 1 >= 2 * HEADS:
        return None
    h = k // NT + 1
    if groups_of(h) == 6:
        return h, 2 * (k % NT) + place
    return (h, k % NT) if place == 0 else None


class Chain:

    def __init__(self, engine, sem):
        self.engine, self.sem, self.n, self.offset = engine, sem, 0, 0

    def then(self, instruction):
        self.n += 1
        instruction.then_inc(self.sem, 1)
        self.engine.wait_ge(self.sem, self.n + self.offset)

    def begin(self, offset):
        self.start, self.offset = self.n, offset
        return self.n

    def end(self, start, per, trips):
        assert self.n - start == per, (self.n - start, per)
        self.n, self.offset = start + per * trips, 0


def trunk_program(nc, I, O):
    f32, f32r = mybir.dt.float32, mybir.dt.float32r
    ALU, ACT, AX = mybir.AluOpType, mybir.ActivationFunctionType, mybir.AxisListType
    nc_base = (nc.sbuf_base + 31) // 32 * 32

    ctx = ExitStack()
    with ctx:
        def at(name, shape, offset, dt=f32):
            return nc.alloc_sbuf_tensor_at(name, shape, dt, offset=nc_base + offset)

        OFF_X, OFF_RAW, OFF_SPLIT, OFF_H = 0, 20480, 53248, 86016
        OFF_R = OFF_H + 40960
        OFF_QC, OFF_E, OFF_OB = OFF_R + 35328, OFF_R + 46848, OFF_R + 62208
        OFF_U = OFF_R + 67328
        OFF_CN = OFF_U + 3200
        OFF_S = OFF_R + 77568
        xT = at("xT", [P, KC, TOK], OFF_X)
        raw = [at(f"raw{i}", [P, UNIT], OFF_RAW + i * UNIT * 4) for i in range(RAW_SLOTS)]
        split = [at(f"split{i}", [P, 2, UNIT], OFF_SPLIT + i * UNIT * 8, f32r) for i in range(2)]
        H = at("H", [P, 2, KC, TOK], OFF_H, f32r)
        MIX = at("MIX", [P, 2, KC, TOK], OFF_H, f32r)
        VC = at("VC", [P, KT_TILES, A_W], OFF_H)
        PT = [at(f"PT{i}", [P, KEYS], OFF_H + 32256 + 2560 * i) for i in range(2)]
        KCn = at("KCn", [P, KT_TILES, HEADS, QK], OFF_H + 18432)
        OFF_CT = OFF_H + 32256
        CQT = [at(f"CQT{i}", [QR, 2, 2, P], OFF_CT + 3072 * i, f32r) for i in range(2)]
        CKT = [at(f"CKT{i}", [P, 2, P], OFF_CT + 3072 * i + 2048, f32r) for i in range(2)]
        rope_c = at("rope_c", [P, HEADS, ROPE_W], OFF_CT + 6144)
        QA = at("QA", [P, NT, A_W], OFF_R)
        KA = at("KA", [P, KT_TILES, A_W], OFF_R + 7680)
        VA = at("VA", [P, KT_TILES, A_W], OFF_R + 16896)
        rope_a = at("rope_a", [P, A_W], OFF_R + 26112)
        QC = at("QC", [P, NT, HEADS, QK], OFF_QC)
        OC = at("OC", [P, NT, HEADS * QK], OFF_QC)[:, :, 0:A_W]
        WL = at("WL", [P, 2, SMALL_W], OFF_E, f32r)
        E = at("E", [P, 3, 2, KEYS], OFF_E)
        CONV = at("CONV", [P, 2, TOK], OFF_OB)
        UU = at("UU", [P, 2, TOK], OFF_U)
        rstdT = at("rstdT", [P, TOK], OFF_U)
        sqn = at("sqn", [P, HEADS * QK], OFF_U)
        CC = at("CC", [P, KV_RANK + ROPE_W], OFF_U + 2560)
        ROWS = at("ROWS", [4, 2, ADA_COLS], OFF_U)
        HM = at("HM", [P, 2, TOK], OFF_U + 5120)
        SQB = at("SQB", [P, NT, A_W], OFF_U)
        SSO, RTO, NTO = (at(n, [P, NT * HEADS], OFF_U + 7680 + 128 * i) for i, n in enumerate(("SSO", "RTO", "NTO")))
        CN = at("CN", [P, NT, C_W], OFF_CN)
        KS = at("KS", [P, KT_TILES, 2, 4, DA], OFF_H + 9216)
        QT = [at(f"QT{s}", [P, 2, TOK], OFF_SPLIT + s * 16384, f32r) for s in range(2)]
        KT = [at(f"KT{s}", [P, 2, KT_TILES * P], OFF_SPLIT + s * 16384 + 5120, f32r) for s in range(2)]
        QS = [at(f"QS{s}", [P, NT, 2, 4, DA], OFF_SPLIT + s * 16384 + 11264) for s in range(2)]
        LT = [at(f"LT{s}", [QK, (NT + KT_TILES) * P], OFF_SPLIT + s * 16384) for s in range(2)]
        ACTB = at("ACTB", [P, 2, KC, TOK], OFF_R, f32r)
        COMB = at("COMB", [P, EXPERTS, TOK], OFF_R + 40960)
        SG = at("SG", [P, 2, TOK], OFF_R + 61440)
        AT = at("AT", [P, 2, TOK], OFF_R + 66560)
        RW = at("RW", [P, KC * EXPERTS], OFF_R + 71680)
        RWS = at("RWS", [P, 2, KC * EXPERTS], OFF_R + 71936, f32r)
        LGT = at("LGT", [EXPERTS, TOK], OFF_R + 66560)
        LG = at("LG", [P, NT, EXPERTS], OFF_R + 72448)
        TOP = at("TOP", [P, NT, 8], OFF_R + 72608)
        IDX = at("IDX", [P, NT, 8], OFF_R + 72768, mybir.dt.uint32)
        IDXF = at("IDXF", [P, NT, 8], OFF_R + 72928)
        GT = at("GT", [P, NT, 4], OFF_R + 73088)
        CB = at("CB", [P, 2, NT, EXPERTS], OFF_R + 73184)
        xn = at("xn", [P, NT, D_MODEL], OFF_H)
        VR = at("VR", [P, DEPTH, P], OFF_R)
        CR = at("CR", [2 * KC, P], OFF_R + 1024)
        LB = at("LB", [P, DEPTH, 4, DA], OFF_R + 1536)
        s_off = [OFF_S]

        def small(name, width, dt=f32):
            t = at(name, [P, width], s_off[0], dt)
            s_off[0] += -(-width * 4 // 32) * 32
            return t

        ident, ones = small("ident", P), small("ones", P)
        MOD = small("MOD", DEPTH * 48 * 2)[:, :].rearrange("p (l m v) -> p l m v", l=DEPTH, v=2)
        GS = small("GS", DEPTH * 2 * KC * 2)[:, :].rearrange("p (l n k v) -> p l n k v", l=DEPTH, n=2, v=2)
        VEC = small("VEC", DEPTH * N_ROWS)[:, :].rearrange("p (l r) -> p l r", l=DEPTH)
        ROPE = small("ROPE", 4 * 64)[:, :].rearrange("p (t s d) -> p t s d", t=4, s=2)
        GR = small("GR", DEPTH * G_W)[:, :].rearrange("p (l g) -> p l g", l=DEPTH)
        CSIL = small("CSIL", 2 * KC)[:, :].rearrange("p (v k) -> p k v", v=2)
        CSPLIT = small("CSPLIT", 4 * KC, f32r)[:, :].rearrange("p (k v) -> p k v", k=KC)
        SEL = small("SEL", 2)[0:4, :]
        LAM, LTMP = small("LAM", DEPTH), small("LTMP", DEPTH * 2)
        SS, SSC = small("SS", 24), small("SSC", 4)
        RT, RTC = small("RT", 24), small("RTC", 4)
        NT_ = small("NT_", 24)
        NM, SM, RC, CNEG = small("NM", 6), small("SM", 6), small("RC", 6), small("CNEG", 3)
        iota8, eps = small("iota8", 8), small("eps", 1)
        assert nc_base + s_off[0] <= nc.sbuf_usable_end, (nc_base + s_off[0], nc.sbuf_usable_end)

        PS = ctx.enter_context(nc.psum_tensor("PS", [P, 8, 512], f32))
        PSF = PS[:, :, :].rearrange("p b n -> p (b n)")

        names = ("const_ready small_loaded x_loaded x_turned x_stored vec_turned vec_stored silu_c "
                 "silu_hi silu_lo rows_out mod_turned ada_out mod_ready lam_in lam_summed lam_exp setup_done "
                 "split_hi split_lo unit_used sq_ready sq_used hm_ready h_hi h_lo "
                 "setA_free setB_free proj_ready proj_free "
                 "nsq_ready nsq_used root_ready x_root eps_ready normed roped cache_loaded stores "
                 "ct_turned ct_hi ct_lo lat_ready lat_q lat_k subln_gained "
                 "stacked turned turn_out scored max_ready exp_ready w_ready pt_ready pt_out o_ready o_stored "
                 "subln_sq subln_sum subln_root subln_done mix_turned mix_hi mix_lo conv_hi conv_lo act_ready act_hi act_lo "
                 "router_loaded router_hi router_lo logits_ready logits_out top_ready top_exp comb_ready comb_turned comb_stored "
                 "y_turned y_storedA y_storedB dve act pool iota_ready").split()
        S = {n: ctx.enter_context(nc.semaphore(n)) for n in names}
        raw_ready = [ctx.enter_context(nc.semaphore(f"raw_ready{i}")) for i in range(RAW_SLOTS)]
        set_free = [S["setA_free"], S["setB_free"]]
        block = ctx.enter_context(nc.Block())

        def raw_count(n):
            extra = sum(32 for l in range(DEPTH)
                        if LAYER_U[l] + U_LATENT <= n
                        and (LAYER_U[l] + U_LATENT - n) % RAW_SLOTS == 0)
            return 16 * (n // RAW_SLOTS + 1) + extra

        def layer_rounds(l):
            return (DENSE_ROUNDS, TAIL_PAIRS) if l == 0 else (EXPERTS, 0)

        V_RANGES = [(0, 0, CTX), (1, CTX, TOK)]

        HALVES = [[(0, 0, CTX), (1, CTX, HALF)], [(1, 0, HALF)]]

        root_at = [l * NORMS + m + 1 for l in range(DEPTH) for m in range(NORMS) if not 2 * NT <= m < 3 * NT]

        def sets(u, r, parity):
            n = products_before(u, parity)
            return n if r is None else r * (ROUND // 2) + n

        @block.sync
        def _(sp):
            def free_slot(n, value=None):
                if n < RAW_SLOTS:
                    return
                sp.wait_ge(S["split_lo"], n - RAW_SLOTS + 1 + (0 if value is None else value))

            def load(n, source, kc, cols, value=None):
                free_slot(n, value)
                dst = raw[n % RAW_SLOTS][:, 0:kc * cols].rearrange("p (k c) -> p k c", k=kc)
                sp.dma_start(dst, source).then_inc(raw_ready[n % RAW_SLOTS], 16)

            def chunks(w):
                return w.rearrange("(k p) n -> p k n", p=P)

            for t in range(NT):
                src = I["x_prompt"][0] if t == 0 else I["x_sample"][0, (t - 1) * P:t * P]
                sp.dma_start(xn[:, t, :], src).then_inc(S["x_loaded"], 16)
            sp.wait_ge(S["const_ready"], 3)
            for v, name in enumerate(("c_ctx", "c")):
                src = (I[name] if v == 0 else I[name][0]).rearrange("(k p) -> k p", p=P)
                sp.dma_start(CR[v * KC:(v + 1) * KC, :], src).then_inc(S["small_loaded"], 16)
            for l in range(DEPTH):
                for row, name, n in ((R_MIX, "norm_mix", 8), (R_FFN, "norm_ffn", 8), (R_BADA, "b_ada", 48),
                                     (R_CB, "conv_b", 2)):
                    sp.dma_start(VR[row:row + n, l, :], I[name][l].rearrange("(k p) -> k p", p=P)).then_inc(
                        S["small_loaded"], 16)
                sp.dma_start(VR[R_CW:R_CW + 6, l, :], I["conv_w"][l].rearrange("w (k p) -> (w k) p", p=P)).then_inc(
                    S["small_loaded"], 16)
                sp.dma_start(VR[R_QA:R_QA + 2, l, 0:QR], I["norm_qa"][l].rearrange("(k p) -> k p", p=QR)).then_inc(
                    S["small_loaded"], 16)
            for l in range(DEPTH):
                w = chunks(I["w_ada"][l])
                for j in range(ADA_UNITS):
                    first, col = KC // 2 * (j % 2), j // 2 * ADA_COLS
                    load(l * ADA_UNITS + j, w[:, first:first + KC // 2, col:col + ADA_COLS], KC // 2, ADA_COLS)
            for l in range(DEPTH):
                base = LAYER_U[l]
                w = chunks(I["w_in"][l])
                for j, col in enumerate((B_COL + W_B, B_COL + 2 * W_B, B_COL)):
                    load(base + U_CONV + j, w[:, :, col:col + W_B], KC, W_B)
                for g, (col, width) in enumerate(PROJ):
                    for half in range(2):
                        load(base + U_QKV + 2 * g + half, w[:, 4 * half:4 * half + 4, col:col + width], 4, width)
                n = base + U_LATENT
                free_slot(n)
                dst = raw[n % RAW_SLOTS]
                qw = HEADS * QK
                sp.dma_start(dst[0:QR, 0:2 * qw].rearrange("p (k c) -> p k c", k=2),
                             I["w_qb"][l].rearrange("(k p) n -> p k n", p=QR)).then_inc(raw_ready[n % RAW_SLOTS], 16)
                sp.dma_start(dst[:, 2 * qw:2 * qw + A_W], I["w_kb"][l]).then_inc(raw_ready[n % RAW_SLOTS], 16)
                sp.dma_start(dst[:, 2 * qw + A_W:SMALL_W], I["w_vb"][l]).then_inc(raw_ready[n % RAW_SLOTS], 16)
                w = chunks(I["w_out"][l])
                for j in range(4):
                    load(base + U_OUT + j, w[:, :, j * 256:(j + 1) * 256], KC, 256)

                n0 = base + U_FFN
                rounds, tail = layer_rounds(l)
                with sp.Fori(0, rounds) as r:
                    if l == 0:
                        wg = I["ffn_w_gate"][0].rearrange("(k p) (r n) -> p k r n", p=P, n=256)
                        wu = I["ffn_w_up"][0].rearrange("(k p) (r n) -> p k r n", p=P, n=256)
                        wd = I["ffn_w_down"][0].rearrange("(r p) n -> p r n", p=P)
                    for j in range(4):
                        n = n0 + 2 * j
                        if l == 0:
                            load(n, wg[:, :, bass.ds(r * 4 + j, 1), :], KC, 256, r * ROUND)
                            load(n + 1, wu[:, :, bass.ds(r * 4 + j, 1), :], KC, 256, r * ROUND)
                        else:
                            for i, name in enumerate(("moe_w_gate", "moe_w_up")):
                                w_ = I[name][0].rearrange("e (k p) n -> p (e k) n", p=P)
                                load(n + i, w_[:, bass.ds(r * KC, KC), j * 256:(j + 1) * 256], KC, 256, r * ROUND)
                    for j in range(4):
                        if l == 0:
                            src = wd[:, bass.ds(r * KC, KC), j * 256:(j + 1) * 256]
                        else:
                            w_ = I["moe_w_down"][0].rearrange("e (k p) n -> p (e k) n", p=P)
                            src = w_[:, bass.ds(r * KC, KC), j * 256:(j + 1) * 256]
                        load(n0 + 8 + j, src, KC, 256, r * ROUND)
                if tail:
                    n = n0 + rounds * ROUND
                    first = rounds * MOE_FF
                    for j in range(tail):
                        for i, name in enumerate(("ffn_w_gate", "ffn_w_up")):
                            c = first + j * 256
                            load(n + 2 * j + i, chunks(I[name][0])[:, :, c:c + 256], KC, 256)
                    for j in range(4):
                        src = I["ffn_w_down"][0][first:].rearrange("(k p) n -> p k n", p=P)
                        load(n + 2 * tail + j, src[:, :, j * 256:(j + 1) * 256], TAIL_FF // P, 256)

        @block.gpsimd
        def _(pool):
            ch = Chain(pool, S["pool"])
            nc.gpsimd.memset(ones[:, :], 1.0).then_inc(S["const_ready"], 1)
            nc.gpsimd.memset(VR[:, :, :], 0.0).then_inc(S["const_ready"], 1)
            ch.then(nc.gpsimd.memset(ident[:, :], 0.0))
            nc.gpsimd.affine_select(out=ident[:, :], in_=ident[:, :], compare_op=ALU.not_equal, fill=1.0, base=0,
                                    pattern=[[-1, P]], channel_multiplier=1).then_inc(S["const_ready"], 1)
            nc.gpsimd.memset(eps[:, :], EPS).then_inc(S["eps_ready"], 1)
            for e in range(8):
                nc.gpsimd.memset(iota8[:, e:e + 1], float(e)).then_inc(S["iota_ready"], 1)
            n_rows = 0
            for l in range(DEPTH):
                for col, name, n in ((G_QA, "qnorm_a", DA), (G_KA, "knorm_a", DA), (G_SUB, "subln_a", VA_W),
                                     (G_KV, "norm_kva", KV_RANK), (G_QC, "qnorm_c", QK), (G_KC, "knorm_c", QK)):
                    pool.dma_start(GR[:, l, col:col + n], I[name][l:l + 1, :].broadcast_to([P, n])).then_inc(
                        S["lam_in"], 16)
                for i, name in enumerate(("lambda_q1", "lambda_k1", "lambda_q2", "lambda_k2")):
                    pool.dma_start(LB[:, l, i, :], I[name][l:l + 1, :].broadcast_to([P, DA])).then_inc(
                        S["lam_in"], 16)
            pool.dma_start(ROPE[:, :, :, :], I["rope"].rearrange("p (t s d) -> p t s d", t=4, s=2)).then_inc(
                S["lam_in"], 16)

            def gain_rope(l, buf, t, groups, d, col, scratch, rotate):
                x = buf
                gain = GR[:, l, col:col + d].unsqueeze(1).broadcast_to([P, groups, d])
                ins = nc.gpsimd.tensor_tensor(x, x, gain, ALU.mult)
                if not rotate:
                    ins.then_inc(S["roped"], 1)
                    return
                ch.then(ins)
                tail = x[:, :, d - ROPE_W:d]
                pairs = tail.rearrange("p g (h s n) -> p g h s n", h=2, s=2)
                out = scratch.rearrange("p g (h s n) -> p g h s n", h=2, s=2)
                cos, sin = ROPE[:, t - 1, 0, :], ROPE[:, t - 1, 1, :].rearrange("p (h s n) -> p h s n", h=2, s=2)
                for s in range(2):
                    ins = nc.gpsimd.tensor_tensor(
                        out[:, :, :, s, :], pairs[:, :, :, 1 - s, :],
                        sin[:, :, s, :].unsqueeze(1).broadcast_to([P, groups, 2, 8]), ALU.mult)
                ch.then(ins)
                ch.then(nc.gpsimd.tensor_tensor(tail, tail, cos.unsqueeze(1).broadcast_to([P, groups, ROPE_W]),
                                                ALU.mult))
                nc.gpsimd.tensor_tensor(tail, tail, scratch, ALU.add).then_inc(S["roped"], 1)

            pool.wait_ge(S["setup_done"], 1)
            pool.wait_ge(S["iota_ready"], 8)
            stores = 0

            for l in range(DEPTH):
                for m in range(2 * NT):
                    g, t = m // NT, m % NT
                    buf = QA if g == 0 else KA
                    pool.wait_ge(S["normed"], l * 21 + m + 1)
                    gain_rope(l, buf[:, t, :].rearrange("p (g d) -> p g d", d=DA), t, 2 * HEADS, DA,
                              (G_QA, G_KA)[g], rope_a[:, :].rearrange("p (g d) -> p g d", d=DA), t > 0)
                    if g == 1 and t == 0:
                        pool.wait_ge(S["roped"], l * 21 + NT + 1)
                        pool.dma_start(O["new_diff_k"][0, l].rearrange("s h c d -> s (h c d)"),
                                       KA[:, 0, :]).then_inc(S["stores"], 16)
                        stores += 16
                pool.wait_ge(S["proj_free"], l * 20 + 3 * NT + 1)
                pool.dma_start(O["new_diff_v"][0, l].rearrange("s h e -> s (h e)"), VA[:, 0, :]).then_inc(S["stores"], 16)
                stores += 16
                pool.wait_ge(S["nsq_used"], l * NORMS + 2 * NT + 1)
                pool.dma_start(O["new_mla_ckv"][0, l], CN[:, 0, Q_RANK:Q_RANK + KV_RANK]).then_inc(S["stores"], 16)
                pool.dma_start(O["new_mla_krope"][0, l], CN[:, 0, Q_RANK + KV_RANK:C_W]).then_inc(S["stores"], 16)
                stores += 32
                def stack(h):
                    if h:
                        pool.wait_ge(S["turned"], l * TURNS + 6 * h)
                    for buf, stack_, hi, lo in ((QA, QS[h % 2], (0, 2), (1, 3)), (KA, KS, (0, 1), (2, 3))):
                        src = buf[:, :, h * 2 * DA:(h + 1) * 2 * DA].rearrange("p t (c d) -> p t c d", c=2)
                        nc.gpsimd.tensor_copy(stack_[:, :, :, hi[1], :].bitcast(f32r), src)
                        ch.then(nc.gpsimd.tensor_copy(stack_[:, :, :, hi[0], :].bitcast(f32r), src))
                        for row in lo:
                            ins = nc.gpsimd.tensor_tensor(stack_[:, :, :, row, :].bitcast(f32r), src,
                                                          stack_[:, :, :, 0, :], ALU.subtract)
                    ins.then_inc(S["stacked"], 1)

                pool.wait_ge(S["roped"], l * 21 + 2 * NT)
                pool.wait_ge(S["cache_loaded"], (l + 1) * 64)
                pool.wait_ge(S["unit_used"], LAYER_U[l] + U_LATENT)
                stack(0)
                tiles = [(i % 2, i // 2) for i in range(2 * NT)] + [(1, NT)]
                for i, (k, t) in enumerate(tiles):
                    pool.wait_ge(S["normed"], l * 21 + 2 * NT + i + 1)
                    gain_rope(l, KCn[:, t, :, :] if k else QC[:, t, :, :], t, HEADS, QK, G_KC if k else G_QC,
                              rope_c[:, :, :], 0 < t < 5)
                pool.wait_ge(S["stores"], stores)
                for h in range(1, HEADS):
                    stack(h)
                pool.wait_ge(S["o_stored"], l * ITEMS + A_ITEMS)
                for t in range(NT):
                    nc.gpsimd.tensor_tensor(SQB[:, t, :], QA[:, t, :], QA[:, t, :], ALU.mult).then_inc(S["subln_sq"], 1)
                for t in range(NT):
                    pool.wait_ge(S["subln_done"], l * NT + t + 1)
                    v = QA[:, t, :].rearrange("p (h e) -> p h e", e=VA_W)
                    gain = GR[:, l, G_SUB:G_SUB + VA_W].unsqueeze(1).broadcast_to([P, HEADS, VA_W])
                    nc.gpsimd.tensor_tensor(v, v, gain, ALU.mult).then_inc(S["subln_gained"], 1)
            for t in range(NT):
                pool.wait_ge(S["y_storedA"], t + 1)
                pool.wait_ge(S["y_storedB"], t + 1)
                dst = O["y_prompt"][0] if t == 0 else O["y_sample"][0, (t - 1) * P:t * P]
                pool.dma_start(dst, xn[:, t, :]).then_inc(S["stores"], 16)
                stores += 16
            pool.wait_ge(S["stores"], stores)


        N_ROW_LOADS = 10 * DEPTH + 1

        def unit_width(l, k):
            if U_QKV <= k < U_LATENT:
                return 4 * PROJ[(k - U_QKV) // 2][1]
            if l == 0 and k >= U_FFN + DENSE_ROUNDS * ROUND + 2 * TAIL_PAIRS:
                return TAIL_FF // P * 256
            return UNIT

        def mixer_act(A, act, l, base, split_hi, squares, nsq, root):
            act.wait_ge(S["unit_used"], base + 1)
            A.copy(UU[:, :, :].rearrange("p c (h n) -> p (c h) n", h=2), PS[:, 0:4, 0:HALF]).then_inc(S["setA_free"], 1)
            split_hi(base + 2)
            split_hi(base + 3)
            split_hi(base + 4)
            act.wait_ge(set_free[0], products_before(base, 0) + 2)
            if l:
                act.wait_ge(S["stores"], l * 64)
            act.dma_start(KA[:, 5, :], I["cache_diff_k"][0, l].rearrange("s h c d -> s (h c d)")).then_inc(
                S["cache_loaded"], 16)
            act.dma_start(VA[:, 5, :], I["cache_diff_v"][0, l].rearrange("s h e -> s (h e)")).then_inc(
                S["cache_loaded"], 16)
            act.dma_start(CC[:, 0:KV_RANK], I["cache_mla_ckv"][0, l]).then_inc(S["cache_loaded"], 16)
            act.dma_start(CC[:, KV_RANK:], I["cache_mla_krope"][0, l]).then_inc(S["cache_loaded"], 16)
            for g in range(4):
                split_hi(base + U_QKV + 2 * g + 2)
                for t in range(NT):
                    m = g * NT + t
                    if t < NT - 1:
                        act.wait_ge(S["proj_ready"], l * 16 + g * (NT - 1) + t + 1)
                    else:
                        act.wait_ge(S["unit_used"], base + U_QKV + 2 * g + 2)
                    dst, w = ((QA, KA, CN, VA)[g][:, t, :], PROJ[g][1])
                    A.copy(dst, PS[:, m % 8, 0:w]).then_inc(S["proj_free"], 1)
                    if g < 2:
                        act.wait_ge(S["proj_free"], l * 20 + m + 1)
                        squares(dst, A_W).then_inc(S["nsq_ready"], 1)
                        nsq[0] += 1
                        if t:
                            root(2 * HEADS, DA)
                if g < 2:
                    root(2 * HEADS, DA)
                if g < 3:
                    split_hi(base + U_QKV + 2 * g + 3)
                if g == 2:
                    act.wait_ge(S["proj_free"], l * 20 + 3 * NT)
                    for t in range(NT):
                        ssq = SSC[:, 2 * (t % 2):2 * (t % 2) + 2]
                        squares(CN[:, t, 0:Q_RANK], Q_RANK, accum=ssq[:, 0:1]).then_inc(S["act"], 1)
                        act.wait_ge(S["act"], 3 * (l * NT + t) + 1)
                        A.activation(sqn[:, 0:KV_RANK], CN[:, t, Q_RANK:Q_RANK + KV_RANK], ACT.Square,
                                     accum_out=ssq[:, 1:2]).then_inc(S["act"], 1)
                        act.wait_ge(S["act"], 3 * (l * NT + t) + 2)
                        A.activation(ssq[:, 0:1], ssq[:, 0:1], ACT.Identity, bias=eps[:, :], scale=1.0 / Q_RANK)
                        A.activation(ssq[:, 1:2], ssq[:, 1:2], ACT.Identity, bias=eps[:, :], scale=1.0 / KV_RANK).then_inc(
                            S["act"], 1)
                        act.wait_ge(S["act"], 3 * (l * NT + t) + 3)
                        A.activation(RTC[:, 2 * (t % 2):2 * (t % 2) + 2], ssq, ACT.Sqrt).then_inc(S["nsq_ready"], 1)
                        nsq[0] += 1
            act.wait_ge(S["unit_used"], base + U_LATENT)

            def turned_hi(t):
                act.wait_ge(S["ct_turned"], l * KT_TILES + t + 1)
                bank = PS[:, t % 2, :]
                if t < NT:
                    for j in range(2):
                        A.activation(CQT[t % 2][:, 0, j, :], bank[0:QR, j * P:(j + 1) * P], ACT.Identity,
                                     scale=VEC[0:QR, l, R_QA + j:R_QA + j + 1])
                A.copy(CKT[t % 2][:, 0, :], bank[:, 2 * P:3 * P]).then_inc(S["ct_hi"], 1)

            turned_hi(0)
            for t in range(KT_TILES):
                if t + 1 < KT_TILES:
                    turned_hi(t + 1)
                act.wait_ge(S["lat_ready"], l * KT_TILES + t + 1)
                if t < NT:
                    A.copy(QC[:, t, :, :].rearrange("p h d -> p (h d)").rearrange("p (a n) -> p a n", a=2),
                           PS[:, 2:4, 0:288]).then_inc(S["lat_q"], 1)
                rope = CN[:, t, Q_RANK + KV_RANK:C_W] if t < NT else CC[:, KV_RANK:]
                A.copy(KCn[:, t, :, NOPE:QK], rope.unsqueeze(1).broadcast_to([P, HEADS, ROPE_W]))
                A.copy(KCn[:, t, :, 0:NOPE], PS[:, 4, 0:A_W].rearrange("p (h d) -> p h d", h=HEADS))
                A.copy(VC[:, t, :], PS[:, 5, 0:A_W]).then_inc(S["lat_k"], 1)
                if t < NT:
                    act.wait_ge(S["lat_q"], l * NT + t + 1)
                    squares(QC[:, t, :, :], HEADS * QK, HEADS).then_inc(S["nsq_ready"], 1)
                    nsq[0] += 1
                act.wait_ge(S["lat_k"], l * KT_TILES + t + 1)
                squares(KCn[:, t, :, :], HEADS * QK, HEADS).then_inc(S["nsq_ready"], 1)
                nsq[0] += 1
                if t < NT:
                    root(HEADS, QK)
                root(HEADS, QK)

            def turn_out(h, g):
                act.wait_ge(S["turned"], l * TURNS + groups_before(h) + g + 1)
                s = h % 2
                if h < HEADS:
                    dst = (QT[s] if g < 3 else KT[s])[:, :, :].rearrange("p c n -> p (c n)")
                    first, end = 512 * (g % 3), (2 * TOK if g < 3 else 12 * P)
                else:
                    dst, first, end = LT[s], 512 * g, 11 * P
                n = min(512, end - first)
                A.copy(dst[:, first:first + n], PS[0:dst.shape[0], 1, 0:n]).then_inc(S["turn_out"], 1)

            for g in range(6):
                turn_out(0, g)
            for k in range(-2, ITEMS):
                if k + 2 < ITEMS:
                    j = k + 2
                    cols = KEYS if TILE_ORDER[j % NT] else P
                    for c in range(comps_of(j)):
                        n = score_of(j, c)
                        bank, m = 2 + 2 * (n % 2), 2 * (j % 3) + c
                        act.wait_ge(S["max_ready"], l * SCORES + n + 1)
                        out = E[:, j % 3, c, 0:cols]
                        if cols == KEYS:
                            src, out = PS[:, bank:bank + 2, 0:HALF], out.rearrange("p (a n) -> p a n", a=2)
                        else:
                            src = PS[:, bank, 0:P]
                        A.activation(out, src, ACT.Exp, bias=NM[:, m:m + 1], accum_out=SM[:, m:m + 1]).then_inc(
                            S["exp_ready"], 1)
                if (hg := groups_at(k, 0)) is not None:
                    turn_out(*hg)
                if k >= 0:
                    cols = KEYS if TILE_ORDER[k % NT] else P
                    act.wait_ge(S["pt_ready"], l * ITEMS + k + 1)
                    A.copy(PT[k % 2][:, 0:cols], PSF[:, 3072:3072 + cols]).then_inc(S["pt_out"], 1)
                if (hg := groups_at(k, 1)) is not None:
                    turn_out(*hg)
                if k == K_ROOT:
                    act.wait_ge(S["subln_sum"], l + 1)
                    A.activation(RTO[:, :], SSO[:, :], ACT.Sqrt).then_inc(S["subln_root"], 1)
                if k == K_OUT:
                    split_hi(base + U_OUT)

            act.wait_ge(S["o_stored"], (l + 1) * 60)
            for w in range(2 * NT):
                i, t = w // NT, w % NT
                if w == NT:
                    A.copy(MIX[:, 0, 3:5, :], CONV[:, :, :]).then_inc(S["conv_hi"], 1)
                act.wait_ge(S["mix_turned"], l * 10 + w + 1)
                A.copy(MIX[:, 0, 5 * i:5 * i + 3, t * P:(t + 1) * P],
                       PS[:, w % 4, 0:3 * P].rearrange("p (c n) -> p c n", c=3)).then_inc(S["mix_hi"], 1)
            for k in range(1, 6):
                split_hi(base + U_OUT + k)
            if l == 1:
                act.dma_start(RW[:, :].rearrange("p (k e) -> p k e", e=EXPERTS),
                              I["router_w"][0].rearrange("(k p) e -> p k e", p=P)).then_inc(S["router_loaded"], 16)
                act.wait_ge(S["router_loaded"], 16)
                A.copy(RWS[:, 0, :], RW[:, :]).then_inc(S["router_hi"], 1)

        def ffn_act(A, act, l, base, split_hi):
            rounds, tail = layer_rounds(l)
            acts0 = 0 if l == 0 else 4 * DENSE_ROUNDS + TAIL_PAIRS

            def round_(r, u0, pairs, extra, ahead):
                d_pairs, d_u = extra
                for k in range(2 * pairs + 4):
                    if k < 2 * pairs:
                        j = k // 2
                        if k % 2 == 0:
                            act.wait_ge(S["unit_used"], u0 + k + 1 + d_u)
                            act.wait_ge(set_free[1], sets(u0 + k, r, 1))
                            A.activation(SG[:, :, :].rearrange("p c (h n) -> p (c h) n", h=2), PS[:, 0:4, 0:HALF],
                                         ACT.Silu).then_inc(set_free[0], 1)
                        else:
                            if l == 0:
                                act.wait_ge(set_free[1], sets(u0 + k, r, 1) + 1)
                            else:
                                act.wait_ge(S["act_ready"], j + 1 + d_pairs)
                            if j == 0:
                                act.wait_ge(S["unit_used"], u0 + d_u)
                            A.copy(ACTB[:, 0, 2 * j:2 * j + 2, :], AT[:, :, :]).then_inc(S["act_hi"], 1)
                    if k + 2 < 2 * pairs + 4 or ahead:
                        split_hi(u0 + k + 2, r)

            u0 = base + U_FFN
            looped = rounds if tail else rounds - 1
            with act.Fori(0, looped) as r:
                round_(r, u0, 4, (r * 4, r * ROUND), True)
            if tail:
                round_(None, u0 + rounds * ROUND, tail, (rounds * 4, 0), True)
            else:
                round_(None, u0 + looped * ROUND, 4, (looped * 4, 0), False)

        @block.scalar
        def _(act):
            A = nc.scalar

            def split_hi(u, r=None):
                du = 0 if r is None else r * ROUND
                n = u
                act.wait_ge(raw_ready[n % RAW_SLOTS], raw_count(n) + (0 if r is None else r * (ROUND // RAW_SLOTS * 16)))
                if u >= 2:
                    act.wait_ge(S["unit_used"], u - 1 + du)
                k = u - LAYER_U[u >= LAYER_U[1]]
                src = raw[n % RAW_SLOTS]
                if k == U_LATENT:
                    qw = 2 * HEADS * QK
                    A.copy(WL[0:QR, 0, 0:qw], src[0:QR, 0:qw])
                    A.copy(WL[:, 0, qw:SMALL_W], src[:, qw:SMALL_W]).then_inc(S["split_hi"], 1)
                    return
                w = unit_width(int(u >= LAYER_U[1]), k)
                A.copy(split[u % 2][:, 0, 0:w], src[:, 0:w]).then_inc(S["split_hi"], 1)

            act.wait_ge(S["vec_stored"], 1)
            A.activation(CSIL, CSIL, ACT.Silu).then_inc(S["silu_c"], 1)
            act.wait_ge(S["silu_c"], 1)
            A.copy(CSPLIT[:, :, 0:2], CSIL).then_inc(S["silu_hi"], 1)
            act.wait_ge(S["lam_summed"], 1)
            A.activation(LTMP[:, :], LTMP[:, :], ACT.Exp).then_inc(S["lam_exp"], 1)
            def rows_out(b, bb):
                act.wait_ge(S["unit_used"], 2 * b + 2)
                A.copy(ROWS[:, bb, :], PS[0:4, 4 + bb, :]).then_inc(S["rows_out"], 1)

            split_hi(0)
            split_hi(1)
            with act.Fori(0, N_ADA // RAW_SLOTS - 1) as i:
                for s in range(RAW_SLOTS):
                    n = s + 2
                    act.wait_ge(raw_ready[n % RAW_SLOTS], raw_count(n) + i * 16)
                    act.wait_ge(S["unit_used"], n - 1 + i * RAW_SLOTS)
                    A.copy(split[s % 2][:, 0, :], raw[n % RAW_SLOTS][:, :]).then_inc(S["split_hi"], 1)
                    if s % 2 == 0:
                        rows_out(2 * i + s // 2, s // 2)
            split_hi(N_ADA - 2)
            rows_out(N_ADA // 2 - 2, 0)
            split_hi(N_ADA - 1)
            rows_out(N_ADA // 2 - 1, 1)
            act.wait_ge(S["setup_done"], 1)
            act.wait_ge(S["eps_ready"], 1)
            split_hi(N_ADA)
            split_hi(N_ADA + 1)
            nsq = [0]

            def squares(src, n, g=None, accum=None):
                if nsq[0]:
                    act.wait_ge(S["nsq_used"], nsq[0])
                ins = A.activation(sqn[:, 0:n] if g is None else sqn[:, 0:n].rearrange("p (g d) -> p g d", g=g), src,
                                   ACT.Square, **({} if accum is None else {"accum_out": accum}))
                return ins

            nroot = [0]

            def root(g, d):
                m = nroot[0] % 2
                act.wait_ge(S["nsq_used"], root_at[nroot[0]])
                sums = SS[:, 12 * m:12 * m + g]
                A.activation(RT[:, 12 * m:12 * m + g], sums, ACT.Sqrt).then_inc(S["root_ready"], 1)
                nroot[0] += 1

            for l in range(DEPTH):
                base = LAYER_U[l]
                for norm in range(2):
                    q = 2 * l + norm
                    if q == 0:
                        act.wait_ge(S["x_stored"], 2 * NT)
                        act.wait_ge(S["small_loaded"], 16)
                    else:
                        last = base if norm == 0 else base + U_FFN
                        for s in range(2):
                            act.wait_ge(set_free[s], products_before(last, s))
                    for kc in range(KC):
                        if kc >= 2:
                            act.wait_ge(S["sq_used"], q * KC + kc - 1)
                        A.activation(HM[:, kc % 2, :], xT[:, kc, :], ACT.Square).then_inc(S["sq_ready"], 1)
                    act.wait_ge(S["sq_used"], (q + 1) * KC)
                    A.activation(rstdT[:, :].rearrange("p (h n) -> p h n", h=2), PS[:, 0:2, 0:HALF], ACT.Sqrt,
                                 bias=eps[:, :], scale=1.0 / D_MODEL).then_inc(S["x_root"], 1)
                    if q == 0:
                        act.wait_ge(S["mod_ready"], 2)
                    for kc in range(KC):
                        act.wait_ge(S["hm_ready"], q * KC + kc + 1)
                        for v, a, b in V_RANGES:
                            sh = MOD[:, l, (M_SHIFT1, M_SHIFT2)[norm] + kc, v:v + 1]
                            ins = A.activation(H[:, 0, kc, a:b], HM[:, kc % 2, a:b], ACT.Identity, bias=sh)
                        ins.then_inc(S["h_hi"], 1)
                    if norm == 0:
                        mixer_act(A, act, l, base, split_hi, squares, nsq, root)
                    else:
                        if l == 1:
                            act.wait_ge(S["top_ready"], 1)
                            A.activation(GT[:, :, 1:2], GT[:, :, 0:1], ACT.Exp).then_inc(S["top_exp"], 1)
                        ffn_act(A, act, l, base, split_hi)
            for t in range(NT):
                act.wait_ge(S["y_turned"], 2 * t + 1)
                A.copy(xn[:, t, 0:512], PS[:, 0, :]).then_inc(S["y_storedA"], 1)

        def mixer_dve(V, dve, ch, l, base, split_lo, sums, finish, refine, nsq):
            for g in range(4):
                split_lo(base + U_QKV + 2 * g + 2)
                if g < 2:
                    for t in range(NT + 1):
                        n = l * 21 + g * NT
                        if t < NT:
                            sums(2 * HEADS, DA, (S["normed"], n + t - 1) if g * NT + t > 1 else None)
                        if t:
                            finish((QA, KA)[g][:, t - 1, :].rearrange("p (g d) -> p g d", d=DA)).then_inc(
                                S["normed"], 1)
                if g < 3:
                    split_lo(base + U_QKV + 2 * g + 3)
                if g == 2:
                    for t in range(NT):
                        dve.wait_ge(S["nsq_ready"], nsq[0] + 1)
                        nsq[0] += 1
                        h = 2 * (t % 2)
                        r = RTC[:, h:h + 2]
                        refine(r, r, SSC[:, h:h + 2], NT_[:, h:h + 2])
                        V.tensor_scalar(CN[:, t, 0:Q_RANK], CN[:, t, 0:Q_RANK], r[:, 0:1], None, ALU.mult)
                        kv = CN[:, t, Q_RANK:Q_RANK + KV_RANK]
                        V.scalar_tensor_tensor(out=kv, in0=kv, scalar=r[:, 1:2], in1=GR[:, l, G_KV:G_KV + KV_RANK],
                                               op0=ALU.mult, op1=ALU.mult).then_inc(S["nsq_used"], 1)

            def turned_lo(t):
                dve.wait_ge(S["ct_hi"], l * KT_TILES + t + 1)
                bank = PS[:, t % 2, :]
                if t < NT:
                    for j in range(2):
                        V.scalar_tensor_tensor(out=CQT[t % 2][:, 1, j, :], in0=bank[0:QR, j * P:(j + 1) * P],
                                               scalar=VEC[0:QR, l, R_QA + j:R_QA + j + 1],
                                               in1=CQT[t % 2][:, 0, j, :].bitcast(f32), op0=ALU.mult, op1=ALU.subtract)
                V.tensor_tensor(CKT[t % 2][:, 1, :], bank[:, 2 * P:3 * P], CKT[t % 2][:, 0, :].bitcast(f32),
                                ALU.subtract).then_inc(S["ct_lo"], 1)

            turned_lo(0)
            for t in range(KT_TILES):
                if t + 1 < KT_TILES:
                    turned_lo(t + 1)
                n = l * 21 + 2 * NT + 2 * t
                if t < NT:
                    sums(HEADS, QK, (S["normed"], n))
                sums(HEADS, QK, (S["normed"], n))
                if t < NT:
                    finish(QC[:, t, :, :]).then_inc(S["normed"], 1)
                finish(KCn[:, t, :, :]).then_inc(S["normed"], 1)

            for k in range(-2, ITEMS + 1):
                if k + 2 < ITEMS:
                    j = k + 2
                    for c in range(comps_of(j)):
                        n = score_of(j, c)
                        bank, m = 2 + 2 * (n % 2), 2 * (j % 3) + c
                        dve.wait_ge(S["scored"], l * SCORES + n + 1)
                        if TILE_ORDER[j % NT]:
                            src, ax = PS[:, bank:bank + 2, 0:HALF], AX.XY
                        else:
                            src, ax = PS[:, bank, 0:P], AX.X
                        V.tensor_reduce(NM[:, m:m + 1], src, op=ALU.max, axis=ax, negate=True).then_inc(
                            S["max_ready"], 1)
                if 0 <= k + 1 < ITEMS:
                    j = k + 1
                    m, cols = 2 * (j % 3), KEYS if TILE_ORDER[j % NT] else P
                    dve.wait_ge(S["exp_ready"], l * SCORES + score_of(j, comps_of(j) - 1) + 1)
                    if j >= 3:
                        dve.wait_ge(S["o_stored"], l * ITEMS + j - 2)
                    n = comps_of(j)
                    ch.then(V.reciprocal(RC[:, m:m + n], SM[:, m:m + n]))
                    if n == 2:
                        ch.then(V.tensor_scalar(CNEG[:, j % 3:j % 3 + 1], RC[:, m + 1:m + 2], SM[:, m:m + 1],
                                                LAM[:, l:l + 1], ALU.mult, ALU.mult))
                        V.scalar_tensor_tensor(out=E[:, j % 3, 0, 0:cols], in0=E[:, j % 3, 1, 0:cols],
                                               scalar=CNEG[:, j % 3:j % 3 + 1], in1=E[:, j % 3, 0, 0:cols],
                                               op0=ALU.mult, op1=ALU.add).then_inc(S["w_ready"], 1)
                if k >= 1:
                    j = k - 1
                    h, t, m = j // NT, TILE_ORDER[j % NT], 2 * (j % 3)
                    dst = (QA[:, t, h * VA_W:(h + 1) * VA_W] if h < HEADS else
                           OC[:, t, (h - HEADS) * VA_W:(h - HEADS + 1) * VA_W])
                    dve.wait_ge(S["o_ready"], l * ITEMS + j + 1)
                    V.tensor_scalar(dst, PS[:, 0, 0:VA_W], RC[:, m:m + 1], None, ALU.mult).then_inc(S["o_stored"], 1)
                if 0 <= k - K_SUM < 2 * NT and (k - K_SUM) % 2 == 0:
                    t = (k - K_SUM) // 2
                    dve.wait_ge(S["subln_sq"], l * NT + t + 1)
                    ch.then(V.tensor_reduce(SSO[:, t * HEADS:(t + 1) * HEADS],
                                            SQB[:, t, :].rearrange("p (h e) -> p h e", e=VA_W), op=ALU.add, axis=AX.X))
                    if t == NT - 1:
                        V.tensor_scalar(SSO[:, :], SSO[:, :], 1.0 / VA_W, EPS, ALU.mult, ALU.add).then_inc(
                            S["subln_sum"], 1)
                if 0 <= k - K_NORM < NT:
                    t = k - K_NORM
                    if t == 0:
                        dve.wait_ge(S["subln_root"], l + 1)
                        refine(RTO[:, :], RTO[:, :], SSO[:, :], NTO[:, :])
                    x = QA[:, t, :].rearrange("p (h e) -> p h e", e=VA_W)
                    V.tensor_tensor(x, x, RTO[:, t * HEADS:(t + 1) * HEADS].unsqueeze(2).broadcast_to([P, HEADS, VA_W]),
                                    ALU.mult).then_inc(S["subln_done"], 1)
                if k == K_OUT + 1:
                    split_lo(base + U_OUT)
            dve.wait_ge(S["o_stored"], (l + 1) * 60)
            for w in range(2 * NT):
                i, t = w // NT, w % NT
                if w == NT:
                    dve.wait_ge(S["conv_hi"], l + 1)
                    V.tensor_tensor(MIX[:, 1, 3:5, :], CONV[:, :, :], MIX[:, 0, 3:5, :].bitcast(f32),
                                    ALU.subtract).then_inc(S["conv_lo"], 1)
                dve.wait_ge(S["mix_hi"], l * 10 + w + 1)
                V.tensor_tensor(MIX[:, 1, 5 * i:5 * i + 3, t * P:(t + 1) * P],
                                PS[:, w % 4, 0:3 * P].rearrange("p (c n) -> p c n", c=3),
                                MIX[:, 0, 5 * i:5 * i + 3, t * P:(t + 1) * P].bitcast(f32), ALU.subtract).then_inc(
                    S["mix_lo"], 1)
            split_lo(base + U_OUT + 1)

        def router_dve(V, dve, ch):
            dve.wait_ge(S["iota_ready"], 8)
            dve.wait_ge(S["logits_ready"], 1)
            V.tensor_copy(LGT[:, :].rearrange("p (h n) -> p h n", h=2), PS[0:EXPERTS, 2:4, 0:HALF]).then_inc(
                S["logits_out"], 1)
            dve.wait_ge(S["logits_ready"], 2)
            ch.then(V.tensor_copy(LG[:, :, :].rearrange("p t e -> p (t e)"), PS[:, 4, 0:NT * EXPERTS]))
            for t in range(NT):
                ch.then(V.max(TOP[:, t, :], LG[:, t, :]))
                ch.then(V.max_index(IDX[:, t, :], TOP[:, t, :], LG[:, t, :]))
            V.tensor_tensor(GT[:, :, 0:1], TOP[:, :, 1:2], TOP[:, :, 0:1], ALU.subtract).then_inc(S["top_ready"], 1)
            ch.then(V.tensor_copy(IDXF[:, :, :], IDX[:, :, :]))
            dve.wait_ge(S["top_exp"], 1)
            ch.then(V.tensor_scalar(GT[:, :, 2:3], GT[:, :, 1:2], 1.0, None, ALU.add))
            ch.then(V.reciprocal(GT[:, :, 2:3], GT[:, :, 2:3]))
            ch.then(V.tensor_tensor(GT[:, :, 3:4], GT[:, :, 2:3], GT[:, :, 1:2], ALU.mult))
            for t in range(NT):
                for i in range(2):
                    ins = V.tensor_scalar(CB[:, i, t, :], iota8[:, :], IDXF[:, t, i:i + 1], GT[:, t, 2 + i:3 + i],
                                          ALU.is_equal, ALU.mult)
            ch.then(ins)
            V.tensor_tensor(CB[:, 0, :, :], CB[:, 0, :, :], CB[:, 1, :, :], ALU.add).then_inc(S["comb_ready"], 1)
            flat = COMB[:, :, :].rearrange("p e n -> p (e n)")
            for g in range(10):
                dve.wait_ge(S["comb_turned"], g + 1)
                V.tensor_copy(flat[:, 512 * g:512 * g + 512], PS[:, 4 + g % 4, :]).then_inc(S["comb_stored"], 1)

        def ffn_dve(V, dve, ch, l, base, split_lo, gated_add):
            rounds, tail = layer_rounds(l)
            acts0 = 0 if l == 0 else 4 * DENSE_ROUNDS + TAIL_PAIRS

            def round_(r, e, u0, pairs, extra, ahead):
                d_pairs, d_u = extra
                n_units = 2 * pairs + 4
                for k in range(n_units):
                    if k < 2 * pairs:
                        j = k // 2
                        if k % 2:
                            dve.wait_ge(S["unit_used"], u0 + k + 1 + d_u)
                            dve.wait_ge(set_free[0], sets(u0 + k - 1, r, 0) + 1)
                            at_ = AT[:, :, :].rearrange("p c (h n) -> p (c h) n", h=2)
                            sg = SG[:, :, :].rearrange("p c (h n) -> p (c h) n", h=2)
                            V.tensor_tensor(at_, sg, PS[:, 4:8, 0:HALF], ALU.mult).then_inc(set_free[1], 1)
                            dve.wait_ge(set_free[1], sets(u0 + k, r, 1) + 1)
                            if l == 1:
                                w = COMB[:, e:e + 1, :] if r is None else COMB[:, bass.ds(e, 1), :]
                                V.tensor_tensor(AT[:, :, :], AT[:, :, :], w.broadcast_to([P, 2, TOK]),
                                                ALU.mult).then_inc(S["act_ready"], 1)
                            dve.wait_ge(S["act_hi"], acts0 + j + 1 + d_pairs)
                            V.tensor_tensor(ACTB[:, 1, 2 * j:2 * j + 2, :], AT[:, :, :],
                                            ACTB[:, 0, 2 * j:2 * j + 2, :].bitcast(f32), ALU.subtract).then_inc(
                                S["act_lo"], 1)
                    else:
                        dve.wait_ge(S["unit_used"], u0 + k + 1 + d_u)
                        gated_add(l, M_GATE2, u0 + k, 2 * (k - 2 * pairs))
                    if k + 2 < n_units or ahead:
                        split_lo(u0 + k + 2, r)

            u0 = base + U_FFN

            looped = rounds if tail else rounds - 1
            with dve.Fori(0, looped) as r:
                round_(r, r, u0, 4, (r * 4, r * ROUND), True)
            if tail:
                round_(None, rounds, u0 + rounds * ROUND, tail, (rounds * 4, 0), True)
            else:
                round_(None, looped, u0 + looped * ROUND, 4, (looped * 4, 0), False)

        @block.vector
        def _(dve):
            V = nc.vector
            ch = Chain(dve, S["dve"])

            def split_lo(u, r=None):
                n = u
                dve.wait_ge(S["split_hi"], u + 1 + (0 if r is None else r * ROUND))
                k = u - LAYER_U[u >= LAYER_U[1]]
                src = raw[n % RAW_SLOTS]
                if k == U_LATENT:
                    qw = 2 * HEADS * QK
                    V.tensor_tensor(WL[0:QR, 1, 0:qw], src[0:QR, 0:qw], WL[0:QR, 0, 0:qw].bitcast(f32), ALU.subtract)
                    V.tensor_tensor(WL[:, 1, qw:SMALL_W], src[:, qw:SMALL_W], WL[:, 0, qw:SMALL_W].bitcast(f32),
                                    ALU.subtract).then_inc(S["split_lo"], 1)
                    return
                w = unit_width(int(u >= LAYER_U[1]), k)
                V.tensor_tensor(split[u % 2][:, 1, 0:w], src[:, 0:w], split[u % 2][:, 0, 0:w].bitcast(f32),
                                ALU.subtract).then_inc(S["split_lo"], 1)

            for i in range(2 * NT):
                t, half = i // 2, i % 2
                dve.wait_ge(S["x_turned"], i + 1)
                V.tensor_copy(xT[:, 4 * half:4 * half + 4, t * P:(t + 1) * P],
                              PS[:, i % 2, :].rearrange("p (k n) -> p k n", k=4)).then_inc(S["x_stored"], 1)
            dve.wait_ge(S["vec_turned"], 1)
            V.tensor_copy(VEC[:, :, :], PS[:, 2, 0:2 * P].rearrange("p (l r) -> p l r", l=2)[:, :, 0:N_ROWS])
            V.tensor_copy(CSIL, PS[:, 2, 2 * P:2 * P + 2 * KC].rearrange("p (v k) -> p k v", v=2)).then_inc(
                S["vec_stored"], 1)
            dve.wait_ge(S["lam_in"], 16 * N_ROW_LOADS)
            ch.then(V.tensor_tensor(LB[:, :, 0:4:2, :], LB[:, :, 0:4:2, :], LB[:, :, 1:4:2, :], ALU.mult))
            V.tensor_reduce(LTMP[:, :].rearrange("p (l i) -> p l i", l=DEPTH), LB[:, :, 0:4:2, :], op=ALU.add,
                            axis=AX.X).then_inc(S["lam_summed"], 1)
            for l in range(DEPTH):
                l_init = 0.8 - 0.6 * math.exp(-0.3 * l)
                for col, n, factor in ((G_QA, DA, DA ** -0.5), (G_SUB, VA_W, 1.0 - l_init), (G_QC, QK, QK ** -0.5)):
                    V.tensor_scalar(GR[:, l, col:col + n], GR[:, l, col:col + n], float(factor), None, ALU.mult)
            dve.wait_ge(S["lam_exp"], 1)
            for l in range(DEPTH):
                l_init = 0.8 - 0.6 * math.exp(-0.3 * l)
                ch.then(V.tensor_tensor(LAM[:, l:l + 1], LTMP[:, 2 * l + 1:2 * l + 2], LTMP[:, 2 * l:2 * l + 1],
                                        ALU.subtract))
                ins = V.tensor_scalar(LAM[:, l:l + 1], LAM[:, l:l + 1], float(-l_init), None, ALU.add)
            ins.then_inc(S["setup_done"], 1)
            def modulation_out(l, b, bb):
                dve.wait_ge(S["mod_turned"], l * ADA_BLOCKS + b + 1)
                bias = VEC[:, l, bass.ds(R_BADA + 4 * b, 4)].unsqueeze(2).broadcast_to([P, 4, 2])
                V.tensor_tensor(MOD[:, l, bass.ds(4 * b, 4), :], PS[:, 6 + bb, 0:8].rearrange("p (m v) -> p m v", v=2),
                                bias, ALU.add).then_inc(S["ada_out"], 1)

            V.tensor_tensor(SEL[:, :], ident[0:4, 0:2], ident[0:4, 2:4], ALU.add).then_inc(S["silu_lo"], 1)
            dve.wait_ge(S["silu_hi"], 1)
            V.tensor_tensor(CSPLIT[:, :, 2:4], CSIL, CSPLIT[:, :, 0:2].bitcast(f32), ALU.subtract).then_inc(
                S["silu_lo"], 1)
            split_lo(0)
            split_lo(1)
            for l in range(DEPTH):
                last = l == DEPTH - 1
                with dve.Fori(0, ADA_UNITS // RAW_SLOTS - last) as i:
                    for s in range(RAW_SLOTS):
                        n = l * ADA_UNITS + s + 2
                        dve.wait_ge(S["split_hi"], n + 1 + i * RAW_SLOTS)
                        V.tensor_tensor(split[s % 2][:, 1, :], raw[n % RAW_SLOTS][:, :],
                                        split[s % 2][:, 0, :].bitcast(f32), ALU.subtract).then_inc(S["split_lo"], 1)
                        if s % 2 == 0:
                            modulation_out(l, 2 * i + s // 2, s // 2)
            split_lo(N_ADA - 2)
            modulation_out(l, ADA_BLOCKS - 2, 0)
            split_lo(N_ADA - 1)
            modulation_out(l, ADA_BLOCKS - 1, 1)
            dve.wait_ge(S["ada_out"], N_ADA // 2)
            for norm, m in ((0, M_SCALE1), (1, M_SCALE2)):
                ch.then(V.tensor_scalar(GS[:, :, norm, :, :], MOD[:, :, m:m + KC, :], 1.0, None, ALU.add))
                first = (R_MIX, R_FFN)[norm]
                g = VEC[:, :, first:first + KC].unsqueeze(3).broadcast_to([P, DEPTH, KC, 2])
                V.tensor_tensor(GS[:, :, norm, :, :], GS[:, :, norm, :, :], g, ALU.mult).then_inc(S["mod_ready"], 1)
            dve.wait_ge(S["mod_ready"], 2)
            split_lo(N_ADA)
            split_lo(N_ADA + 1)
            nsq = [0]

            def refine(r, root_, mean, tmp):
                ch.then(V.reciprocal(r, root_))
                ch.then(V.tensor_tensor(tmp, r, r, ALU.mult))
                ch.then(V.scalar_tensor_tensor(out=tmp, in0=tmp, scalar=-0.5, in1=mean, op0=ALU.mult, op1=ALU.mult))
                ch.then(V.scalar_tensor_tensor(out=r, in0=tmp, scalar=1.5, in1=r, op0=ALU.add, op1=ALU.mult))

            nroot = [0, 0]

            def sums(g, d, former=None):
                if former is not None:
                    dve.wait_ge(*former)
                dve.wait_ge(S["nsq_ready"], nsq[0] + 1)
                nsq[0] += 1
                m = nroot[0] % 2
                s_ = SS[:, 12 * m:12 * m + g]
                ch.then(V.tensor_reduce(s_, sqn[:, 0:g * d].rearrange("p (g d) -> p g d", g=g), op=ALU.add, axis=AX.X))
                V.tensor_scalar(s_, s_, 1.0 / d, EPS, ALU.mult, ALU.add).then_inc(S["nsq_used"], 1)
                nroot[0] += 1

            def finish(x):
                g, d = x.shape[1], x.shape[2]
                m = nroot[1] % 2
                nroot[1] += 1
                dve.wait_ge(S["root_ready"], nroot[1])
                r = RT[:, 12 * m:12 * m + g]
                refine(r, r, SS[:, 12 * m:12 * m + g], NT_[:, 12 * m:12 * m + g])
                return V.tensor_tensor(x, x, r.unsqueeze(2).broadcast_to([P, g, d]), ALU.mult)

            def gated_add(l, gate, u, chunks):
                for c in range(2):
                    for hf in range(2):
                        for v, a, b in HALVES[hf]:
                            k = chunks + c
                            x = xT[:, k, hf * HALF + a:hf * HALF + b]
                            ins = V.scalar_tensor_tensor(out=x, in0=PS[:, 4 * (u % 2) + 2 * c + hf, a:b],
                                                         scalar=MOD[:, l, gate + k, v:v + 1], in1=x,
                                                         op0=ALU.mult, op1=ALU.add)
                ins.then_inc(set_free[u % 2], 1)

            for l in range(DEPTH):
                base = LAYER_U[l]
                for norm in range(2):
                    q = 2 * l + norm
                    dve.wait_ge(S["x_root"], q + 1)
                    mean = HM[:, 0, :]
                    ch.then(V.tensor_scalar(mean.rearrange("p (h n) -> p h n", h=2), PS[:, 0:2, 0:HALF],
                                            1.0 / D_MODEL, EPS, ALU.mult, ALU.add))
                    refine(rstdT[:, :], rstdT[:, :], mean, HM[:, 1, :])
                    if q == 3:
                        dve.wait_ge(S["router_hi"], 1)
                        V.tensor_tensor(RWS[:, 1, :], RW[:, :], RWS[:, 0, :].bitcast(f32), ALU.subtract).then_inc(
                            S["router_lo"], 1)
                    for kc in range(KC + 1):
                        if kc < KC:
                            if kc >= 2:
                                dve.wait_ge(S["h_lo"], q * KC + kc - 1)
                            for v, a, b in V_RANGES:
                                ins = V.scalar_tensor_tensor(out=HM[:, kc % 2, a:b], in0=xT[:, kc, a:b],
                                                             scalar=GS[:, l, norm, kc, v:v + 1], in1=rstdT[:, a:b],
                                                             op0=ALU.mult, op1=ALU.mult)
                            ins.then_inc(S["hm_ready"], 1)
                        if kc:
                            k = kc - 1
                            dve.wait_ge(S["hm_ready"], q * KC + k + 1)
                            dve.wait_ge(S["h_hi"], q * KC + k + 1)
                            for v, a, b in V_RANGES:
                                sh = MOD[:, l, (M_SHIFT1, M_SHIFT2)[norm] + k, v:v + 1]
                                ins = V.scalar_tensor_tensor(out=H[:, 1, k, a:b], in0=HM[:, k % 2, a:b], scalar=sh,
                                                             in1=H[:, 0, k, a:b].bitcast(f32), op0=ALU.add,
                                                             op1=ALU.subtract)
                            ins.then_inc(S["h_lo"], 1)
                    if norm == 0:
                        split_lo(base + 2)
                        dve.wait_ge(S["unit_used"], base + 2)
                        dve.wait_ge(S["setA_free"], products_before(base, 0) + 1)
                        uu = UU[:, :, :].rearrange("p c (h n) -> p (c h) n", h=2)
                        V.tensor_tensor(uu, uu, PS[:, 4:8, 0:HALF], ALU.mult).then_inc(set_free[1], 1)
                        dve.wait_ge(set_free[1], products_before(base, 1) + 1)
                        split_lo(base + 3)
                        for c in range(2):
                            tap = [VEC[:, l, R_CW + 2 * w + c:R_CW + 2 * w + c + 1] for w in range(3)]
                            ch.then(V.tensor_scalar(CONV[:, c, :], UU[:, c, :], tap[1],
                                                    VEC[:, l, R_CB + c:R_CB + c + 1], ALU.mult, ALU.add))
                            for a, b, w in ((0, CTX, CTX), (CTX, TOK, GRID_W)):
                                src = UU[:, c, a:b].rearrange("p (r w) -> p r w", w=w)
                                dst = CONV[:, c, a:b].rearrange("p (r w) -> p r w", w=w)
                                ch.then(V.scalar_tensor_tensor(out=dst[:, :, 1:w], in0=src[:, :, 0:w - 1], scalar=tap[0],
                                                               in1=dst[:, :, 1:w], op0=ALU.mult, op1=ALU.add))
                                ch.then(V.scalar_tensor_tensor(out=dst[:, :, 0:w - 1], in0=src[:, :, 1:w],
                                                               scalar=tap[2], in1=dst[:, :, 0:w - 1], op0=ALU.mult,
                                                               op1=ALU.add))
                        dve.wait_ge(S["unit_used"], base + 3)
                        cv = CONV[:, :, :].rearrange("p c (h n) -> p (c h) n", h=2)
                        V.tensor_tensor(cv, cv, PS[:, 0:4, 0:HALF], ALU.mult).then_inc(set_free[0], 1)
                        split_lo(base + 4)
                        mixer_dve(V, dve, ch, l, base, split_lo, sums, finish, refine, nsq)
                        for j in range(4):
                            u = base + U_OUT + j
                            dve.wait_ge(S["unit_used"], u + 1)
                            gated_add(l, M_GATE1, u, 2 * j)
                            split_lo(u + 2)
                    else:
                        if l == 1:
                            router_dve(V, dve, ch)
                        ffn_dve(V, dve, ch, l, base, split_lo, gated_add)
            for t in range(NT):
                dve.wait_ge(S["y_turned"], 2 * t + 2)
                V.tensor_copy(xn[:, t, 512:1024], PS[:, 1, :]).then_inc(S["y_storedB"], 1)

        def mixer_pe(T, pe, l, base, turn, product, h_ready):
            for j in range(3):
                if j == 2:
                    pe.wait_ge(set_free[0], products_before(base, 0) + 1)
                product(base + j, KC, H, ready=None if j else h_ready)
            for s in range(2):
                pe.wait_ge(set_free[s], products_before(base + U_QKV, s))
            for g in range(4):
                w_ = PROJ[g][1]
                for half in range(2):
                    u = base + U_QKV + 2 * g + half
                    pe.wait_ge(S["split_lo"], u + 1)
                    W = split[u % 2][:, :, 0:4 * w_].rearrange("p s (k n) -> p s k n", k=4)
                    for t in range(NT):
                        m = g * NT + t
                        if half == 0 and m >= 8:
                            pe.wait_ge(S["proj_free"], l * 20 + m - 7)
                        for k in range(4):
                            for w, a in ((0, 0), (0, 1), (1, 0)):
                                ins = T.matmul(PS[:, m % 8, 0:w_], H[:, a, 4 * half + k, t * P:(t + 1) * P], W[:, w, k, :],
                                               start=(half == 0 and k == 0 and w == 0 and a == 0),
                                               stop=(half == 1 and k == 3 and w == 1))
                        if half == 1 and t < NT - 1:
                            ins.then_inc(S["proj_ready"], 1)
                    ins.then_inc(S["unit_used"], 1)
            pe.wait_ge(S["proj_free"], (l + 1) * 20)

            def turn_c(t):
                if t >= 2:
                    pe.wait_ge(S["ct_lo"], l * KT_TILES + t - 1)
                if t < NT:
                    pe.wait_ge(S["nsq_used"], l * NORMS + 2 * NT + t + 1)
                    for j in range(2):
                        turn(PS[0:QR, t % 2, j * P:(j + 1) * P], CN[:, t, j * QR:(j + 1) * QR])
                    kv = CN[:, t, Q_RANK:Q_RANK + KV_RANK]
                else:
                    pe.wait_ge(S["cache_loaded"], (l + 1) * 64)
                    kv = CC[:, 0:KV_RANK]
                turn(PS[:, t % 2, 2 * P:3 * P], kv).then_inc(S["ct_turned"], 1)

            pe.wait_ge(S["split_lo"], base + U_LATENT + 1)
            qw = HEADS * QK
            passes = ((0, 0), (1, 0), (0, 1))
            turn_c(0)
            for t in range(KT_TILES):
                if t + 1 < KT_TILES:
                    turn_c(t + 1)
                pe.wait_ge(S["ct_lo"], l * KT_TILES + t + 1)
                if t:
                    pe.wait_ge(S["lat_k"], l * KT_TILES + t)
                if t < NT:
                    for hf in range(2):
                        for j in range(2):
                            for a, w in passes:
                                T.matmul(PS[:, 2 + hf, 0:288], CQT[t % 2][:, a, j, :],
                                         WL[0:QR, w, j * qw + hf * 288:j * qw + (hf + 1) * 288],
                                         start=(j == 0 and a == 0 and w == 0), stop=(j == 1 and w == 1))
                for i in range(2):
                    for a, w in passes:
                        ins = T.matmul(PS[:, 4 + i, 0:A_W], CKT[t % 2][:, a, :],
                                       WL[:, w, 2 * qw + i * A_W:2 * qw + (i + 1) * A_W],
                                       start=(a == 0 and w == 0), stop=(w == 1))
                ins.then_inc(S["lat_ready"], 1)
            pe.wait_ge(S["lat_ready"], (l + 1) * KT_TILES)
            pe.sem_inc(S["unit_used"], 1)

            def turn_group(h, g):
                n = l * TURNS + groups_before(h) + g
                if h or g:
                    pe.wait_ge(S["turn_out"], n)
                if h < HEADS:
                    stack, tiles, first = (QS[h % 2], NT, 4 * g) if g < 3 else (KS, KT_TILES, 4 * (g - 3))
                    blocks = [stack[:, j % tiles, j // tiles, :, :].rearrange("p a d -> p (a d)")
                              for j in range(first, min(first + 4, 2 * tiles))]
                else:
                    blocks = [QC[:, j, h - HEADS, :] if j < NT else KCn[:, j - NT, h - HEADS, :]
                              for j in range(4 * g, min(4 * g + 4, NT + KT_TILES))]
                for i, block in enumerate(blocks):
                    ins = turn(PS[0:block.shape[1], 1, i * P:(i + 1) * P], block)
                ins.then_inc(S["turned"], 1)

            def score(j, c):
                h, t, n = j // NT, TILE_ORDER[j % NT], score_of(j, c)
                s = h % 2
                if n >= 2:
                    pe.wait_ge(S["exp_ready"], l * SCORES + n - 1)
                if j % NT == 0 and c == 0:
                    pe.wait_ge(S["turn_out"], l * TURNS + groups_before(h + 1))
                width = HALF if t else P
                for hf in range(2 if t else 1):
                    first = P + hf * HALF if t else 0
                    if h < HEADS:
                        q, k_ = QT[s][:, c, t * P:(t + 1) * P], KT[s][:, c, first:first + width]
                    else:
                        q, k_ = LT[s][:, t * P:(t + 1) * P], LT[s][:, TOK + first:TOK + first + width]
                    ins = T.matmul(PS[:, 2 + 2 * (n % 2) + hf, 0:width], q, k_, start=True, stop=True)
                ins.then_inc(S["scored"], 1)

            pe.wait_ge(S["lat_k"], (l + 1) * KT_TILES)
            pe.wait_ge(S["stacked"], l * HEADS + 1)
            for g in range(6):
                turn_group(0, g)
            for k in range(-2, ITEMS + 1):
                if k + 2 < ITEMS:
                    for c in range(comps_of(k + 2)):
                        score(k + 2, c)
                if (hg := groups_at(k, 0)) is not None:
                    if hg == (HEADS, 0):
                        pe.wait_ge(S["roped"], (l + 1) * 21)
                    if hg[0] < HEADS and hg[1] == 0:
                        pe.wait_ge(S["stacked"], l * HEADS + hg[0] + 1)
                    turn_group(*hg)
                if k >= 1:
                    j = k - 1
                    h, t = j // NT, TILE_ORDER[j % NT]
                    pe.wait_ge(S["pt_out"], l * ITEMS + j + 1)
                    if j:
                        pe.wait_ge(S["o_stored"], l * ITEMS + j)
                    tiles = range(1, 6) if t else range(1)
                    V, col = (VA, h * VA_W) if h < HEADS else (VC, (h - HEADS) * VA_W)
                    for i, kt in enumerate(tiles):
                        ins = T.matmul(PS[:, 0, 0:VA_W], PT[j % 2][:, i * P:(i + 1) * P], V[:, kt, col:col + VA_W],
                                       start=(i == 0), stop=(i == len(tiles) - 1))
                    ins.then_inc(S["o_ready"], 1)
                if 0 <= k < ITEMS:
                    if comps_of(k) == 2:
                        pe.wait_ge(S["w_ready"], l * A_ITEMS + k + 1)
                    else:
                        pe.wait_ge(S["exp_ready"], l * SCORES + score_of(k, 0) + 1)
                    for i in range(5 if TILE_ORDER[k % NT] else 1):
                        ins = turn(PSF[:, 3072 + i * P:3072 + (i + 1) * P], E[:, k % 3, 0, i * P:(i + 1) * P])
                    ins.then_inc(S["pt_ready"], 1)
                if (hg := groups_at(k, 1)) is not None:
                    turn_group(*hg)
            pe.wait_ge(S["o_stored"], (l + 1) * 60)
            for w in range(2 * NT):
                i, t = w // NT, w % NT
                if i == 0:
                    pe.wait_ge(S["subln_gained"], l * NT + t + 1)
                if w >= 4:
                    pe.wait_ge(S["mix_lo"], l * 10 + w - 3)
                for c in range(3):
                    src = QA[:, t, c * P:(c + 1) * P] if i == 0 else OC[:, t, c * P:(c + 1) * P]
                    ins = turn(PS[:, w % 4, c * P:(c + 1) * P], src)
                ins.then_inc(S["mix_turned"], 1)
            pe.wait_ge(S["mix_lo"], (l + 1) * 10)
            pe.wait_ge(S["conv_lo"], l + 1)
            for j in range(4):
                u = base + U_OUT + j
                if j >= 2:
                    pe.wait_ge(set_free[u % 2], products_before(u, u % 2))
                product(u, KC, MIX)

        def ffn_pe(T, pe, l, base, turn, product, h_ready):
            if l == 1:
                pe.wait_ge(S["router_lo"], 1)
                for k in range(KC):
                    h_ready(k)
                    for a, w in ((0, 0), (1, 0), (0, 1)):
                        for hf in range(2):
                            ins = T.matmul(PS[0:EXPERTS, 2 + hf, 0:HALF], RWS[:, w, k * EXPERTS:(k + 1) * EXPERTS],
                                           H[:, a, k, hf * HALF:(hf + 1) * HALF], start=(k == 0 and a == 0 and w == 0),
                                           stop=(k == KC - 1 and w == 1))
                ins.then_inc(S["logits_ready"], 1)
                pe.wait_ge(S["logits_out"], 1)
                for t in range(NT):
                    ins = turn(PS[:, 4, t * EXPERTS:(t + 1) * EXPERTS], LGT[:, t * P:(t + 1) * P])
                ins.then_inc(S["logits_ready"], 1)

            def combine():
                pe.wait_ge(S["comb_ready"], 1)
                for g in range(10):
                    if g >= 4:
                        pe.wait_ge(S["comb_stored"], g - 3)
                    for j in range(4):
                        e, t = (4 * g + j) // NT, (4 * g + j) % NT
                        ins = T.matmul(PS[:, 4 + g % 4, j * P:(j + 1) * P], CB[:, 0, t, e:e + 1].broadcast_to([P, P]),
                                       ident[:, :], start=True, stop=True)
                    ins.then_inc(S["comb_turned"], 1)
                pe.wait_ge(S["comb_stored"], 10)

            rounds, tail = layer_rounds(l)
            acts0 = 0 if l == 0 else 4 * DENSE_ROUNDS + TAIL_PAIRS

            def round_(r, u0, pairs, kd, d_pairs, after_first=None):
                def act_ready(k):
                    if k % 2 == 0:
                        pe.wait_ge(S["act_lo"], acts0 + k // 2 + 1 + d_pairs)

                for k in range(2 * pairs + 4):
                    u = u0 + k
                    free = products_before(u, u % 2)
                    pe.wait_ge(set_free[u % 2], free if r is None else r * (ROUND // 2) + free)
                    ready = {0: h_ready, 2 * pairs: act_ready}.get(k)
                    product(u, KC if k < 2 * pairs else kd, H if k < 2 * pairs else ACTB, r, ready)
                    if k == 0 and after_first is not None:
                        after_first()

            u0 = base + U_FFN
            first = int(l == 1)
            if first:
                round_(None, u0, 4, KC, 0, combine)
            with pe.Fori(first, rounds) as r:
                round_(r, u0, 4, KC, r * 4)
            if tail:
                round_(None, u0 + rounds * ROUND, tail, TAIL_FF // P, rounds * 4)

        @block.tensor
        def _(pe):
            T = nc.tensor

            def turn(out, in_):
                return T.transpose(out, in_, ident[0:in_.shape[0], 0:in_.shape[0]])

            def product(u, k_chunks, A, r=None, ready=None):
                pe.wait_ge(S["split_lo"], u + 1 + (0 if r is None else r * ROUND))
                W = split[u % 2][:, :, 0:k_chunks * 256].rearrange("p s (k n) -> p s k n", k=k_chunks)
                for k in range(k_chunks):
                    if ready is not None:
                        ready(k)
                    for c in range(2):
                        for w, a in ((0, 0), (0, 1), (1, 0)):
                            for hf in range(2):
                                ins = T.matmul(PS[:, 4 * (u % 2) + 2 * c + hf, 0:HALF],
                                               W[:, w, k, c * P:(c + 1) * P], A[:, a, k, hf * HALF:(hf + 1) * HALF],
                                               start=(k == 0 and w == 0 and a == 0),
                                               stop=(k == k_chunks - 1 and w == 1))
                ins.then_inc(S["unit_used"], 1)

            pe.wait_ge(S["const_ready"], 3)
            pe.wait_ge(S["x_loaded"], 16 * NT)
            for i in range(2 * NT):
                if i >= 2:
                    pe.wait_ge(S["x_stored"], i - 1)
                for k in range(4):
                    kc = 4 * (i % 2) + k
                    ins = turn(PS[:, i % 2, k * P:(k + 1) * P], xn[:, i // 2, kc * P:(kc + 1) * P])
                ins.then_inc(S["x_turned"], 1)
            pe.wait_ge(S["small_loaded"], 16 * (2 + 6 * DEPTH))
            for l in range(DEPTH):
                turn(PS[:, 2, l * P:(l + 1) * P], VR[:, l, :])
            turn(PS[:, 2, 2 * P:2 * P + 2 * KC], CR[:, :]).then_inc(S["vec_turned"], 1)
            pe.wait_ge(S["silu_lo"], 2)

            def modulation(i, first):
                for s in range(RAW_SLOTS):
                    bb, half = s // 2, s % 2
                    pe.wait_ge(S["split_lo"], s + 1 + i * RAW_SLOTS)
                    W = split[half][:, :, :].rearrange("p a (k n) -> p a k n", k=KC // 2)
                    for k in range(KC // 2):
                        for a in range(2):
                            ins = T.matmul(PS[0:4, 4 + bb, :], CSPLIT[:, 4 * half + k, :], W[:, a, k, :],
                                           start=(s % 2 == 0 and k == 0 and a == 0),
                                           stop=(half == 1 and k == KC // 2 - 1 and a == 1))
                    ins.then_inc(S["unit_used"], 1)
                    if half:
                        pe.wait_ge(S["rows_out"], bb + 1 + 2 * i)
                        if not first:
                            pe.wait_ge(S["ada_out"], bb - 1 + 2 * i)
                        for c in range(4):
                            ins = T.matmul(PS[:, 6 + bb, 2 * c:2 * c + 2], ROWS[:, bb, c * P:(c + 1) * P], SEL[:, :],
                                           start=True, stop=True)
                        ins.then_inc(S["mod_turned"], 1)

            modulation(0, True)
            with pe.Fori(1, N_ADA // RAW_SLOTS) as i:
                modulation(i, False)
            pe.wait_ge(S["ada_out"], N_ADA // 2)

            for l in range(DEPTH):
                base = LAYER_U[l]
                for norm in range(2):
                    q = 2 * l + norm
                    for kc in range(KC):
                        pe.wait_ge(S["sq_ready"], q * KC + kc + 1)
                        for hf in range(2):
                            ins = T.matmul(PS[:, hf, 0:HALF], ones[:, :], HM[:, kc % 2, hf * HALF:(hf + 1) * HALF],
                                           start=(kc == 0), stop=(kc == KC - 1))
                        ins.then_inc(S["sq_used"], 1)

                    def h_ready(k, q=q):
                        pe.wait_ge(S["h_lo"], q * KC + k + 1)

                    if norm == 0:
                        mixer_pe(T, pe, l, base, turn, product, h_ready)
                    else:
                        ffn_pe(T, pe, l, base, turn, product, h_ready)
            for i in range(2 * NT):
                t = i // 2
                if i == 0:
                    for s in range(2):
                        pe.wait_ge(set_free[s], products_before(LAYER_U[1] + U_FFN + FFN_UNITS[1], s))
                elif i >= 2:
                    pe.wait_ge(S[("y_storedA", "y_storedB")[i % 2]], t)
                for k in range(4):
                    ins = turn(PS[:, i % 2, k * P:(k + 1) * P], xT[:, 4 * (i % 2) + k, t * P:(t + 1) * P])
                ins.then_inc(S["y_turned"], 1)

_INPUTS = ["x_prompt", "x_sample", "cache_diff_k", "cache_diff_v", "cache_mla_ckv", "cache_mla_krope", "c", "c_ctx",
           "w_ada", "b_ada", "norm_mix", "norm_ffn", "w_in", "qnorm_a", "knorm_a", "lambda_q1", "lambda_k1",
           "lambda_q2", "lambda_k2", "subln_a", "conv_w", "conv_b", "norm_qa", "w_qb", "norm_kva", "w_kb", "w_vb",
           "qnorm_c", "knorm_c", "w_out", "ffn_w_gate", "ffn_w_up", "ffn_w_down", "router_w", "moe_w_gate",
           "moe_w_up", "moe_w_down"]
_OUTPUTS = [("y_prompt", (1, CTX, D_MODEL)), ("y_sample", (1, LAT, D_MODEL)),
            ("new_diff_k", (1, DEPTH, CTX, HEADS, 2, DA)), ("new_diff_v", (1, DEPTH, CTX, HEADS, VA_W)),
            ("new_mla_ckv", (1, DEPTH, CTX, KV_RANK)), ("new_mla_krope", (1, DEPTH, CTX, ROPE_W))]


def rope_table():
    n = ROPE_W // 4
    inv = np.power(np.float32(10000.0), -np.arange(n, dtype=np.float32) / np.float32(n)).astype(np.float32)
    t = np.arange(LAT)
    out = np.zeros((LAT, 2, 2, 2, n), np.float32)
    for half, pos in enumerate((t // GRID_W, t % GRID_W)):
        ang = pos.astype(np.float32)[:, None] * inv[None, :]
        out[:, 0, half, 0] = out[:, 0, half, 1] = np.cos(ang)
        out[:, 1, half, 0], out[:, 1, half, 1] = -np.sin(ang), np.sin(ang)
    return np.ascontiguousarray(out.reshape(4, P, 64).transpose(1, 0, 2).reshape(P, 256))


def kernel(**inputs):
    import concourse.bacc as bacc
    from concourse.bass_utils import run_bass_kernel_spmd

    nc = bacc.Bacc("TRN2", target_bir_lowering=False, num_devices=1)
    arrays, I, O = {}, {}, {}
    for name in _INPUTS:
        a = np.ascontiguousarray(inputs[name])
        arrays["in_" + name] = a
        I[name] = nc.dram_tensor("in_" + name, a.shape, mybir.dt.from_np(a.dtype), kind="ExternalInput").ap()
    table = rope_table()
    arrays["in_rope"] = table
    I["rope"] = nc.dram_tensor("in_rope", table.shape, mybir.dt.float32, kind="ExternalInput").ap()
    for name, shape in _OUTPUTS:
        O[name] = nc.dram_tensor("out_" + name, shape, mybir.dt.float32, kind="ExternalOutput").ap()
    trunk_program(nc, I, O)
    result = run_bass_kernel_spmd(nc, [arrays], core_ids=[0]).results[0]
    return tuple(result["out_" + name] for name, _ in _OUTPUTS)
```
